# Optimizing a Trainium2 kernel written in Bass

```python
import jax, jax.numpy as jnp
from jax import lax
import numpy as np
import math

D_MODEL = 1024
BATCH = 1
SEQ = 512
DEPTH = 2

CHUNK = 64
D_CONV = D_MODEL // 4
CONV_WIDTH = 31
SB_HEAD_DIM = 64
D_SB = D_MODEL // 2
N_SB_HEADS = D_SB // SB_HEAD_DIM
RET_HEAD_DIM = 64
D_RET = D_MODEL // 4
N_RET_HEADS = D_RET // RET_HEAD_DIM
D_MIX = D_CONV + D_SB + D_RET
D_IN_PROJ = 2 * D_CONV + 3 * D_SB + 4 * D_RET
D_FF = ((8 * D_MODEL // 3 + 127) // 128) * 128
Q_BLOCK = 128
ROPE_BASE = 10000.0
EPS = 1e-6


def rms_norm(x, g):
    xf = x.astype(jnp.float32)
    y = xf * lax.rsqrt(jnp.mean(xf * xf, axis=-1, keepdims=True) + EPS)
    return (y * g.astype(jnp.float32)).astype(x.dtype)

def layer_norm(x, g, b):
    xf = x.astype(jnp.float32)
    mu = jnp.mean(xf, axis=-1, keepdims=True)
    xc = xf - mu
    var = jnp.mean(xc * xc, axis=-1, keepdims=True)
    return (xc * lax.rsqrt(var + EPS) * g.astype(jnp.float32) + b.astype(jnp.float32)).astype(x.dtype)

def swiglu(h, w_in, w_out):
    gate, up = jnp.split(h @ w_in, 2, axis=-1)
    return (jax.nn.silu(gate) * up) @ w_out

def conv_module(u, conv_w, conv_b, ln_g, ln_b):
    a, b = jnp.split(u, 2, axis=-1)
    v = a * jax.nn.sigmoid(b)
    v = jnp.pad(v, ((0, 0), (CONV_WIDTH - 1, 0), (0, 0)))
    y = lax.conv_general_dilated(
        v, conv_w[:, None, :].astype(v.dtype), window_strides=(1,), padding="VALID",
        dimension_numbers=("NWC", "WIO", "NWC"), feature_group_count=D_CONV)
    y = y + conv_b
    return jax.nn.silu(layer_norm(y, ln_g, ln_b))

def stick_breaking(q, k, v):
    B, S, H, Dh = q.shape
    nb = S // Q_BLOCK
    qb = q.reshape(B, nb, Q_BLOCK, H, Dh).transpose(1, 0, 2, 3, 4)
    kpos = jnp.arange(S)
    scale = Dh ** -0.5

    def block(args):
        qi, i = args
        z = jnp.einsum("bqhd,bkhd->bhqk", qi, k,
                       preferred_element_type=jnp.float32) * scale
        qpos = i * Q_BLOCK + jnp.arange(Q_BLOCK)
        mask = kpos[None, :] < qpos[:, None]
        log_beta = jax.nn.log_sigmoid(z)
        log_not = jnp.where(mask, jax.nn.log_sigmoid(-z), 0.0)
        remain = lax.cumsum(log_not, axis=3, reverse=True) - log_not
        w = jnp.where(mask, jnp.exp(log_beta + remain), 0.0)
        return jnp.einsum("bhqk,bkhd->bqhd", w.astype(v.dtype), v)

    out = lax.map(block, (qb, jnp.arange(nb)))
    return out.transpose(1, 0, 2, 3, 4).reshape(B, S, H, Dh)

def rotary(x, pos):
    half = x.shape[-1] // 2
    inv = 1.0 / (ROPE_BASE ** (jnp.arange(half, dtype=jnp.float32) / half))
    ang = pos.astype(jnp.float32)[:, None] * inv[None, :]
    cos = jnp.cos(ang)[None, :, None, :]
    sin = jnp.sin(ang)[None, :, None, :]
    x1 = x[..., :half].astype(jnp.float32)
    x2 = x[..., half:].astype(jnp.float32)
    return jnp.concatenate([x1 * cos - x2 * sin, x1 * sin + x2 * cos], axis=-1).astype(x.dtype)

def retention(q, k, v):
    B, S, H, Dh = q.shape
    nc = S // CHUNK
    log_gamma = jnp.log1p(-jnp.exp2(-5.0 - jnp.arange(H, dtype=jnp.float32)))
    qc = (q * (Dh ** -0.5)).reshape(B, nc, CHUNK, H, Dh)
    kc = k.reshape(B, nc, CHUNK, H, Dh)
    vc = v.reshape(B, nc, CHUNK, H, Dh)
    idx = jnp.arange(CHUNK, dtype=jnp.float32)
    d_intra = jnp.exp(log_gamma[:, None, None] * jnp.abs(idx[:, None] - idx[None, :]))
    scores = jnp.einsum("bnihd,bnjhd->bnhij", qc, kc,
                        preferred_element_type=jnp.float32) * d_intra
    y_intra = jnp.einsum("bnhij,bnjhe->bnihe", scores, vc.astype(jnp.float32))
    k_decay = jnp.exp(log_gamma[None, :] * (CHUNK - 1 - idx)[:, None])
    kv = jnp.einsum("bnjhd,jh,bnjhe->bnhde", kc.astype(jnp.float32), k_decay,
                    vc.astype(jnp.float32))
    chunk_decay = jnp.exp(log_gamma * CHUNK)[None, :, None, None]

    def step(state, kv_n):
        return chunk_decay * state + kv_n, state

    _, s_prev = lax.scan(step, jnp.zeros((B, H, Dh, Dh), jnp.float32),
                         kv.transpose(1, 0, 2, 3, 4))
    s_prev = s_prev.transpose(1, 0, 2, 3, 4)
    q_decay = jnp.exp(log_gamma[None, :] * (idx + 1.0)[:, None])
    y_cross = jnp.einsum("bnihd,ih,bnhde->bnihe", qc.astype(jnp.float32), q_decay, s_prev)
    return (y_intra + y_cross).reshape(B, S, H, Dh)

def head_norm(y, g):
    B, S, H, Dh = y.shape
    mu = jnp.mean(y, axis=-1, keepdims=True)
    yc = y - mu
    var = jnp.mean(yc * yc, axis=-1, keepdims=True)
    return (yc * lax.rsqrt(var + EPS)).reshape(B, S, H * Dh) * g.astype(jnp.float32)

def hybrid_mixer(h, w_in, conv_w, conv_b, conv_ln_g, conv_ln_b, ret_norm_g, w_out, pos):
    B, S, _ = h.shape
    o1 = 2 * D_CONV
    o2 = o1 + D_SB
    o3 = o2 + D_SB
    o4 = o3 + D_SB
    o5 = o4 + D_RET
    o6 = o5 + D_RET
    o7 = o6 + D_RET
    u_conv, q_sb, k_sb, v_sb, q_r, k_r, v_r, g_r = jnp.split(
        h @ w_in, [o1, o2, o3, o4, o5, o6, o7], axis=-1)
    y_conv = conv_module(u_conv, conv_w, conv_b, conv_ln_g, conv_ln_b)
    sb = lambda t: t.reshape(B, S, N_SB_HEADS, SB_HEAD_DIM)
    y_sb = stick_breaking(sb(q_sb), sb(k_sb), sb(v_sb)).reshape(B, S, D_SB)
    rt = lambda t: t.reshape(B, S, N_RET_HEADS, RET_HEAD_DIM)
    y_r = retention(rotary(rt(q_r), pos), rotary(rt(k_r), pos), rt(v_r))
    y_r = jax.nn.silu(g_r.astype(jnp.float32)) * head_norm(y_r, ret_norm_g)
    y = jnp.concatenate([y_conv, y_sb, y_r.astype(h.dtype)], axis=-1)
    return y @ w_out

def first_inputs(seed: int = 0) -> dict:
    key = jax.random.key(seed)
    ks = jax.random.split(key, 20)
    f32 = jnp.float32
    nrm = lambda k, shape, scale: jax.random.normal(k, shape, f32) * scale
    gain = lambda k, shape: 1.0 + 0.02 * jax.random.normal(k, shape, f32)
    return {
        "x": jax.random.normal(ks[0], (BATCH, SEQ, D_MODEL), f32),
        "ffn1_norm": gain(ks[1], (DEPTH, D_MODEL)),
        "ffn1_w_in": nrm(ks[2], (DEPTH, D_MODEL, 2 * D_FF), D_MODEL ** -0.5),
        "ffn1_w_out": nrm(ks[3], (DEPTH, D_FF, D_MODEL), D_FF ** -0.5),
        "mix_norm": gain(ks[4], (DEPTH, D_MODEL)),
        "mix_w_in": nrm(ks[5], (DEPTH, D_MODEL, D_IN_PROJ), D_MODEL ** -0.5),
        "conv_w": nrm(ks[6], (DEPTH, CONV_WIDTH, D_CONV), CONV_WIDTH ** -0.5),
        "conv_b": nrm(ks[7], (DEPTH, D_CONV), 0.02),
        "conv_ln_g": gain(ks[8], (DEPTH, D_CONV)),
        "conv_ln_b": nrm(ks[9], (DEPTH, D_CONV), 0.02),
        "ret_norm_g": gain(ks[10], (DEPTH, D_RET)),
        "mix_w_out": nrm(ks[11], (DEPTH, D_MIX, D_MODEL), D_MIX ** -0.5),
        "ffn2_norm": gain(ks[12], (DEPTH, D_MODEL)),
        "ffn2_w_in": nrm(ks[13], (DEPTH, D_MODEL, 2 * D_FF), D_MODEL ** -0.5),
        "ffn2_w_out": nrm(ks[14], (DEPTH, D_FF, D_MODEL), D_FF ** -0.5),
        "final_norm": gain(ks[15], (D_MODEL,)),
    }

def first_block(x, ffn1_norm, ffn1_w_in, ffn1_w_out, mix_norm, mix_w_in, conv_w, conv_b,
              conv_ln_g, conv_ln_b, ret_norm_g, mix_w_out, ffn2_norm, ffn2_w_in, ffn2_w_out,
              final_norm):
    S = x.shape[1]
    pos = jnp.arange(S)
    for l in range(DEPTH):
        x = x + 0.5 * swiglu(rms_norm(x, ffn1_norm[l]), ffn1_w_in[l], ffn1_w_out[l])
        x = x + hybrid_mixer(rms_norm(x, mix_norm[l]), mix_w_in[l], conv_w[l], conv_b[l],
                             conv_ln_g[l], conv_ln_b[l], ret_norm_g[l], mix_w_out[l], pos)
        x = x + 0.5 * swiglu(rms_norm(x, ffn2_norm[l]), ffn2_w_in[l], ffn2_w_out[l])
    return rms_norm(x, final_norm)


DEPTH_2 = 1

MLA_WIDTH = D_MODEL // 2
MLA_V_DIM = 64
MLA_HEADS = MLA_WIDTH // MLA_V_DIM
MLA_QK_NOPE = 64
MLA_QK_ROPE = 32
MLA_Q_RANK = D_MODEL // 4
MLA_KV_RANK = D_MODEL // 8
ROPE_THETA = 10000.0
GDN_WIDTH = D_MODEL // 4
GDN_HEAD_DIM = 64
GDN_HEADS = GDN_WIDTH // GDN_HEAD_DIM
GDN_CONV = 4
POOL_WIDTH = D_MODEL - MLA_WIDTH - GDN_WIDTH
POOL_WINDOWS = (2, 4, 8, 16)
POOL_GROUPS = 4
POOL_GROUP_DIM = POOL_WIDTH // POOL_GROUPS
MIX_WIDTH = MLA_WIDTH + GDN_WIDTH + POOL_WIDTH
IN_SIZES = (MLA_Q_RANK, MLA_KV_RANK, MLA_QK_ROPE, GDN_WIDTH, GDN_WIDTH, GDN_WIDTH, GDN_WIDTH, GDN_HEADS, GDN_HEADS, POOL_WIDTH)
IN_PROJ_DIM = sum(IN_SIZES)
N_GROUPS = 4
EXPERTS_PER_GROUP = 8
N_EXPERTS = N_GROUPS * EXPERTS_PER_GROUP
TOP_K = 2
EXPERT_FF = D_MODEL // 4
MOE_BLOCK = 128
DEEPNORM_ALPHA = (2 * DEPTH_2) ** 0.25
DEEPNORM_BETA = (8 * DEPTH_2) ** -0.25
LN_EPS = 1e-5
RMS_EPS = 1e-6


F32 = jnp.float32

def layer_norm_2(x, g, b):
    xf = x.astype(F32)
    mu = jnp.mean(xf, axis=-1, keepdims=True)
    var = jnp.mean(jnp.square(xf - mu), axis=-1, keepdims=True)
    return ((xf - mu) * lax.rsqrt(var + LN_EPS)).astype(x.dtype) * g + b

def rms_norm_2(x, g):
    xf = x.astype(F32)
    return (xf * lax.rsqrt(jnp.mean(xf * xf, axis=-1, keepdims=True) + RMS_EPS)).astype(x.dtype) * g

def l2_norm(x):
    xf = x.astype(F32)
    return xf * lax.rsqrt(jnp.sum(xf * xf, axis=-1, keepdims=True) + RMS_EPS)

def split_sizes(x, sizes):
    offs, acc = [], 0
    for s in sizes[:-1]:
        acc += s
        offs.append(acc)
    return jnp.split(x, offs, axis=-1)

def rope_tables(seq):
    inv_freq = jnp.power(ROPE_THETA, -jnp.arange(0, MLA_QK_ROPE, 2, dtype=F32) / MLA_QK_ROPE)
    ang = jnp.arange(seq, dtype=F32)[:, None] * inv_freq[None, :]
    return jnp.cos(ang), jnp.sin(ang)

def apply_rope(x, cos, sin):
    xf = x.astype(F32)
    x1, x2 = jnp.split(xf, 2, axis=-1)
    return jnp.concatenate([x1 * cos - x2 * sin, x2 * cos + x1 * sin], axis=-1).astype(x.dtype)

def mla_attention(c_q, c_kv, k_rope, q_norm_g, kv_norm_g, w_uq, w_ukv, cos, sin):
    B, S, _ = c_q.shape
    q = (rms_norm_2(c_q, q_norm_g) @ w_uq).reshape(B, S, MLA_HEADS, MLA_QK_NOPE + MLA_QK_ROPE)
    q_nope, q_rope = q[..., :MLA_QK_NOPE], q[..., MLA_QK_NOPE:]
    q_rope = apply_rope(q_rope, cos[:, None, :], sin[:, None, :])
    kv = (rms_norm_2(c_kv, kv_norm_g) @ w_ukv).reshape(B, S, MLA_HEADS, MLA_QK_NOPE + MLA_V_DIM)
    k_nope, v = kv[..., :MLA_QK_NOPE], kv[..., MLA_QK_NOPE:]
    k_rope = apply_rope(k_rope, cos, sin)
    scale = (MLA_QK_NOPE + MLA_QK_ROPE) ** -0.5
    outs = []
    for qb in range(S // Q_BLOCK):
        q0, kend = qb * Q_BLOCK, (qb + 1) * Q_BLOCK
        s = (jnp.einsum('bqhd,bkhd->bhqk', q_nope[:, q0:kend], k_nope[:, :kend])
             + jnp.einsum('bqhd,bkd->bhqk', q_rope[:, q0:kend], k_rope[:, :kend]))
        s = s.astype(F32) * scale
        q_chunk = jnp.arange(q0, kend) // CHUNK
        k_chunk = jnp.arange(kend) // CHUNK
        allowed = k_chunk[None, :] <= q_chunk[:, None]
        p = jax.nn.softmax(jnp.where(allowed, s, -jnp.inf), axis=-1).astype(v.dtype)
        outs.append(jnp.einsum('bhqk,bkhd->bqhd', p, v[:, :kend]))
    return jnp.concatenate(outs, axis=1).reshape(B, S, MLA_WIDTH)

def causal_depthwise_conv(x, w):
    C = x.shape[-1]
    return lax.conv_general_dilated(x, w[:, None, :].astype(x.dtype), window_strides=(1,),
                                    padding=[(GDN_CONV - 1, 0)],
                                    dimension_numbers=('NWC', 'WIO', 'NWC'),
                                    feature_group_count=C)

def gated_delta_rule(q, k, v, g, beta):
    B, S, H, dk = q.shape
    dv = v.shape[-1]
    nc = S // CHUNK

    def to_chunks(t):
        t = t.astype(F32).reshape((B, nc, CHUNK, H) + t.shape[3:])
        return jnp.moveaxis(t, 3, 1)

    qc = to_chunks(q) * dk ** -0.5
    kc, vc = to_chunks(k), to_chunks(v)
    gc = jnp.cumsum(to_chunks(g), axis=-1)
    bc = to_chunks(beta)
    idx = jnp.arange(CHUNK)
    incl = idx[:, None] >= idx[None, :]
    strict = idx[:, None] > idx[None, :]
    diff = gc[..., :, None] - gc[..., None, :]
    decay = jnp.where(incl, jnp.exp(jnp.where(incl, diff, 0.0)), 0.0)
    kb = kc * bc[..., None]
    a_mat = jnp.where(strict, jnp.einsum('bhnid,bhnjd->bhnij', kb, kc) * decay, 0.0)
    lower = a_mat + jnp.eye(CHUNK, dtype=F32)
    rhs = jnp.concatenate([vc * bc[..., None], kb * jnp.exp(gc)[..., None]], axis=-1)
    sol = lax.linalg.triangular_solve(lower, rhs, left_side=True, lower=True, unit_diagonal=True)
    u, w = sol[..., :dv], sol[..., dv:]
    qk = jnp.where(incl, jnp.einsum('bhnid,bhnjd->bhnij', qc, kc) * decay, 0.0)
    q_dec = qc * jnp.exp(gc)[..., None]
    k_dec = kc * jnp.exp(gc[..., -1:] - gc)[..., None]
    g_last = jnp.exp(gc[..., -1])

    def step(state, inp):
        q_i, k_i, u_i, w_i, qk_i, gl_i = inp
        v_new = u_i - jnp.einsum('bhck,bhkv->bhcv', w_i, state)
        o_i = jnp.einsum('bhck,bhkv->bhcv', q_i, state) + jnp.einsum('bhij,bhjv->bhiv', qk_i, v_new)
        state = state * gl_i[..., None, None] + jnp.einsum('bhck,bhcv->bhkv', k_i, v_new)
        return state, o_i

    xs = tuple(jnp.moveaxis(t, 2, 0) for t in (q_dec, k_dec, u, w, qk, g_last))
    _, o = lax.scan(step, jnp.zeros((B, H, dk, dv), F32), xs)
    o = jnp.moveaxis(o, 0, 2).reshape(B, H, S, dv)
    return jnp.transpose(o, (0, 2, 1, 3))

def gdn_mixer(q, k, v, z, a, b, conv_w, a_log, dt_bias, out_g):
    B, S, _ = q.shape
    qkv = jax.nn.silu(causal_depthwise_conv(jnp.concatenate([q, k, v], axis=-1), conv_w))
    q, k, v = jnp.split(qkv, 3, axis=-1)
    shp = (B, S, GDN_HEADS, GDN_HEAD_DIM)
    q, k, v = l2_norm(q.reshape(shp)), l2_norm(k.reshape(shp)), v.reshape(shp)
    g = -jnp.exp(a_log.astype(F32)) * jax.nn.softplus(a.astype(F32) + dt_bias.astype(F32))
    beta = jax.nn.sigmoid(b.astype(F32))
    o = gated_delta_rule(q, k, v, g, beta).astype(z.dtype)
    o = rms_norm_2(o, out_g) * jax.nn.silu(z.reshape(shp))
    return o.reshape(B, S, GDN_WIDTH)

def pool_mixer(p, pool_w, pool_scale):
    B, S, _ = p.shape
    pg = p.reshape(B, S, POOL_GROUPS, POOL_GROUP_DIM).astype(F32)
    cs = jnp.cumsum(pg, axis=1)
    cs = jnp.concatenate([jnp.zeros_like(cs[:, :1]), cs], axis=1)
    t = jnp.arange(S)
    means = []
    for gi, win in enumerate(POOL_WINDOWS):
        start = jnp.maximum(t + 1 - win, 0)
        cnt = (t + 1 - start).astype(F32)
        cs_g = cs[:, :, gi, :]
        means.append((cs_g[:, 1:] - cs_g[:, start]) / cnt[None, :, None])
    delta = (jnp.stack(means, axis=2) - pg).astype(p.dtype)
    mixed = jnp.einsum('bsgc,gcd->bsgd', delta, pool_w)
    return mixed.reshape(B, S, POOL_WIDTH) * pool_scale

def hybrid_mixer_2(h, w_in, q_norm_g, kv_norm_g, w_uq, w_ukv, conv_w, a_log, dt_bias, gdn_g,
                 pool_w, pool_scale, w_out, cos, sin):
    proj = h @ w_in
    c_q, c_kv, k_rope, gq, gk, gv, gz, ga, gb, p = split_sizes(proj, IN_SIZES)
    y_mla = mla_attention(c_q, c_kv, k_rope, q_norm_g, kv_norm_g, w_uq, w_ukv, cos, sin)
    y_gdn = gdn_mixer(gq, gk, gv, gz, ga, gb, conv_w, a_log, dt_bias, gdn_g)
    y_pool = pool_mixer(p, pool_w, pool_scale)
    return jnp.concatenate([y_mla, y_gdn, y_pool], axis=-1) @ w_out

def grouped_expert_ffn(hf, expert, weights, w_gate, w_up, w_down):
    T, D = hf.shape
    A = T * TOP_K
    flat_e = expert.reshape(A)
    flat_tok = jnp.arange(A, dtype=jnp.int32) // TOP_K
    flat_w = weights.reshape(A).astype(hf.dtype)
    order = jnp.argsort(flat_e)
    se = flat_e[order]
    counts = jax.ops.segment_sum(jnp.ones((A,), jnp.int32), flat_e, num_segments=N_EXPERTS)
    padded = (counts + MOE_BLOCK - 1) // MOE_BLOCK * MOE_BLOCK
    pad_end = jnp.cumsum(padded)
    pad_start = pad_end - padded
    start = jnp.cumsum(counts) - counts
    dest = pad_start[se] + (jnp.arange(A, dtype=jnp.int32) - start[se])
    nb = (A + N_EXPERTS * (MOE_BLOCK - 1) + MOE_BLOCK - 1) // MOE_BLOCK
    P = nb * MOE_BLOCK
    buf_tok = jnp.full((P,), T, jnp.int32).at[dest].set(flat_tok[order])
    buf_w = jnp.zeros((P,), hf.dtype).at[dest].set(flat_w[order])
    block_expert = jnp.clip(jnp.searchsorted(pad_end, jnp.arange(nb) * MOE_BLOCK, side='right'), 0, N_EXPERTS - 1)
    xpad = jnp.concatenate([hf, jnp.zeros((1, D), hf.dtype)], axis=0)
    xb = xpad[buf_tok].reshape(nb, MOE_BLOCK, D)

    def block_ffn(args):
        xb_i, e = args
        return (jax.nn.silu(xb_i @ w_gate[e]) * (xb_i @ w_up[e])) @ w_down[e]

    yb = lax.map(block_ffn, (xb, block_expert)).reshape(P, D)
    out = jnp.zeros((T + 1, D), yb.dtype).at[buf_tok].add(yb * buf_w[:, None])
    return out[:T]

def hierarchical_moe(h, w_rg, b_rg, w_re, b_re, w_gate, w_up, w_down):
    B, S, D = h.shape
    hf = h.reshape(B * S, D)
    g_prob = jax.nn.softmax((hf @ w_rg + b_rg).astype(F32), axis=-1)
    g_p, g_sel = lax.top_k(g_prob, 1)
    e_logit = (hf @ w_re + b_re).astype(F32).reshape(-1, N_GROUPS, EXPERTS_PER_GROUP)
    e_logit = jnp.take_along_axis(e_logit, g_sel[:, :, None], axis=1)[:, 0]
    e_p, e_idx = lax.top_k(jax.nn.softmax(e_logit, axis=-1), TOP_K)
    weights = g_p * e_p / jnp.sum(e_p, axis=-1, keepdims=True)
    expert = g_sel * EXPERTS_PER_GROUP + e_idx
    return grouped_expert_ffn(hf, expert, weights, w_gate, w_up, w_down).reshape(B, S, D)

def second_inputs(seed: int = 0) -> dict:
    key = jax.random.key(seed)
    ks = jax.random.split(key, 32)
    L, D = DEPTH_2, D_MODEL

    def nrm(k, shape, scale):
        return jax.random.normal(k, shape, F32) * scale

    dt = jnp.exp(jax.random.uniform(ks[9], (L, GDN_HEADS), F32, math.log(1e-3), math.log(1e-1)))
    return {
        'x': nrm(ks[0], (BATCH, SEQ, D), 1.0),
        'c': nrm(ks[1], (BATCH, D), 1.0),
        'w_in': nrm(ks[2], (L, D, IN_PROJ_DIM), D ** -0.5),
        'mla_q_norm': 1.0 + nrm(ks[3], (L, MLA_Q_RANK), 0.05),
        'mla_kv_norm': 1.0 + nrm(ks[4], (L, MLA_KV_RANK), 0.05),
        'mla_w_uq': nrm(ks[5], (L, MLA_Q_RANK, MLA_HEADS * (MLA_QK_NOPE + MLA_QK_ROPE)), MLA_Q_RANK ** -0.5),
        'mla_w_ukv': nrm(ks[6], (L, MLA_KV_RANK, MLA_HEADS * (MLA_QK_NOPE + MLA_V_DIM)), MLA_KV_RANK ** -0.5),
        'gdn_conv': nrm(ks[7], (L, GDN_CONV, 3 * GDN_WIDTH), GDN_CONV ** -0.5),
        'gdn_a_log': jnp.log(jax.random.uniform(ks[8], (L, GDN_HEADS), F32, 1.0, 16.0)),
        'gdn_dt_bias': dt + jnp.log(-jnp.expm1(-dt)),
        'gdn_out_norm': 1.0 + nrm(ks[10], (L, GDN_HEAD_DIM), 0.05),
        'pool_w': nrm(ks[11], (L, POOL_GROUPS, POOL_GROUP_DIM, POOL_GROUP_DIM), POOL_GROUP_DIM ** -0.5),
        'pool_scale': 1.0 + nrm(ks[12], (L, POOL_WIDTH), 0.05),
        'w_out': nrm(ks[13], (L, MIX_WIDTH, D), MIX_WIDTH ** -0.5 * DEEPNORM_BETA),
        'w_mod': nrm(ks[14], (L, D, 6 * D), 0.2 * D ** -0.5),
        'b_mod': nrm(ks[15], (L, 6 * D), 0.02),
        'ln1_g': 1.0 + nrm(ks[16], (L, D), 0.05),
        'ln1_b': nrm(ks[17], (L, D), 0.02),
        'ln2_g': 1.0 + nrm(ks[18], (L, D), 0.05),
        'ln2_b': nrm(ks[19], (L, D), 0.02),
        'router_w_group': nrm(ks[20], (L, D, N_GROUPS), D ** -0.5),
        'router_b_group': nrm(ks[21], (L, N_GROUPS), 0.01),
        'router_w_expert': nrm(ks[22], (L, D, N_EXPERTS), D ** -0.5),
        'router_b_expert': nrm(ks[23], (L, N_EXPERTS), 0.01),
        'moe_w_gate': nrm(ks[24], (L, N_EXPERTS, D, EXPERT_FF), D ** -0.5),
        'moe_w_up': nrm(ks[25], (L, N_EXPERTS, D, EXPERT_FF), D ** -0.5),
        'moe_w_down': nrm(ks[26], (L, N_EXPERTS, EXPERT_FF, D), EXPERT_FF ** -0.5 * DEEPNORM_BETA),
    }

def second_block(x, c, w_in, mla_q_norm, mla_kv_norm, mla_w_uq, mla_w_ukv, gdn_conv, gdn_a_log,
              gdn_dt_bias, gdn_out_norm, pool_w, pool_scale, w_out, w_mod, b_mod, ln1_g, ln1_b,
              ln2_g, ln2_b, router_w_group, router_b_group, router_w_expert, router_b_expert,
              moe_w_gate, moe_w_up, moe_w_down):
    cos, sin = rope_tables(x.shape[1])
    c_act = jax.nn.silu(c)
    for l in range(DEPTH_2):
        mod = c_act @ w_mod[l] + b_mod[l]
        sh1, sc1, gt1, sh2, sc2, gt2 = [m[:, None, :] for m in jnp.split(mod, 6, axis=-1)]
        h = x * (1.0 + sc1) + sh1
        y = hybrid_mixer_2(h, w_in[l], mla_q_norm[l], mla_kv_norm[l], mla_w_uq[l], mla_w_ukv[l],
                         gdn_conv[l], gdn_a_log[l], gdn_dt_bias[l], gdn_out_norm[l],
                         pool_w[l], pool_scale[l], w_out[l], cos, sin)
        x = layer_norm_2(DEEPNORM_ALPHA * x + (1.0 + gt1) * y, ln1_g[l], ln1_b[l])
        h = x * (1.0 + sc2) + sh2
        y = hierarchical_moe(h, router_w_group[l], router_b_group[l], router_w_expert[l],
                             router_b_expert[l], moe_w_gate[l], moe_w_up[l], moe_w_down[l])
        x = layer_norm_2(DEEPNORM_ALPHA * x + (1.0 + gt2) * y, ln2_g[l], ln2_b[l])
    return x


def setup_inputs(seed=0):
    out = dict(first_inputs(seed))
    for name, value in second_inputs(seed + 1).items():
        if name != "x":
            out[name + "_2"] = value
    return out


def reference(
    x, ffn1_norm, ffn1_w_in, ffn1_w_out, mix_norm, mix_w_in, conv_w, conv_b, conv_ln_g,
    conv_ln_b, ret_norm_g, mix_w_out, ffn2_norm, ffn2_w_in, ffn2_w_out, final_norm, c_2, w_in_2,
    mla_q_norm_2, mla_kv_norm_2, mla_w_uq_2, mla_w_ukv_2, gdn_conv_2, gdn_a_log_2,
    gdn_dt_bias_2, gdn_out_norm_2, pool_w_2, pool_scale_2, w_out_2, w_mod_2, b_mod_2, ln1_g_2,
    ln1_b_2, ln2_g_2, ln2_b_2, router_w_group_2, router_b_group_2, router_w_expert_2,
    router_b_expert_2, moe_w_gate_2, moe_w_up_2, moe_w_down_2,
):
    x = first_block(
        x, ffn1_norm, ffn1_w_in, ffn1_w_out, mix_norm, mix_w_in, conv_w, conv_b, conv_ln_g,
        conv_ln_b, ret_norm_g, mix_w_out, ffn2_norm, ffn2_w_in, ffn2_w_out, final_norm,
    )
    return second_block(
        x, c_2, w_in_2, mla_q_norm_2, mla_kv_norm_2, mla_w_uq_2, mla_w_ukv_2, gdn_conv_2,
        gdn_a_log_2, gdn_dt_bias_2, gdn_out_norm_2, pool_w_2, pool_scale_2, w_out_2, w_mod_2,
        b_mod_2, ln1_g_2, ln1_b_2, ln2_g_2, ln2_b_2, router_w_group_2, router_b_group_2,
        router_w_expert_2, router_b_expert_2, moe_w_gate_2, moe_w_up_2, moe_w_down_2,
    )


_drawn_inputs = setup_inputs


def setup_inputs(seed=0):
    import zlib

    import numpy as np

    out = dict(_drawn_inputs(seed))
    spreads = {}
    factors = {'ffn1_norm': 2.707,
     'conv_ln_g': 4.112,
     'conv_ln_b': 4.161,
     'ret_norm_g': 4.755,
     'ffn2_norm': 3.888,
     'mla_q_norm_2': 8.0,
     'mla_kv_norm_2': 6.815,
     'gdn_out_norm_2': 17.42,
     'pool_scale_2': 9.701,
     'router_b_group_2': 26.716,
     'router_b_expert_2': 6.724}
    for name, (base, spread) in spreads.items():
        noise = np.random.default_rng([zlib.crc32(name.encode()), seed]).standard_normal(out[name].shape)
        drawn = base * np.exp(spread * noise) if base else spread * noise
        out[name] = __import__('jax').numpy.asarray(drawn.astype(out[name].dtype))
    for name, factor in factors.items():
        out[name] = (out[name] * factor).astype(out[name].dtype)
    return out
```

```python
from contextlib import ExitStack

import concourse.bass as bass
import numpy as np
from concourse import mybir

F32 = mybir.dt.float32
U32 = mybir.dt.uint32
ACT = mybir.ActivationFunctionType
ALU = mybir.AluOpType
AXX = mybir.AxisListType.X

P = 128
T = 512
D = 1024
KD = D // P
NT = T // P
DEPTH = 2
FF = 2816
KF = FF // P
CW = 256
SLOT = KD * CW
NSLOT = 5
HEAD = 64
CHUNK = 64
SB_HEADS = 8
RET_HEADS = 4
CONV_TAPS = 31
PAD = CONV_TAPS - 1
MLA_HEADS = 8
NOPE, ROPE = 64, 32
QK = NOPE + ROPE
GDN_HEADS = 4
GDN_TAPS = 4
POOL_WINDOWS = (2, 4, 8, 16)
EXPERTS = 32
GROUPS = 4
PER_GROUP = EXPERTS // GROUPS
ALPHA = 2 ** 0.25
RMS_EPS, LN_EPS = 1e-6, 1e-5
BIG = 1e30


def constant_tables():
    i = np.arange(P)
    row, col = i[:, None], i[None, :]
    same64 = (row // 64) == (col // 64)
    t = {}
    t["ident"] = np.eye(P)
    t["ones"] = np.ones((P, P))
    t["sum64"] = same64 * 1.0
    t["mean64"] = same64 / 64.0
    t["centre64"] = np.eye(P) - same64 / 64.0
    t["neg_suffix"] = -1.0 * (row >= col)
    t["neg_ones"] = -np.ones((P, P))
    t["swap64"] = np.where(same64, np.where(row == col + 32, -1.0 * (col % 64 < 32), 0.0)
                           + np.where(row == col - 32, 1.0 * (col % 64 >= 32), 0.0), 0.0)
    r, c = row - NOPE, col - NOPE
    inside = (r >= 0) & (r < ROPE) & (c >= 0) & (c < ROPE)
    t["swap32"] = np.where(inside, np.where(r == c + 16, -1.0 * (c < 16), 0.0)
                           + np.where(r == c - 16, 1.0 * (c >= 16), 0.0), 0.0)
    t["incl"] = same64 * (row <= col) * 1.0
    t["strict"] = same64 * (row < col) * 1.0
    t["later"] = same64 * (row > col) * 1.0
    for lv in range(6):
        s = 2 ** lv
        t[f"level{lv}"] = 1.0 * (((col // s) % 2 == 1) & (row // s == col // s - 1))
    pos = np.arange(T, dtype=np.float32)
    inv = (1.0 / (np.float32(10000.0) ** (np.arange(32, dtype=np.float32) / np.float32(32)))).astype(np.float32)
    ang = (pos[None, :] * inv[i % 32][:, None]).astype(np.float32)
    t["cos64"], t["sin64"] = np.cos(ang.astype(np.float64)), np.sin(ang.astype(np.float64))
    inv = (np.float32(10000.0) ** (-np.arange(0, 32, 2, dtype=np.float32) / np.float32(32))).astype(np.float32)
    ang = (pos[None, :] * inv[i % 16][:, None]).astype(np.float32)
    t["cos32"], t["sin32"] = np.cos(ang.astype(np.float64)), np.sin(ang.astype(np.float64))
    tt = np.arange(T)[None, :]
    for h in range(RET_HEADS):
        gamma = 1.0 - 2.0 ** (-5.0 - h)
        t[f"decay{h}"] = np.where(tt // CHUNK >= row // CHUNK, gamma ** np.abs(tt - row), 0.0) * HEAD ** -0.5
    for g in range(2):
        win = np.array([POOL_WINDOWS[2 * g + (p >= 64)] for p in range(P)])[:, None]
        t[f"inv_count{g}"] = 1.0 / np.minimum(tt + 1, win)
    t["rms_eps"] = np.full((P, 1), RMS_EPS)
    t["ln_eps"] = np.full((P, 1), LN_EPS)
    t["one"] = np.ones((P, 1))
    t["expert_id"] = np.tile(np.arange(EXPERTS)[None, :], (P, 1))
    t["pad"] = np.full((P, 4), -BIG)
    return {k: np.asarray(v, np.float32) for k, v in t.items()}


def offsets(widths):
    at, out = 0, {}
    for name, w in widths:
        out[name] = (at, at + w)
        at += w
    return out, at


CONSTS = constant_tables()
CONST_AT, CONST_W = offsets([(k, v.shape[1]) for k, v in CONSTS.items()])
PARAM_AT, PARAM_W = offsets([
    ("ffn1_norm", DEPTH * KD), ("mix_norm", DEPTH * KD), ("ffn2_norm", DEPTH * KD), ("final_norm", KD),
    ("conv_w", DEPTH * 2 * CONV_TAPS), ("conv_b", DEPTH * 2), ("conv_ln_g", DEPTH * 2),
    ("conv_ln_b", DEPTH * 2), ("ret_norm_g", DEPTH * 2),
    ("c", KD), ("b_mod", 6 * KD), ("q_norm", 2), ("kv_norm", 1), ("gdn_conv", 6 * GDN_TAPS),
    ("gdn_g", 1), ("pool_scale", 2), ("pool_w", 128), ("router_w", KD * (GROUPS + EXPERTS)),
    ("ln1_g", KD), ("ln1_b", KD), ("ln2_g", KD), ("ln2_b", KD)])
ROW_AT, ROW_W = offsets([("dt_bias", GDN_HEADS), ("a_log", GDN_HEADS), ("router_b", GROUPS + EXPERTS)])


class Queue:

    def __init__(self, sem):
        self.sem, self.count, self.steps, self.reached = sem, 0, [], {}

    def wait(self, *marks):
        for sem, value in marks:
            if value > self.reached.get(id(sem), 0):
                self.reached[id(sem)] = value
                self.steps.append(lambda e, s=sem, v=value: e.wait_ge(s, v))

    def do(self, op, *marks):
        self.wait(*marks)
        self.count += 1
        self.steps.append(lambda e: op(e).then_inc(self.sem, 1))
        return self.sem, self.count

    def quiet(self, op, *marks):
        self.wait(*marks)
        self.steps.append(op)

    @property
    def last(self):
        return (self.sem, self.count)


class Buffer:
    def __init__(self, ap):
        self.ap, self.free = ap, ()

    def release(self, *marks):
        self.free = marks


class Rotation:

    def __init__(self, aps):
        self.buffers, self.n = [Buffer(a) for a in aps], 0

    def take(self):
        b = self.buffers[self.n % len(self.buffers)]
        self.n += 1
        assert b.free is not None, "taken before its readers are queued"
        out = Buffer(b.ap)
        out.free, b.free = b.free, None
        out.release = lambda *marks, b=b: setattr_free(b, marks)
        return out


def setattr_free(b, marks):
    b.free = marks


def build(nc, io, stages=None):
    with ExitStack() as ctx:
        def sbuf(name, shape, dt=F32):
            return ctx.enter_context(nc.sbuf_tensor(name, shape, dt))

        def sem(name):
            return ctx.enter_context(nc.semaphore(name))

        x = sbuf("x", [P, KD, T])
        h = sbuf("h", [P, KD, T])
        ring = sbuf("ring", [P, NSLOT, SLOT])
        arena = sbuf("arena", [P, 48 * T])
        const = sbuf("const", [P, CONST_W])
        param = sbuf("param", [P, PARAM_W])
        rowp = sbuf("rowp", [1, ROW_W])
        small = sbuf("small", [P, 512])
        psum = ctx.enter_context(nc.psum_tensor("psum", [P, 8, T], F32))

        V, A, PE, G = (Queue(sem(f"{n}_done")) for n in ("vector", "scalar", "tensor", "gpsimd"))
        S = Queue(sem("sync_unused"))
        slot_full = [sem(f"slot{i}_full") for i in range(NSLOT)]
        s_const, s_x, s_out = sem("const_loaded"), sem("x_loaded"), sem("out_stored")

        def tile(i, n=1):
            return arena[:, i * T:(i + n) * T]

        def K(name, a=0, b=None):
            lo, hi = CONST_AT[name]
            return const[:, lo + a:(hi if b is None else lo + b)]

        def W(name, a=0, b=None):
            lo, hi = PARAM_AT[name]
            return param[:, lo + a:(hi if b is None else lo + b)]

        banks = Rotation([psum[:, i, :] for i in range(8)])

        def mm(out, lhsT, rhs, start, stop, *marks, last=False, loose=False):
            def op(e):
                return e.matmul(out, lhsT, rhs, start=start, stop=stop, skip_group_check=loose)
            return PE.do(op, *marks) if last else PE.quiet(op, *marks)

        def act(out, in_, func, *marks, scale=1.0, bias=0.0, accum=None):
            if accum is not None:
                return A.do(lambda e: e.activation(out, in_, func, bias=bias, scale=scale, accum_out=accum), *marks)
            return A.do(lambda e: e.activation(out, in_, func, bias=bias, scale=scale), *marks)

        def tt(out, a, b, op, *marks, q=V):
            return q.do(lambda e: e.tensor_tensor(out, a, b, op), *marks)

        def ts(out, a, s1, s2, op0, op1, *marks, q=V):
            if op1 is None:
                return q.do(lambda e: e.tensor_scalar(out, a, s1, None, op0), *marks)
            return q.do(lambda e: e.tensor_scalar(out, a, s1, s2, op0, op1), *marks)

        def stt(out, a, s, b, op0, op1, *marks):
            return V.do(lambda e: e.scalar_tensor_tensor(out=out, in0=a, scalar=s, in1=b, op0=op0, op1=op1), *marks)

        def copy(out, a, *marks, q=V):
            if q is A:
                return act(out, a, ACT.Copy, *marks)
            return q.do(lambda e: e.tensor_copy(out, a), *marks)

        def fence():
            marks = [q.last for q in (V, A, PE, G) if q.count]
            for q in (V, A, PE, G):
                q.wait(*[m for m in marks])

        loads = [0]
        slot_free = [()] * NSLOT

        def load(src, width=SLOT):
            i = loads[0] % NSLOT
            use = loads[0] // NSLOT + 1
            loads[0] += 1
            assert slot_free[i] is not None, "slot filled before its readers are queued"
            S.wait(*slot_free[i])
            slot_free[i] = None
            S.steps.append(lambda e: e.dma_start(ring[:, i, 0:width], src).then_inc(slot_full[i], 16))
            return i, (slot_full[i], 16 * use)

        def done_with(i, *marks):
            slot_free[i] = marks

        def inv_root(out, ss, n, eps, *marks):
            m = act(out, ss, ACT.Ln, *marks, scale=1.0 / n, bias=K(eps)[0:out.shape[0]])
            return act(out, out, ACT.Exp, m, scale=-0.5)

        def sigmoid_of(buf, src, *marks):
            m = act(buf, src, ACT.Exp, *marks, scale=-1.0)
            m = ts(buf, buf, 1.0, None, ALU.add, None, m)
            return V.do(lambda e: e.reciprocal(buf, buf), m)

        S.steps.append(lambda e: e.dma_start(const[:, :], io["consts"]).then_inc(s_const, 16))
        S.steps.append(lambda e: e.dma_start(param[:, :], io["params"]).then_inc(s_const, 16))
        S.steps.append(lambda e: e.dma_start(rowp[:, :], io["rows"]).then_inc(s_const, 16))
        S.steps.append(lambda e: e.dma_start(x[:, :, :], io["xT"].rearrange("(t p) n -> p t n", p=P)).then_inc(s_x, 16))
        for q in (V, A, PE, G):
            q.wait((s_const, 48), (s_x, 16))

        temps = Rotation([tile(i) for i in range(40, 48)])

        class SquareSum:

            def __init__(self, n, stat="ones"):
                self.n, self.k, self.waiting = n, 0, []
                self.bank, self.stat = None, stat

            def add(self, src, *marks, square=True):
                buf = temps.take()
                if square:
                    m = act(buf.ap, src, ACT.Square, *marks, *buf.free)
                    self.waiting.append((buf, buf.ap, m))
                else:
                    raise NotImplementedError

            def flush(self):
                for buf, ap, m in self.waiting:
                    if self.bank is None:
                        self.bank = banks.take()
                    mark = mm(self.bank.ap, K(self.stat), ap, self.k == 0, self.k == self.n - 1, m,
                              *(self.bank.free if self.k == 0 else ()), last=True)
                    buf.release(mark)
                    self.k += 1
                    self.mark = mark
                self.waiting = []

        def rms_to_h(stats, gain, at):
            stats.flush()
            r = temps.take()
            m = inv_root(r.ap, stats.bank.ap, D, "rms_eps", stats.mark, *r.free)
            stats.bank.release(m)
            marks = [stt(h[:, k, :], x[:, k, :], W(gain, at + k, at + k + 1), r.ap, ALU.mult, ALU.mult,
                         m, PE.last) for k in range(KD)]
            r.release(marks[-1])
            return marks

        def project(out, kt_n, lhs, rhs, *marks, rhs_marks=None):
            for kt in range(kt_n):
                extra = (rhs_marks[kt],) if rhs_marks else ()
                m = mm(out, lhs(kt), rhs(kt), kt == 0, kt == kt_n - 1, *(marks if kt == 0 else ()), *extra,
                       last=kt == kt_n - 1)
            return m

        mod = small[:, 0:6 * KD]
        c_act = small[:, 48:56]
        mod_acc = [tile(22), tile(23)]
        mod_bank = []

        def mod_start():
            m = act(c_act, W("c"), ACT.Exp, scale=-1.0)
            m = ts(c_act, c_act, 1.0, None, ALU.add, None, m)
            m = V.do(lambda e: e.reciprocal(c_act, c_act), m)
            return tt(c_act, c_act, W("c"), ALU.mult, m)

        def mod_step(j, ready):
            i, full = load(io["w_mod"][j])
            acc = mod_acc[j % 2][:, 0:CW]
            free = mod_bank[j - 2:j - 1] if j >= 2 else []
            m = ts(acc, ring[:, i, 0:CW], c_act[:, 0:1], None, ALU.mult, None, full, ready, *free)
            for k in range(1, KD):
                m = stt(acc, ring[:, i, k * CW:(k + 1) * CW], c_act[:, k:k + 1], acc, ALU.mult, ALU.add, m)
            done_with(i, m)
            b = banks.take()
            for n in range(2):
                mark = mm(b.ap[:, n:n + 1], acc[:, n * P:(n + 1) * P], K("one"), True, True, m, *b.free, last=True)
            mod_bank.append(mark)
            m = tt(mod[:, 2 * j:2 * j + 2], b.ap[:, 0:2], W("b_mod", 2 * j, 2 * j + 2), ALU.add, mark)
            b.release(m)
            return m

        def ffn(h_ready, w_in, w_out, stats, aside=None):
            hid_ready = []
            for j in range(FF // CW):
                ig, full_g = load(w_in[j])
                iu, full_u = load(w_in[FF // CW + j])
                for n in range(2):
                    f = 2 * j + n
                    bg, bu = banks.take(), banks.take()
                    cols = slice(n * P, (n + 1) * P)
                    mg = project(bg.ap, KD, lambda k: ring[:, ig, k * CW + n * P:k * CW + n * P + P],
                                 lambda k: h[:, k, :], full_g, *bg.free, rhs_marks=h_ready)
                    mu = project(bu.ap, KD, lambda k: ring[:, iu, k * CW + n * P:k * CW + n * P + P],
                                 lambda k: h[:, k, :], full_u, *bu.free)
                    s = temps.take()
                    m = sigmoid_of(s.ap, bg.ap, mg, *s.free)
                    m = tt(s.ap, bg.ap, s.ap, ALU.mult, m)
                    bg.release(m)
                    m = tt(tile(f), bu.ap, s.ap, ALU.mult, m, mu)
                    bu.release(m)
                    s.release(m)
                    hid_ready.append(m)
                done_with(ig, mg)
                done_with(iu, mu)
                if aside:
                    aside(j)
            for j in range(D // CW):
                bb = [banks.take(), banks.take()]
                for k0 in range(0, KF, KD):
                    kn = min(KD, KF - k0)
                    i, full = load(w_out[j, :, k0 * CW:(k0 + kn) * CW], kn * CW)
                    for n in range(2):
                        for k in range(kn):
                            kt = k0 + k
                            m = mm(bb[n].ap, ring[:, i, k * CW + n * P:k * CW + n * P + P], tile(kt), kt == 0,
                                   kt == KF - 1, full, hid_ready[kt], *(bb[n].free if kt == 0 else ()),
                                   last=k == kn - 1)
                        if kt == KF - 1:
                            d = 2 * j + n
                            mx = stt(x[:, d, :], bb[n].ap, 0.5, x[:, d, :], ALU.mult, ALU.add, m)
                            bb[n].release(mx)
                            if stats:
                                stats.add(x[:, d, :], mx)
                    done_with(i, m)
                    if stats and k0 == 0:
                        pass
                if stats and j:
                    pair, stats.waiting = stats.waiting[-2:], stats.waiting[:-2]
                    stats.flush()
                    stats.waiting = pair

        def mixer1(layer, h_ready, stats):
            w_in, w_out = io["mix_w_in"][layer], io["mix_w_out"][layer]
            gate_b, q_sb, k_sb, v_sb, q_r, k_r, v_r, g_r, acc = 20, 0, 4, 8, 12, 14, 16, 18, 20
            vpad = arena[:, 22 * T:22 * T + 2 * (PAD + T)].rearrange("p (t n) -> p t n", t=2)
            soft = [arena[:, 25 * T + 1280 * i:25 * T + 1280 * (i + 1)] for i in range(6)]
            m_pad = V.do(lambda e: e.memset(vpad[:, :, 0:PAD], 0.0))

            def proj_T(j, take):
                i, full = load(w_in[j])
                for n in range(2):
                    b = banks.take()
                    m = project(b.ap, KD, lambda k: ring[:, i, k * CW + n * P:k * CW + n * P + P],
                                lambda k: h[:, k, :], full, *b.free, rhs_marks=h_ready)
                    take(n, b, m)
                done_with(i, m)

            def proj_N(j, take):
                i, full = load(w_in[j])
                for t in range(NT):
                    b = banks.take()
                    m = project(b.ap[:, 0:CW], KD, lambda k: h[:, k, t * P:(t + 1) * P],
                                lambda k: ring[:, i, k * CW:(k + 1) * CW], full, *b.free)
                    take(t, b, m)
                done_with(i, m)

            def keep(dst, q=A, scale=1.0):
                def take(n, b, m):
                    if scale == 1.0:
                        mk = copy(tile(dst + n), b.ap, m, q=q)
                    else:
                        mk = act(tile(dst + n), b.ap, ACT.Copy, m, scale=scale)
                    b.release(mk)
                    ready[dst + n] = mk
                return take

            ready = {}
            a_banks = []
            proj_T(0, lambda n, b, m: a_banks.append((b, m)))

            def conv_gate(n, b, m):
                s = temps.take()
                ms = sigmoid_of(s.ap, b.ap, m, *s.free)
                b.release(ms)
                ab, ma = a_banks[n]
                mv = tt(vpad[:, n, PAD:PAD + T], ab.ap, s.ap, ALU.mult, ma, ms)
                ab.release(mv)
                s.release(mv)
                ready["v", n] = mv
            proj_T(1, conv_gate)
            for j in range(2):
                proj_T(2 + j, keep(q_sb + 2 * j, scale=HEAD ** -0.5))
            for j in range(2):
                proj_T(4 + j, keep(k_sb + 2 * j, q=V))
            for j in range(2):
                def keep_v(t, b, m, j=j):
                    mk = copy(tile(v_sb + t)[:, j * CW:(j + 1) * CW], b.ap[:, 0:CW], m, q=A)
                    b.release(mk)
                    ready["v_sb", t, j] = mk
                proj_N(6 + j, keep_v)

            def rotate(dst):
                def take(n, b, m):
                    plain = temps.take()
                    mp = copy(plain.ap, b.ap, m, *plain.free, q=A)
                    b.release(mp)
                    sw = banks.take()
                    ms = mm(sw.ap, K("swap64"), plain.ap, True, True, mp, *sw.free, last=True)
                    m1 = tt(tile(dst + n), plain.ap, K("cos64"), ALU.mult, mp)
                    turned = temps.take()
                    m2 = tt(turned.ap, sw.ap, K("sin64"), ALU.mult, ms, *turned.free)
                    sw.release(m2)
                    plain.release(m1, ms)
                    m3 = tt(tile(dst + n), tile(dst + n), turned.ap, ALU.add, m1, m2)
                    turned.release(m3)
                    ready[dst + n] = m3
                return take
            proj_T(8, rotate(q_r))
            proj_T(9, rotate(k_r))

            def keep_vr(t, b, m):
                mk = copy(arena[:, v_r * T + t * CW:v_r * T + (t + 1) * CW], b.ap[:, 0:CW], m, q=A)
                b.release(mk)
                ready["v_r", t] = mk
            proj_N(10, keep_vr)
            proj_T(11, keep(g_r, q=V))
            projected = PE.last

            def conv_taps():
                for tap in range(CONV_TAPS):
                    for n in range(2):
                        at = (layer * 2 + n) * CONV_TAPS + tap
                        w = W("conv_w", at, at + 1)
                        src = vpad[:, n, tap:tap + T]
                        if tap == 0:
                            b0 = W("conv_b", layer * 2 + n, layer * 2 + n + 1)
                            ready["conv", n] = ts(tile(acc + n), src, w, b0, ALU.mult, ALU.add, m_pad, ready["v", n])
                        else:
                            ready["conv", n] = stt(tile(acc + n), src, w, tile(acc + n), ALU.mult, ALU.add,
                                                   ready["conv", n])
                        yield
            conv = conv_taps()

            def conv_some(n):
                for _ in range(n):
                    next(conv, None)

            part = {0: (0, 0, 0), 1: (512, 1, 0), 3: (896, 1, 384), 2: (1024, 2, 0)}
            order = (0, 1, 3, 2)
            spans = ((0, 512), (512, 1024), (1024, 1280))
            turns = [Rotation(soft[2 * i:2 * i + 2]) for i in range(3)]

            def head_rows(i):
                return slice(HEAD * (i % 2), HEAD * (i % 2) + HEAD)

            def before_only(buf, queue_after):
                marks = []
                for kt in order:
                    blk = buf[:, part[kt][0]:part[kt][0] + P]
                    marks.append(G.do(lambda e, blk=blk: e.affine_select(
                        out=blk, in_=blk, compare_op=ALU.is_gt, fill=0.0, base=0, pattern=[[1, P]],
                        channel_multiplier=-1), queue_after))
                return marks[-1]

            def sb_scores(i):
                rows = head_rows(i)
                q, k = tile(q_sb + i // 2), tile(k_sb + i // 2)
                bb = [banks.take() for _ in range(3)]
                for kt in order:
                    _, bi, c = part[kt]
                    n = T - kt * P
                    m = mm(bb[bi].ap[:, c:c + n], k[rows, kt * P:(kt + 1) * P], q[rows, kt * P:T],
                           c == 0, True, *bb[bi].free, ready[q_sb + i // 2], ready[k_sb + i // 2],
                           last=True, loose=True)
                e, sp = turns[0].take(), turns[1].take()
                for bi, (a, b) in enumerate(spans):
                    me = act(e.ap[:, a:b], bb[bi].ap[:, 0:b - a], ACT.Abs, m, *e.free)
                me = act(e.ap, e.ap, ACT.Exp, me, scale=-1.0)
                me = act(e.ap, e.ap, ACT.Ln, me, bias=K("one"))
                for bi, (a, b) in enumerate(spans):
                    ms = stt(sp.ap[:, a:b], bb[bi].ap[:, 0:b - a], 0.0, e.ap[:, a:b], ALU.max, ALU.add, me, *sp.free)
                e.release(ms)
                return bb, sp, before_only(sp.ap, ms), ms

            def sb_mix(i, bb, sp, sp_ready, z_read):
                rows = head_rows(i)
                w = turns[2].take()
                for kt in order:
                    _, bi, c = part[kt]
                    for kj in range(kt, NT):
                        off, n = part[kj][0], T - kj * P
                        dst = c + (kj - kt) * P
                        m = mm(bb[bi].ap[:, dst:dst + n], K("neg_suffix" if kj == kt else "neg_ones"),
                               sp.ap[:, off:off + n], False, True, sp_ready, z_read, last=kj == NT - 1, loose=True)
                    if kt == 0:
                        m_first = m
                sp.release(m)
                for bi, (a, b) in enumerate(spans):
                    mw = act(w.ap[:, a:b], bb[bi].ap[:, 0:b - a], ACT.Exp, m_first if bi == 0 else m, *w.free)
                    bb[bi].release(mw)
                mw = before_only(w.ap, mw)
                o = banks.take()
                for kt in range(NT):
                    off, n = part[kt][0], T - kt * P
                    m = mm(o.ap[rows, kt * P:T], tile(v_sb + kt)[:, i * HEAD:(i + 1) * HEAD], w.ap[:, off:off + n],
                           kt == 0, kt == NT - 1, mw, ready["v_sb", kt, i * HEAD // CW], *o.free, last=True)
                w.release(m)
                mo = copy(h[rows, 2 + i // 2, :], o.ap[rows, :], m, projected)
                o.release(mo)
                ready["y", 2 + i // 2, i % 2] = mo

            nxt = sb_scores(0)
            for i in range(SB_HEADS):
                cur = nxt
                if i + 1 < SB_HEADS:
                    nxt = sb_scores(i + 1)
                conv_some(7)
                sb_mix(i, *cur)
            conv_some(2 * CONV_TAPS)

            def ret_scores(i):
                rows = head_rows(i)
                out = []
                for kt in range(NT):
                    n = T - kt * P
                    b, s = banks.take(), temps.take()
                    m = mm(b.ap[:, 0:n], tile(k_r + i // 2)[rows, kt * P:(kt + 1) * P],
                           tile(q_r + i // 2)[rows, kt * P:T], True, True, *b.free, ready[q_r + i // 2],
                           ready[k_r + i // 2], last=True)
                    ms = tt(s.ap[:, 0:n], b.ap[:, 0:n], K(f"decay{i}", 0, n), ALU.mult, m, *s.free)
                    b.release(ms)
                    out.append((s, ms))
                return out

            def ret_mix(i, scored):
                rows = head_rows(i)
                o = banks.take()
                for kt, (s, ms) in enumerate(scored):
                    n = T - kt * P
                    m = mm(o.ap[rows, kt * P:T], arena[:, v_r * T + kt * CW + i * HEAD:v_r * T + kt * CW + (i + 1) * HEAD],
                           s.ap[:, 0:n], kt == 0, kt == NT - 1, ms, ready["v_r", kt], *o.free, last=True)
                    s.release(m)
                y = tile(q_sb + i // 2)
                mo = copy(y[rows, :], o.ap[rows, :], m, PE.last, q=A)
                o.release(mo)
                ready["ret", i] = mo

            nxt = ret_scores(0)
            for i in range(RET_HEADS):
                cur = nxt
                if i + 1 < RET_HEADS:
                    nxt = ret_scores(i + 1)
                ret_mix(i, cur)

            mean = banks.take()
            for n in range(2):
                m = mm(mean.ap, K("ones"), tile(acc + n), n == 0, n == 1, ready["conv", n], *mean.free, last=True)
            var = SquareSum(2)
            for n in range(2):
                m1 = act(tile(k_sb + n), mean.ap, ACT.Copy, m, scale=-1.0 / 256)
                m2 = tt(tile(acc + n), tile(acc + n), tile(k_sb + n), ALU.add, m1)
                ready["conv", n] = m2
                var.add(tile(acc + n), m2)
            mean.release(m1)

            centred, hvar = [], []
            for n in range(2):
                b = banks.take()
                m = mm(b.ap, K("centre64"), tile(q_sb + n), True, True, ready["ret", 2 * n], ready["ret", 2 * n + 1],
                       *b.free, last=True)
                centred.append((b, m))
                sv = SquareSum(1, "sum64")
                sv.add(b.ap, m)
                hvar.append(sv)
            var.flush()
            r = temps.take()
            mr = inv_root(r.ap, var.bank.ap, 256, "rms_eps", var.mark, *r.free)
            var.bank.release(mr)
            for n in range(2):
                s = temps.take()
                at = layer * 2 + n
                m = stt(tile(acc + n), tile(acc + n), W("conv_ln_g", at, at + 1), r.ap, ALU.mult, ALU.mult, mr, ready["conv", n])
                m = ts(tile(acc + n), tile(acc + n), W("conv_ln_b", at, at + 1), None, ALU.add, None, m)
                ms = sigmoid_of(s.ap, tile(acc + n), m, *s.free)
                m = tt(h[:, n, :], tile(acc + n), s.ap, ALU.mult, m, ms, projected)
                s.release(m)
                ready["y", n, 0] = ready["y", n, 1] = m
            r.release(m)
            for n in range(2):
                hvar[n].flush()
                r = temps.take()
                mr = inv_root(r.ap, hvar[n].bank.ap, HEAD, "rms_eps", hvar[n].mark, *r.free)
                hvar[n].bank.release(mr)
                s = temps.take()
                ms = sigmoid_of(s.ap, tile(g_r + n), ready[g_r + n], *s.free)
                ms = tt(s.ap, s.ap, tile(g_r + n), ALU.mult, ms)
                b, _ = centred[n]
                m = tt(r.ap, b.ap, r.ap, ALU.mult, mr)
                b.release(m)
                at = layer * 2 + n
                m = stt(h[:, 6 + n, :], r.ap, W("ret_norm_g", at, at + 1), s.ap, ALU.mult, ALU.mult, m, ms, projected)
                r.release(m)
                s.release(m)
                ready["y", 6 + n, 0] = ready["y", 6 + n, 1] = m
            y_ready = [mk for n in range(KD) for mk in (ready["y", n, 0], ready["y", n, 1])]
            out_project(w_out, y_ready, lambda d, b, m: residual(d, b, m, stats), stats)

        def residual(d, b, m, stats):
            mx = tt(x[:, d, :], b.ap, x[:, d, :], ALU.add, m)
            b.release(mx)
            stats.add(x[:, d, :], mx)

        def out_project(w_out, y_ready, take, stats):
            for j in range(D // CW):
                i, full = load(w_out[j])
                for n in range(2):
                    b = banks.take()
                    m = project(b.ap, KD, lambda k: ring[:, i, k * CW + n * P:k * CW + n * P + P],
                                lambda k: h[:, k, :], full, *b.free, *(y_ready if j == 0 and n == 0 else ()))
                    take(2 * j + n, b, m)
                done_with(i, m)
                if j and stats:
                    pair, stats.waiting = stats.waiting[-2:], stats.waiting[:-2]
                    stats.flush()
                    stats.waiting = pair

        def mixer2(h_ready):
            qf, kf, v_nat = 0, 8, 16
            gpad = arena[:, 20 * T:20 * T + 6 * (GDN_TAPS - 1 + T)].rearrange("p (t n) -> p t n", t=6)
            z_t = 27
            PP = 16
            ppad = arena[:, 29 * T:29 * T + 2 * (PP + T)].rearrange("p (t n) -> p t n", t=2)
            cq, ckv = 32, 34
            prob = Rotation([tile(35 + i) for i in range(4)])
            flip = Rotation([arena[:, 39 * T + 1280 * i:39 * T + 1280 * (i + 1)] for i in range(2)])
            ab = small[:, 64:96].rearrange("p (t n) -> p t n", t=NT)
            w_in = io["w_in2"]
            ready = {}
            m_pads = (V.do(lambda e: e.memset(gpad[:, :, 0:GDN_TAPS - 1], 0.0)),
                      V.do(lambda e: e.memset(ppad[:, :, 0:PP], 0.0)))

            def proj(i, full, n, m_rows, take, at=None, rows=None):
                b = banks.take()
                c0 = n * P if at is None else at
                out = b.ap[0:m_rows, :]
                m = project(out, KD, lambda k: ring[:, i, k * CW + c0:k * CW + c0 + m_rows],
                            lambda k: h[:, k, :], full, *b.free, rhs_marks=h_ready)
                take(n, b, m)
                return m

            def keep(dst, name, q=A):
                def take(n, b, m):
                    mk = copy(dst(n), b.ap, m, *m_pads, q=q)
                    b.release(mk)
                    ready[name, n] = mk
                return take

            i, full = load(w_in[0])
            for n in range(2):
                m = proj(i, full, n, P, keep(lambda n: tile(cq + n), "cq"))
            done_with(i, m)
            i, full = load(w_in[1])
            proj(i, full, 0, P, keep(lambda n: tile(ckv), "ckv"))
            kr = Buffer(tile(44))

            def keep_kr(n, b, m):
                mk = copy(kr.ap[NOPE:QK, :], b.ap[NOPE:QK, :], m, *kr.free, q=A)
                b.release(mk)
                ready["kr"] = mk
            proj(i, full, 1, QK, keep_kr, at=P)
            b = banks.take()
            for t in range(NT):
                m = project(b.ap[:, 8 * t:8 * t + 8], KD, lambda k: h[:, k, t * P:(t + 1) * P],
                            lambda k: ring[:, i, k * CW + P + QK:k * CW + P + QK + 8], full, *b.free)
            mk = copy(ab, b.ap[:, 0:32].rearrange("p (t n) -> p t n", t=NT), m)
            b.release(mk)
            ready["ab"] = mk
            done_with(i, m)
            for g in range(3):
                i, full = load(w_in[2 + g])
                for n in range(2):
                    m = proj(i, full, n, P, keep(lambda n, g=g: gpad[:, 2 * g + n, GDN_TAPS - 1:], ("g", g), q=(A, V)[g % 2]))
                done_with(i, m)
            i, full = load(w_in[5])
            for n in range(2):
                m = proj(i, full, n, P, keep(lambda n: tile(z_t + n), "z"))
            done_with(i, m)
            i, full = load(w_in[6])
            for n in range(2):
                m = proj(i, full, n, P, keep(lambda n: ppad[:, n, PP:], "p", q=V))
            done_with(i, m)
            projected = PE.last

            def latent_norm(tiles, names, gain):
                s = SquareSum(len(tiles))
                for t, nm in zip(tiles, names):
                    s.add(tile(t), ready[nm])
                s.flush()
                r = temps.take()
                m = inv_root(r.ap, s.bank.ap, P * len(tiles), "rms_eps", s.mark, *r.free)
                s.bank.release(m)
                for n, t in enumerate(tiles):
                    mk = stt(tile(t), tile(t), W(gain, n, n + 1), r.ap, ALU.mult, ALU.mult, m)
                r.release(mk)
                return mk
            ckv_ready = latent_norm([ckv], [("ckv", 0)], "kv_norm")
            cq_ready = latent_norm([cq, cq + 1], [("cq", 0), ("cq", 1)], "q_norm")

            def rotate(rows_ap, mp, *marks):
                sw = banks.take()
                r = slice(NOPE, QK)
                ms = mm(sw.ap[r, :], K("swap32")[r, NOPE:QK], rows_ap, True, True, mp, *sw.free, last=True)
                s = temps.take()
                m2 = tt(s.ap[r, :], sw.ap[r, :], K("sin32")[r, :], ALU.mult, ms, *s.free)
                sw.release(m2)
                m1 = tt(rows_ap, rows_ap, K("cos32")[r, :], ALU.mult, mp, ms)
                m3 = tt(rows_ap, rows_ap, s.ap[r, :], ALU.add, m1, m2)
                s.release(m3)
                return m3
            ready["kr"] = rotate(kr.ap[NOPE:QK, :], ready["kr"])

            i, full = load(io["w_ukv"], MLA_HEADS * P)
            for hd in range(MLA_HEADS):
                b = banks.take()
                m = mm(b.ap[0:NOPE, :], ring[:, i, hd * P:hd * P + NOPE], tile(ckv), True, True, full, ckv_ready,
                       *b.free, last=True)
                mk = copy(tile(kf + hd)[0:NOPE, :], b.ap[0:NOPE, :], m, q=A)
                b.release(mk)
                m2 = copy(tile(kf + hd)[NOPE:QK, :], kr.ap[NOPE:QK, :], ready["kr"], q=G)
                ready["k", hd] = (mk, m2)
            for t in range(NT):
                b = banks.take()
                vcols = ring[:, i, 0:MLA_HEADS * P].rearrange("p (h c) -> p h c", c=P)[:, :, NOPE:P]
                m = mm(b.ap, tile(ckv)[:, t * P:(t + 1) * P], vcols, True, True, *b.free, last=True)
                mk = copy(tile(v_nat + t), b.ap, m, q=V)
                b.release(mk)
                ready["v", t] = mk
            done_with(i, m)
            i, full = load(io["w_uq"], 2 * MLA_HEADS * QK)
            for hd in range(MLA_HEADS):
                b = banks.take()
                for k in range(2):
                    c0 = k * MLA_HEADS * QK + hd * QK
                    m = mm(b.ap[0:QK, :], ring[:, i, c0:c0 + QK], tile(cq + k), k == 0, k == 1, full, cq_ready,
                           *b.free, last=True)
                mk = copy(tile(qf + hd)[0:QK, :], b.ap[0:QK, :], m, q=A)
                b.release(mk)
                ready["q", hd] = rotate(tile(qf + hd)[NOPE:QK, :], mk)
            done_with(i, m)

            scale = QK ** -0.5
            mx, neg, rs = small[:, 96:128], small[:, 128:160], small[:, 160:192]

            def mla_scores(hd):
                out = []
                for t in range(NT):
                    n = (t + 1) * P
                    c = hd * NT + t
                    b, p = banks.take(), prob.take()
                    m = mm(b.ap[:, 0:n], tile(qf + hd)[0:QK, t * P:n], tile(kf + hd)[0:QK, 0:n], True, True,
                           *b.free, ready["q", hd], *ready["k", hd], last=True)
                    m = V.do(lambda e, b=b, n=n: e.memset(b.ap[0:CHUNK, n - CHUNK:n], -BIG), m)
                    m = V.do(lambda e, b=b, n=n, c=c: e.tensor_reduce(mx[:, c:c + 1], b.ap[:, 0:n], AXX, ALU.max), m)
                    m = ts(neg[:, c:c + 1], mx[:, c:c + 1], -scale, None, ALU.mult, None, m)
                    m = act(p.ap[:, 0:n], b.ap[:, 0:n], ACT.Exp, m, *p.free, scale=scale, bias=neg[:, c:c + 1],
                            accum=rs[:, c:c + 1])
                    b.release(m)
                    m = V.do(lambda e, c=c: e.reciprocal(rs[:, c:c + 1], rs[:, c:c + 1]), m)
                    m = ts(p.ap[:, 0:n], p.ap[:, 0:n], rs[:, c:c + 1], None, ALU.mult, None, m)
                    out.append((p, m))
                return out

            part = {0: (0, 0, 0), 1: (512, 1, 0), 3: (896, 1, 384), 2: (1024, 2, 0)}
            spans = ((0, 512), (512, 1024), (1024, 1280))

            def mla_mix(hd, probs):
                rows = slice(HEAD * (hd % 2), HEAD * (hd % 2) + HEAD)
                bb, f = [banks.take() for _ in range(3)], flip.take()
                for t, (p, mp) in enumerate(probs):
                    for kt in range(t + 1):
                        _, bi, c = part[kt]
                        c += (t - kt) * P
                        m = PE.do(lambda e, o=bb[bi].ap[:, c:c + P], s=p.ap[:, kt * P:(kt + 1) * P]:
                                  e.transpose(o, s, K("ident")), mp, *bb[bi].free)
                    p.release(m)
                for bi, (a, b) in enumerate(spans):
                    mf = copy(f.ap[:, a:b], bb[bi].ap[:, 0:b - a], m, *f.free, q=V if bi == 0 else A)
                    bb[bi].release(mf)
                    if bi == 0:
                        mf0 = mf
                o = banks.take()
                for kt in range(NT):
                    off, n = part[kt][0], T - kt * P
                    m = mm(o.ap[rows, kt * P:T], tile(v_nat + kt)[:, hd * HEAD:(hd + 1) * HEAD], f.ap[:, off:off + n],
                           kt == 0, kt == NT - 1, mf0, mf, ready["v", kt], *o.free, last=True)
                f.release(m)
                mo = copy(h[rows, hd // 2, :], o.ap[rows, :], m, projected, q=A)
                o.release(mo)
                ready["y", hd // 2, hd % 2] = mo

            for hd in range(MLA_HEADS):
                mla_mix(hd, mla_scores(hd))

            s2, s4 = (arena[:, 35 * T + i * 2 * (PP + T):35 * T + (i + 1) * 2 * (PP + T)].rearrange(
                "p (t n) -> p t n", t=2) for i in range(2))
            fence()
            lo, hi = slice(0, 64), slice(64, 128)
            sums = {}
            src, mk = ppad, (ready["p", 0], ready["p", 1], *m_pads)
            W16 = PP + T
            sel = [tile(41), tile(42)]
            m = None
            cur, nxt_ = ppad, [s2, s4]
            for lvl, sh in enumerate((1, 2, 4, 8)):
                dst = nxt_[lvl % 2]
                ma = V.do(lambda e, d=dst, c=cur, sh=sh: e.tensor_copy(d[:, :, 0:sh], c[:, :, 0:sh]), *(mk if m is None else (m,)))
                mb = tt(dst[:, :, sh:W16], cur[:, :, sh:W16], cur[:, :, 0:W16 - sh], ALU.add, *(mk if m is None else (m,)))
                g, rows = lvl // 2, (lo, hi)[lvl % 2]
                mc = tt(sel[g][rows, :], dst[rows, g, PP:W16], K(f"inv_count{g}")[rows, :], ALU.mult, ma, mb)
                m = mc
                cur = dst
            scaled = []
            for g in range(2):
                m1 = tt(sel[g], sel[g], ppad[:, g, PP:W16], ALU.subtract, m)
                b, b2 = banks.take(), banks.take()
                mA = mm(b.ap[lo, :], W("pool_w", g * 64, g * 64 + 64)[lo, :], sel[g][lo, :], True, True, m1, *b.free, last=True)
                mB = mm(b2.ap[hi, :], W("pool_w", g * 64, g * 64 + 64)[hi, :], sel[g][hi, :], True, True, m1, *b2.free, last=True)
                for bb_, rows, mm_ in ((b, lo, mA), (b2, hi, mB)):
                    mk2 = ts(h[rows, 6 + g, :], bb_.ap[rows, :], W("pool_scale", g, g + 1)[rows, :], None, ALU.mult, None,
                             mm_, projected)
                    bb_.release(mk2)
                    ready["y", 6 + g, 0 if rows is lo else 1] = mk2

            fence()
            gtemps = Rotation([tile(15), tile(46), tile(47)])
            qkv = arena[:, 0:6 * T]
            sig = arena[:, 6 * T:12 * T]
            mc = []
            for n in range(6):
                for tap in range(GDN_TAPS):
                    w = W("gdn_conv", n * GDN_TAPS + tap, n * GDN_TAPS + tap + 1)
                    src = gpad[:, n, tap:tap + T]
                    if tap == 0:
                        m = ts(tile(n), src, w, None, ALU.mult, None)
                    else:
                        m = stt(tile(n), src, w, tile(n), ALU.mult, ALU.add, m)
            m = sigmoid_of(sig, qkv, m)
            conv_ready = tt(qkv, qkv, sig, ALU.mult, m)
            qT, kT, vT = (lambda f: tile(f)), (lambda f: tile(2 + f)), (lambda f: tile(4 + f))
            unit = []
            for n in range(4):
                s = gtemps.take()
                m = act(s.ap, tile(n), ACT.Square, conv_ready, *s.free)
                b = banks.take()
                m = mm(b.ap, K("sum64"), s.ap, True, True, m, *b.free, last=True)
                s.release(m)
                r = gtemps.take()
                m = inv_root(r.ap, b.ap, 1.0, "rms_eps", m, *r.free)
                b.release(m)
                m = stt(tile(n), tile(n), HEAD ** -0.5 if n < 2 else 1.0, r.ap, ALU.mult, ALU.mult, m)
                r.release(m)
                unit.append(m)

            def cols(a):
                return small[:, a:a + 16]
            g_c, beta_c, t_c, gc_c, be_c, kd_c, dt_c = (cols(a) for a in (192, 208, 224, 240, 256, 272, 288))
            bc = small[:, 304:312]
            b = banks.take()
            m = mm(b.ap[:, 0:8], K("ones")[0:1, :], rowp[0:1, 0:8], True, True, *b.free, last=True)
            m = copy(bc, b.ap[:, 0:8], m)
            b.release(m)
            m_exp = act(bc[:, 4:8], bc[:, 4:8], ACT.Exp, m)
            for t in range(NT):
                m = tt(dt_c[:, 4 * t:4 * t + 4], ab[:, t, 0:4], bc[:, 0:4], ALU.add, m)
            m1 = act(t_c, dt_c, ACT.Abs, m)
            m1 = act(t_c, t_c, ACT.Exp, m1, scale=-1.0)
            m1 = act(t_c, t_c, ACT.Ln, m1, bias=K("one"))
            m1 = stt(t_c, dt_c, 0.0, t_c, ALU.max, ALU.add, m1)
            for t in range(NT):
                m1 = stt(g_c[:, 4 * t:4 * t + 4], t_c[:, 4 * t:4 * t + 4], -1.0, bc[:, 4:8], ALU.mult, ALU.mult, m1, m_exp)
            m2 = act(beta_c.rearrange("p (t n) -> p t n", t=NT), ab[:, :, 4:8], ACT.Exp, ready["ab"], scale=-1.0)
            m2 = ts(beta_c, beta_c, 1.0, None, ALU.add, None, m2)
            m2 = V.do(lambda e: e.reciprocal(beta_c, beta_c), m2)
            b = banks.take()
            m = mm(b.ap[:, 0:16], K("incl"), g_c, True, True, m1, *b.free, last=True)
            mB = mm(b.ap[:, 16:32], K("later"), g_c, True, True, last=True)
            m = copy(gc_c, b.ap[:, 0:16], mB)
            me = act(be_c, b.ap[:, 0:16], ACT.Exp, mB, m)
            me2 = act(kd_c, b.ap[:, 16:32], ACT.Exp, mB, m)
            b.release(m, me2)
            gates = tt(be_c, be_c, beta_c, ALU.mult, me, m2)
            gates2 = (m, me2, gates)

            AT, QKT, TT, UU, XX = 38, 42, 6, 20, 10
            BT = (24, 25, 26, 14)
            eB, kb = (36, 37), (32, 33)
            for hd in range(GDN_HEADS):
                rows, f = slice(HEAD * (hd % 2), HEAD * (hd % 2) + HEAD), hd // 2
                gb, bbk = banks.take(), banks.take()
                for which, col, mat, bank in ((0, g_c, "incl", gb), (1, beta_c, "ident", bbk)):
                    s = gtemps.take()
                    for t in range(NT):
                        c = 4 * t + hd
                        m = ts(s.ap[:, t * P:(t + 1) * P], K("ones"), col[:, c:c + 1], None, ALU.mult, None,
                               *s.free, m1, m2, q=G)
                    for t in range(NT):
                        m = mm(bank.ap[:, t * P:(t + 1) * P], s.ap[:, t * P:(t + 1) * P], K(mat), True, True, m,
                               *bank.free, last=True)
                    s.release(m)
                    if which == 0:
                        m_gb = m
                    else:
                        m_bb = m
                me = act(tile(eB[f])[rows, :], gb.ap[rows, :], ACT.Exp, m_gb)
                ready["e", hd] = me
                dT = gtemps.take()
                for t in range(NT):
                    c = 4 * t + hd
                    m = ts(dT.ap[:, t * P:(t + 1) * P], gb.ap[:, t * P:(t + 1) * P], gc_c[:, c:c + 1], 0.0,
                           ALU.subtract, ALU.min, m_gb, me, *dT.free, *gates2)
                gb.release(m, me)
                m = act(dT.ap, dT.ap, ACT.Exp, m)
                m_kb = tt(tile(kb[f])[rows, :], kT(f)[rows, :], bbk.ap[rows, :], ALU.mult, m_bb, unit[2 + f])
                bbk.release(m_kb)
                ab_, qb_ = banks.take(), banks.take()
                for bank, rhs in ((ab_, tile(kb[f])), (qb_, qT(f))):
                    for t in range(NT):
                        sl = slice(t * P, (t + 1) * P)
                        mk = mm(bank.ap[:, sl], kT(f)[rows, sl], rhs[rows, sl], True, True, m_kb, unit[f], unit[2 + f],
                                *bank.free, last=True)
                for bank, dst, mask in ((ab_, AT + hd, "strict"), (qb_, QKT + hd, "incl")):
                    m3 = tt(tile(dst), bank.ap, dT.ap, ALU.mult, mk, m)
                    bank.release(m3)
                    for t in range(NT):
                        sl = slice(t * P, (t + 1) * P)
                        m4 = tt(tile(dst)[:, sl], tile(dst)[:, sl], K(mask), ALU.mult, m3, q=G)
                    ready[dst] = m4
                dT.release(m3)

            t_ready, u_ready = {}, {}
            for lv in range(6):
                for hd in range(GDN_HEADS):
                    B_, X_ = tile(BT[hd]), tile(XX + hd)
                    T_, U_ = tile(TT + hd), tile(UU + hd)
                    for t in range(NT):
                        sl = slice(t * P, (t + 1) * P)
                        mb = tt(B_[:, sl], tile(AT + hd)[:, sl], K(f"level{lv}"), ALU.mult, ready[AT + hd],
                                *((u_ready[hd], t_ready[hd]) if lv else ()), q=G)
                    b = banks.take()
                    for t in range(NT):
                        sl = slice(t * P, (t + 1) * P)
                        m = mm(b.ap[:, sl], B_[:, sl], K("ident") if lv == 0 else T_[:, sl], True, True, mb, *b.free,
                               *((t_ready[hd],) if lv else ()), last=True)
                    if lv == 0:
                        for t in range(NT):
                            sl = slice(t * P, (t + 1) * P)
                            t_ready[hd] = tt(T_[:, sl], K("ident"), b.ap[:, sl], ALU.subtract, m)
                            u_ready[hd] = tt(U_[:, sl], K("ident"), B_[:, sl], ALU.subtract, mb)
                        b.release(t_ready[hd])
                        continue
                    mx_ = copy(X_, b.ap, m, q=A)
                    b.release(mx_)
                    b1, b2 = banks.take(), banks.take()
                    for t in range(NT):
                        sl = slice(t * P, (t + 1) * P)
                        if lv < 5:
                            ma_ = mm(b1.ap[:, sl], U_[:, sl], X_[:, sl], True, True, mx_, u_ready[hd], *b1.free, last=True)
                        mb_ = mm(b2.ap[:, sl], X_[:, sl], U_[:, sl], True, True, mx_, u_ready[hd], *b2.free, last=True)
                    if lv < 5:
                        t_ready[hd] = tt(T_, T_, b1.ap, ALU.subtract, ma_, mb_)
                        b1.release(t_ready[hd])
                    else:
                        b1.release(*b1.free)
                    u_ready[hd] = tt(U_, U_, b2.ap, ALU.subtract, mb_)
                    b2.release(u_ready[hd])

            fence()
            knat, vb, kbg, kdc, uu, wT, qd, oT = (arena[:, a * T:(a + 2) * T] for a in (6, 8, 10, 12, 14, 16, 18, 34))
            for src, dst in ((2, knat), (4, vb)):
                for half in range(2):
                    b = banks.take()
                    for tl in range(2):
                        t = 2 * half + tl
                        for f in range(2):
                            m = PE.do(lambda e, o=b.ap[:, tl * CW + f * P:tl * CW + (f + 1) * P],
                                      s=tile(src + f)[:, t * P:(t + 1) * P]: e.transpose(o, s, K("ident")), *b.free)
                    mk = copy(dst[:, half * T:(half + 1) * T], b.ap, m, q=(V, A)[half])
                    b.release(mk)
                    ready["nat", src, half] = mk
            nat = [ready["nat", s, hf] for s in (2, 4) for hf in range(2)]
            for c in range(16):
                sl = slice(c * HEAD, (c + 1) * HEAD)
                m_kbg = ts(kbg[:, sl], knat[:, sl], be_c[:, c:c + 1], None, ALU.mult, None, *nat)
                m_vb = ts(vb[:, sl], vb[:, sl], beta_c[:, c:c + 1], None, ALU.mult, None, *nat)
                m_kd = ts(kdc[:, sl], knat[:, sl], kd_c[:, c:c + 1], None, ALU.mult, None, *nat, q=G)
            for f in range(2):
                m_qd = tt(qd[:, f * T:(f + 1) * T], qT(f), tile(eB[f]), ALU.mult)
            ub = [banks.take(), banks.take()]
            for c in range(16):
                t, hd = c // 4, c % 4
                m = mm(ub[c // 8].ap[:, c % 8 * HEAD:(c % 8 + 1) * HEAD], tile(UU + hd)[:, t * P:(t + 1) * P],
                       vb[:, c * HEAD:(c + 1) * HEAD], True, True, m_vb, *ub[c // 8].free, last=True)
            for i in range(2):
                m_u = copy(uu[:, i * T:(i + 1) * T], ub[i].ap, m)
                ub[i].release(m_u)
            for f in range(2):
                bp = [banks.take(), banks.take()]
                for t in range(NT):
                    for par in range(2):
                        hd, c = 2 * f + par, 4 * t + 2 * f + par
                        rows = slice(HEAD * par, HEAD * par + HEAD)
                        m = mm(bp[par].ap[rows, t * P:(t + 1) * P], kbg[:, c * HEAD:(c + 1) * HEAD],
                               tile(UU + hd)[:, t * P:(t + 1) * P], True, True, m_kbg, *bp[par].free, last=True)
                for par in range(2):
                    rows = slice(HEAD * par, HEAD * par + HEAD)
                    m_w = copy(wT[rows, f * T:(f + 1) * T], bp[par].ap[rows, :], m, q=A)
                    bp[par].release(m_w)

            state = tile(46)[:, 0:2 * HEAD]
            vn = tile(47)[:, 0:4 * HEAD]
            m_s = [V.do(lambda e: e.memset(state, 0.0))] * 2
            m_vn0 = V.do(lambda e: e.memset(vn, 0.0))
            m_vn = m_vn0
            last_o = ()
            for ch in range(T // CHUNK):
                t, c0 = ch // 2, CHUNK * (ch % 2)
                crow = slice(c0, c0 + CHUNK)
                csl = slice(ch * CHUNK, (ch + 1) * CHUNK)
                vbk = [banks.take(), banks.take()]
                for hd in range(GDN_HEADS):
                    f, par = hd // 2, hd % 2
                    rows = slice(HEAD * par, HEAD * par + HEAD)
                    m = mm(vbk[par].ap[crow, f * HEAD:(f + 1) * HEAD], wT[rows, f * T + ch * CHUNK:f * T + (ch + 1) * CHUNK],
                           state[rows, f * HEAD:(f + 1) * HEAD], True, True, m_w, *m_s, *vbk[par].free, last=True)
                for par in range(2):
                    u_ = uu.rearrange("p (t f q d) -> p t f q d", t=NT, f=2, q=2)[crow, t, :, par, :]
                    o_ = vn.rearrange("p (f q d) -> p f q d", f=2, q=2)[crow, :, par, :]
                    m_vn = tt(o_, u_, vbk[par].ap[crow, 0:2 * HEAD].rearrange("p (f d) -> p f d", f=2), ALU.subtract,
                              m, m_u, m_vn0, *last_o)
                    vbk[par].release(m_vn)
                sbk = [banks.take(), banks.take()]
                for hd in range(GDN_HEADS):
                    f, par = hd // 2, hd % 2
                    rows = slice(HEAD * par, HEAD * par + HEAD)
                    c = 4 * t + hd
                    m = mm(sbk[par].ap[rows, f * HEAD:(f + 1) * HEAD], kdc[crow, c * HEAD:(c + 1) * HEAD],
                           vn[crow, hd * HEAD:(hd + 1) * HEAD], True, True, m_vn, m_kd, *sbk[par].free, last=True)
                obk = [banks.take(), banks.take()]
                for hd in range(GDN_HEADS):
                    f, par = hd // 2, hd % 2
                    rows = slice(HEAD * par, HEAD * par + HEAD)
                    o = obk[par].ap[rows, f * HEAD:(f + 1) * HEAD]
                    mm(o, state[rows, f * HEAD:(f + 1) * HEAD], qd[rows, f * T + ch * CHUNK:f * T + (ch + 1) * CHUNK],
                       True, False, m_qd, *obk[par].free)
                    mo = mm(o, vn[:, hd * HEAD:(hd + 1) * HEAD], tile(QKT + hd)[:, csl], False, True, m_vn, last=True)
                m_s = []
                for hd in range(GDN_HEADS):
                    f, par = hd // 2, hd % 2
                    rows = slice(HEAD * par, HEAD * par + HEAD)
                    st = state[rows, f * HEAD:(f + 1) * HEAD]
                    m_s.append(stt(st, st, tile(eB[f])[rows, (ch + 1) * CHUNK - 1:(ch + 1) * CHUNK],
                                   sbk[par].ap[rows, f * HEAD:(f + 1) * HEAD], ALU.mult, ALU.add, m, mo))
                for par in range(2):
                    sbk[par].release(m_s[-1])
                    rows = slice(HEAD * par, HEAD * par + HEAD)
                    m_o = copy(oT.rearrange("p (f n) -> p f n", f=2)[rows, :, csl],
                               obk[par].ap[rows, 0:2 * HEAD].rearrange("p (f d) -> p f d", f=2), mo, q=A)
                    obk[par].release(m_o)
                last_o = (mo,)
            for f in range(2):
                s, r = gtemps_late[f]
                o_ = oT[:, f * T:(f + 1) * T]
                m = act(tile(s), o_, ACT.Square, m_o)
                b = banks.take()
                m = mm(b.ap, K("sum64"), tile(s), True, True, m, *b.free, last=True)
                m = inv_root(tile(r), b.ap, HEAD, "rms_eps", m)
                b.release(m)
                m = stt(o_, o_, W("gdn_g"), tile(r), ALU.mult, ALU.mult, m)
                m2 = sigmoid_of(tile(s), tile(z_t + f), m)
                m2 = tt(tile(s), tile(s), tile(z_t + f), ALU.mult, m2)
                m = tt(h[:, 4 + f, :], o_, tile(s), ALU.mult, m, m2)
                ready["y", 4 + f, 0] = ready["y", 4 + f, 1] = m
            return [mk for n in range(KD) for mk in (ready["y", n, 0], ready["y", n, 1])]
        gtemps_late = ((6, 8), (10, 12))

        def layer_norm(marks, gain, shift):
            mean = banks.take()
            for k in range(KD):
                m = mm(mean.ap, K("ones"), x[:, k, :], k == 0, k == KD - 1, marks[k], *mean.free, last=True)
            mu = Buffer(tile(39))
            m = act(mu.ap, mean.ap, ACT.Copy, m, V.last, scale=-1.0 / D)
            mean.release(m)
            var = SquareSum(KD)
            for k in range(KD):
                mc_ = tt(x[:, k, :], x[:, k, :], mu.ap, ALU.add, m)
                var.add(x[:, k, :], mc_)
                var.flush()
            r = temps.take()
            m = inv_root(r.ap, var.bank.ap, D, "ln_eps", var.mark, *r.free)
            var.bank.release(m)
            out = []
            for k in range(KD):
                m1 = stt(x[:, k, :], x[:, k, :], W(gain, k, k + 1), r.ap, ALU.mult, ALU.mult, m)
                out.append(ts(x[:, k, :], x[:, k, :], W(shift, k, k + 1), None, ALU.add, None, m1))
            r.release(out[-1])
            return out

        def modulate(x_ready, which):
            sh, sc = which * 3 * KD, which * 3 * KD + KD
            return [ts(h[:, k, :], x[:, k, :], mod[:, sc + k:sc + k + 1], mod[:, sh + k:sh + k + 1], ALU.mult, ALU.add,
                       x_ready[k], PE.last) for k in range(KD)]

        def gated(d, src, which, m, release=None):
            gt = which * 3 * KD + 2 * KD + d
            s = temps.take()
            m = ts(s.ap, src, mod[:, gt:gt + 1], None, ALU.mult, None, m, *s.free)
            if release:
                release(m)
            m = stt(x[:, d, :], x[:, d, :], ALPHA, s.ap, ALU.mult, ALU.add, m)
            s.release(m)
            return m

        def moe(h_ready):
            y = lambda d: tile(d)
            wsel = tile(8)
            nat = small[:, 320:448]
            m_rows = None
            for t in range(NT):
                b = banks.take()
                for k in range(KD):
                    mm(b.ap[:, 0:36], h[:, k, t * P:(t + 1) * P], W("router_w", 36 * k, 36 * k + 36), k == 0, False,
                       h_ready[k], *b.free)
                m = mm(b.ap[:, 0:36], K("ones")[0:1, :], rowp[0:1, 8:44], False, True, last=True)
                g8, top, e_ = nat[:, 0:8], nat[:, 8:16], nat[:, 16:24]
                m1 = copy(g8[:, 0:4], b.ap[:, 0:4], m)
                m1 = copy(g8[:, 4:8], K("pad"), m1)
                m1 = V.do(lambda e: e.max(top, g8), m1)
                idx = small[:, 448:456].bitcast(U32)
                m1 = V.do(lambda e: e.max_index(idx, top, g8), m1)
                gi, gp, ng = nat[:, 24:25], nat[:, 25:26], nat[:, 26:27]
                m1 = copy(gi, idx[:, 0:1], m1)
                m1 = ts(ng, top[:, 0:1], -1.0, None, ALU.mult, None, m1)
                m1 = act(e_[:, 0:4], g8[:, 0:4], ACT.Exp, m1, bias=ng, accum=gp)
                m1 = V.do(lambda e: e.reciprocal(gp, gp), m1)
                lg, keep_ = nat[:, 32:64], nat[:, 64:96]
                m1 = ts(nat[:, 27:28], gi, float(PER_GROUP), None, ALU.mult, None, m1)
                m1 = ts(keep_, K("expert_id"), nat[:, 27:28], None, ALU.subtract, None, m1)
                m1 = ts(lg, keep_, 0.0, None, ALU.is_ge, None, m1)
                m1 = ts(keep_, keep_, float(PER_GROUP), None, ALU.is_lt, None, m1)
                m1 = tt(keep_, keep_, lg, ALU.mult, m1)
                m1 = ts(lg, keep_, 1.0, BIG, ALU.subtract, ALU.mult, m1)
                m1 = tt(keep_, keep_, b.ap[:, 4:36], ALU.mult, m1)
                b.release(m1)
                m1 = tt(lg, lg, keep_, ALU.add, m1)
                m1 = V.do(lambda e: e.max(top, lg), m1)
                m1 = V.do(lambda e: e.max_index(idx, top, lg), m1)
                i2, d2 = nat[:, 28:30], nat[:, 30:31]
                m1 = copy(i2, idx[:, 0:2], m1)
                m1 = tt(d2, top[:, 1:2], top[:, 0:1], ALU.subtract, m1)
                m1 = act(d2, d2, ACT.Exp, m1)
                w1, w2 = nat[:, 96:97], nat[:, 97:98]
                m1 = ts(w1, d2, 1.0, None, ALU.add, None, m1)
                m1 = V.do(lambda e: e.reciprocal(w1, w1), m1)
                m1 = tt(w1, w1, gp, ALU.mult, m1)
                m1 = tt(w2, w1, d2, ALU.mult, m1)
                m1 = ts(lg, K("expert_id"), i2[:, 0:1], w1, ALU.is_equal, ALU.mult, m1)
                m1 = ts(keep_, K("expert_id"), i2[:, 1:2], w2, ALU.is_equal, ALU.mult, m1)
                m1 = tt(lg, lg, keep_, ALU.add, m1)
                b = banks.take()
                m = PE.do(lambda e, b=b: e.transpose(b.ap[0:EXPERTS, 0:P], lg, K("ident")), m1, *b.free)
                m_rows = copy(wsel[0:EXPERTS, t * P:(t + 1) * P], b.ap[0:EXPERTS, 0:P], m)
                b.release(m_rows)
                V.wait(m_rows)
            sel_t = Rotation([tile(9)[0:EXPERTS, i * P:(i + 1) * P] for i in range(4)])
            actt = Rotation([tile(10 + i) for i in range(6)])
            y_ready = [None] * KD
            held = None

            def down(e, slots, hid):
                i, full = slots
                for d in range(KD):
                    b = banks.take()
                    for k in range(2):
                        m = mm(b.ap, ring[:, i, k * D + d * P:k * D + (d + 1) * P], hid[k][0].ap, k == 0, k == 1, full,
                               hid[k][1], *b.free, last=True)
                    if e == 0:
                        y_ready[d] = copy(y(d), b.ap, m)
                    else:
                        y_ready[d] = tt(y(d), b.ap, y(d), ALU.add, m, y_ready[d])
                    b.release(y_ready[d])
                for k in range(2):
                    hid[k][0].release(m)
                done_with(i, m)

            for e in range(EXPERTS):
                ig, fg = load(io["moe_gate"][e])
                iu, fu = load(io["moe_up"][e])
                s = sel_t.take()
                m = ts(s.ap, K("ones")[0:EXPERTS, :], K("ident")[0:EXPERTS, e:e + 1], None, ALU.mult, None, *s.free, q=G)
                wb = banks.take()
                m = mm(wb.ap, s.ap, wsel[0:EXPERTS, :], True, True, m, m_rows, *wb.free, last=True)
                s.release(m)
                wbs = temps.take()
                m_w = copy(wbs.ap, wb.ap, m, *wbs.free, q=A)
                wb.release(m_w)
                hid = []
                for n in range(2):
                    bg, bu = banks.take(), banks.take()
                    mg = project(bg.ap, KD, lambda k: ring[:, ig, k * CW + n * P:k * CW + n * P + P],
                                 lambda k: h[:, k, :], fg, *bg.free)
                    mu = project(bu.ap, KD, lambda k: ring[:, iu, k * CW + n * P:k * CW + n * P + P],
                                 lambda k: h[:, k, :], fu, *bu.free)
                    s, a_ = temps.take(), actt.take()
                    m = sigmoid_of(s.ap, bg.ap, mg, *s.free)
                    m = tt(s.ap, bg.ap, s.ap, ALU.mult, m)
                    bg.release(m)
                    m = tt(s.ap, bu.ap, s.ap, ALU.mult, m, mu)
                    bu.release(m)
                    m = tt(a_.ap, s.ap, wbs.ap, ALU.mult, m, m_w, *a_.free, q=G)
                    s.release(m)
                    hid.append((a_, m))
                wbs.release(m)
                done_with(ig, mg)
                done_with(iu, mu)
                if held:
                    down(*held)
                held = (e, load(io["moe_down"][e]), hid)
            down(*held)
            return y_ready

        def run():
            stats = SquareSum(KD)
            for k in range(KD):
                stats.add(x[:, k, :])
                stats.flush()
            c_ready = mod_start()
            for layer in range(DEPTH):
                hr = rms_to_h(stats, "ffn1_norm", layer * KD)
                stats = SquareSum(KD)
                aside = None
                if layer == 0:
                    def aside(j):
                        for n in range(24 * j // 11, 24 * (j + 1) // 11):
                            mod_marks.append(mod_step(n, c_ready))
                ffn(hr, io["ffn1_in"][layer], io["ffn1_out"][layer], stats, aside)
                if layer == 0:
                    for a in (KD, 4 * KD):
                        sl = mod[:, a:a + 2 * KD]
                        mod_marks.append(ts(sl, sl, 1.0, None, ALU.add, None, *mod_marks))
                if stage("ffn1"):
                    return
                hr = rms_to_h(stats, "mix_norm", layer * KD)
                fence()
                stats = SquareSum(KD)
                mixer1(layer, hr, stats)
                if stage("mix1"):
                    return
                hr = rms_to_h(stats, "ffn2_norm", layer * KD)
                fence()
                stats = SquareSum(KD)
                ffn(hr, io["ffn2_in"][layer], io["ffn2_out"][layer], stats)
                if stage("ffn2"):
                    return
            stats.flush()
            r = temps.take()
            m = inv_root(r.ap, stats.bank.ap, D, "rms_eps", stats.mark, *r.free)
            stats.bank.release(m)
            xr = [stt(x[:, k, :], x[:, k, :], W("final_norm", k, k + 1), r.ap, ALU.mult, ALU.mult, m) for k in range(KD)]
            r.release(xr[-1])
            fence()
            if stage("first"):
                return
            hr = modulate(xr, 0)
            V.wait(hr[-1])
            nonlocal_temps(45, 48)
            y_ready = mixer2(hr)
            fence()
            nonlocal_temps(40, 48)
            if stage("mixed"):
                for k in range(KD):
                    copy(x[:, k, :], h[:, k, :])
                return
            xr = [None] * KD

            def take(d, b, m):
                xr[d] = gated(d, b.ap, 0, m, b.release)
            out_project(io["w_out2"], y_ready, take, None)
            xr = layer_norm(xr, "ln1_g", "ln1_b")
            if stage("ln1"):
                return
            hr = modulate(xr, 1)
            fence()
            ym = moe(hr)
            xr = [gated(d, tile(d), 1, ym[d]) for d in range(KD)]
            layer_norm(xr, "ln2_g", "ln2_b")

        def nonlocal_temps(a, b):
            temps.buffers, temps.n = [Buffer(tile(i)) for i in range(a, b)], 0

        seen = {}
        mod_marks = []

        def stage(name):
            seen[name] = seen.get(name, 0) + 1
            return stages == f"{name}.{seen[name]}"

        run()
        S.wait(V.last)
        S.steps.append(lambda e: e.dma_start(io["outT"].rearrange("(t p) n -> p t n", p=P), x[:, :, :]).then_inc(s_out, 16))
        S.wait((s_out, 16))

        block = ctx.enter_context(nc.Block())

        @block.sync
        def _(e):
            for s in S.steps:
                s(e)

        @block.scalar
        def _(e):
            for s in A.steps:
                s(e)

        @block.vector
        def _(e):
            for s in V.steps:
                s(e)

        @block.gpsimd
        def _(e):
            for s in G.steps:
                s(e)

        @block.tensor
        def _(e):
            for s in PE.steps:
                s(e)


def column_chunks(w):
    *lead, k, n = w.shape
    w = w.reshape(*lead, k // P, P, n // CW, CW)
    w = np.moveaxis(w, -2, -4)
    return np.ascontiguousarray(np.swapaxes(w, -3, -2)).reshape(*lead, n // CW, P, k // P * CW)


def feature_columns(v):
    v = np.asarray(v)
    return v.reshape(-1, P).T


def pack(i):
    a = {k: np.asarray(v) for k, v in i.items()}
    w2 = a["w_in_2"][0]
    perm = np.concatenate([np.arange(0, 384), np.arange(320, 416), np.arange(1440, 1448), np.arange(0, 24),
                           np.arange(416, 1440), np.arange(1448, 1704)])
    params = {
        "ffn1_norm": feature_columns(a["ffn1_norm"]), "mix_norm": feature_columns(a["mix_norm"]),
        "ffn2_norm": feature_columns(a["ffn2_norm"]), "final_norm": feature_columns(a["final_norm"]),
        "conv_w": a["conv_w"].reshape(DEPTH, CONV_TAPS, 2, P).transpose(3, 0, 2, 1).reshape(P, -1),
        "conv_b": feature_columns(a["conv_b"]), "conv_ln_g": feature_columns(a["conv_ln_g"]),
        "conv_ln_b": feature_columns(a["conv_ln_b"]), "ret_norm_g": feature_columns(a["ret_norm_g"]),
        "c": feature_columns(a["c_2"]), "b_mod": feature_columns(a["b_mod_2"]),
        "q_norm": feature_columns(a["mla_q_norm_2"]), "kv_norm": feature_columns(a["mla_kv_norm_2"]),
        "gdn_conv": a["gdn_conv_2"][0].reshape(GDN_TAPS, 6, P).transpose(2, 1, 0).reshape(P, -1),
        "gdn_g": np.concatenate([a["gdn_out_norm_2"][0]] * 2)[:, None],
        "pool_scale": feature_columns(a["pool_scale_2"]),
        "pool_w": a["pool_w_2"][0].reshape(2, 2, 64, 64).transpose(1, 2, 0, 3).reshape(P, 128),
        "router_w": np.concatenate([a["router_w_group_2"][0], a["router_w_expert_2"][0]], 1)
        .reshape(KD, P, 36).transpose(1, 0, 2).reshape(P, -1),
        "ln1_g": feature_columns(a["ln1_g_2"]), "ln1_b": feature_columns(a["ln1_b_2"]),
        "ln2_g": feature_columns(a["ln2_g_2"]), "ln2_b": feature_columns(a["ln2_b_2"]),
    }
    return {
        "xT": np.ascontiguousarray(a["x"][0].T),
        "consts": np.concatenate(list(CONSTS.values()), 1),
        "params": np.ascontiguousarray(np.concatenate([params[k] for k in PARAM_AT], 1)),
        "rows": np.concatenate([a["gdn_dt_bias_2"][0], a["gdn_a_log_2"][0], a["router_b_group_2"][0],
                                a["router_b_expert_2"][0]])[None, :],
        "ffn1_in": column_chunks(a["ffn1_w_in"]), "ffn1_out": column_chunks(a["ffn1_w_out"]),
        "mix_w_in": column_chunks(a["mix_w_in"]), "mix_w_out": column_chunks(a["mix_w_out"]),
        "ffn2_in": column_chunks(a["ffn2_w_in"]), "ffn2_out": column_chunks(a["ffn2_w_out"]),
        "w_mod": column_chunks(a["w_mod_2"][0]),
        "w_in2": column_chunks(w2[:, perm]),
        "w_uq": np.ascontiguousarray(a["mla_w_uq_2"][0].reshape(2, P, MLA_HEADS * QK).transpose(1, 0, 2)).reshape(P, -1),
        "w_ukv": np.ascontiguousarray(a["mla_w_ukv_2"][0]),
        "w_out2": column_chunks(a["w_out_2"][0]),
        "moe_gate": column_chunks(a["moe_w_gate_2"][0])[:, 0],
        "moe_up": column_chunks(a["moe_w_up_2"][0])[:, 0],
        "moe_down": np.ascontiguousarray(a["moe_w_down_2"][0].reshape(EXPERTS, 2, P, D).transpose(0, 2, 1, 3))
        .reshape(EXPERTS, P, 2 * D),
    }


def kernel(**inputs):
    import concourse.bacc as bacc
    from concourse.bass_utils import run_bass_kernel_spmd

    nc = bacc.Bacc("TRN2", target_bir_lowering=False, num_devices=1)
    arrays = pack(inputs)
    io = {k: nc.dram_tensor(k, v.shape, mybir.dt.from_np(v.dtype), kind="ExternalInput").ap() for k, v in arrays.items()}
    io["outT"] = nc.dram_tensor("outT", (D, T), F32, kind="ExternalOutput").ap()
    build(nc, io)
    r = run_bass_kernel_spmd(nc, [arrays], core_ids=[0])
    return np.ascontiguousarray(np.asarray(r.results[0]["outT"]).T)[None]
```

```python
from contextlib import ExitStack

import concourse.bass as bass
import numpy as np
from concourse import mybir

F32 = mybir.dt.float32
U32 = mybir.dt.uint32
ACT = mybir.ActivationFunctionType
ALU = mybir.AluOpType
AXX = mybir.AxisListType.X

P = 128
T = 512
D = 1024
KD = D // P
NT = T // P
DEPTH = 2
FF = 2816
KF = FF // P
CW = 256
SLOT = KD * CW
NSLOT = 5
HEAD = 64
CHUNK = 64
SB_HEADS = 8
RET_HEADS = 4
CONV_TAPS = 31
PAD = CONV_TAPS - 1
MLA_HEADS = 8
NOPE, ROPE = 64, 32
QK = NOPE + ROPE
GDN_HEADS = 4
GDN_TAPS = 4
POOL_WINDOWS = (2, 4, 8, 16)
EXPERTS = 32
NBLOCK = EXPERTS + (2 * T - EXPERTS) // P
GROUPS = 4
PER_GROUP = EXPERTS // GROUPS
ALPHA = 2 ** 0.25
RMS_EPS, LN_EPS = 1e-6, 1e-5
BIG = 1e30


def constant_tables():
    i = np.arange(P)
    row, col = i[:, None], i[None, :]
    same64 = (row // 64) == (col // 64)
    t = {}
    t["ident"] = np.eye(P)
    t["ones"] = np.ones((P, P))
    t["sum64"] = same64 * 1.0
    t["mean64"] = same64 / 64.0
    t["centre64"] = np.eye(P) - same64 / 64.0
    t["neg_suffix"] = -1.0 * (row >= col)
    t["neg_ones"] = -np.ones((P, P))
    t["swap64"] = np.where(same64, np.where(row == col + 32, -1.0 * (col % 64 < 32), 0.0)
                           + np.where(row == col - 32, 1.0 * (col % 64 >= 32), 0.0), 0.0)
    r, c = row - NOPE, col - NOPE
    inside = (r >= 0) & (r < ROPE) & (c >= 0) & (c < ROPE)
    t["swap32"] = np.where(inside, np.where(r == c + 16, -1.0 * (c < 16), 0.0)
                           + np.where(r == c - 16, 1.0 * (c >= 16), 0.0), 0.0)
    t["incl"] = same64 * (row <= col) * 1.0
    t["strict"] = same64 * (row < col) * 1.0
    t["later"] = same64 * (row > col) * 1.0
    for lv in range(6):
        s = 2 ** lv
        t[f"level{lv}"] = 1.0 * (((col // s) % 2 == 1) & (row // s == col // s - 1))
    pos = np.arange(T, dtype=np.float32)
    inv = (1.0 / (np.float32(10000.0) ** (np.arange(32, dtype=np.float32) / np.float32(32)))).astype(np.float32)
    ang = (pos[None, :] * inv[i % 32][:, None]).astype(np.float32)
    t["cos64"], t["sin64"] = np.cos(ang.astype(np.float64)), np.sin(ang.astype(np.float64))
    inv = (np.float32(10000.0) ** (-np.arange(0, 32, 2, dtype=np.float32) / np.float32(32))).astype(np.float32)
    ang = (pos[None, :] * inv[i % 16][:, None]).astype(np.float32)
    t["cos32"], t["sin32"] = np.cos(ang.astype(np.float64)), np.sin(ang.astype(np.float64))
    tt = np.arange(T)[None, :]
    for h in range(RET_HEADS):
        gamma = 1.0 - 2.0 ** (-5.0 - h)
        t[f"decay{h}"] = np.where(tt // CHUNK >= row // CHUNK, gamma ** np.abs(tt - row), 0.0) * HEAD ** -0.5
    for g in range(2):
        win = np.array([POOL_WINDOWS[2 * g + (p >= 64)] for p in range(P)])[:, None]
        t[f"inv_count{g}"] = 1.0 / np.minimum(tt + 1, win)
    t["rms_eps"] = np.full((P, 1), RMS_EPS)
    t["ln_eps"] = np.full((P, 1), LN_EPS)
    t["one"] = np.ones((P, 1))
    t["expert_id"] = np.tile(np.arange(EXPERTS)[None, :], (P, 1))
    t["before"] = 1.0 * (row < col)
    t["token_id"] = i[:, None] + P * np.arange(NT)[None, :]
    t["pad"] = np.full((P, 4), -BIG)
    return {k: np.asarray(v, np.float32) for k, v in t.items()}


def offsets(widths):
    at, out = 0, {}
    for name, w in widths:
        out[name] = (at, at + w)
        at += w
    return out, at


CONSTS = constant_tables()
CONST_AT, CONST_W = offsets([(k, v.shape[1]) for k, v in CONSTS.items()])
PARAM_AT, PARAM_W = offsets([
    ("ffn1_norm", DEPTH * KD), ("mix_norm", DEPTH * KD), ("ffn2_norm", DEPTH * KD), ("final_norm", KD),
    ("conv_w", DEPTH * 2 * CONV_TAPS), ("conv_b", DEPTH * 2), ("conv_ln_g", DEPTH * 2),
    ("conv_ln_b", DEPTH * 2), ("ret_norm_g", DEPTH * 2),
    ("c", KD), ("b_mod", 6 * KD), ("q_norm", 2), ("kv_norm", 1), ("gdn_conv", 6 * GDN_TAPS),
    ("gdn_g", 1), ("pool_scale", 2), ("pool_w", 128), ("router_w", KD * (GROUPS + EXPERTS)),
    ("ln1_g", KD), ("ln1_b", KD), ("ln2_g", KD), ("ln2_b", KD)])
ROW_AT, ROW_W = offsets([("dt_bias", GDN_HEADS), ("a_log", GDN_HEADS), ("router_b", GROUPS + EXPERTS)])


SCRATCH = {"h_rows": (T, D), "slot_token": (NBLOCK * P, 1), "block_rows": (NBLOCK * P, D)}


class Queue:

    def __init__(self, sem):
        self.sem, self.count, self.steps, self.reached = sem, 0, [], {}

    def wait(self, *marks):
        for sem, value in marks:
            if value > self.reached.get(id(sem), 0):
                self.reached[id(sem)] = value
                self.steps.append(lambda e, s=sem, v=value: e.wait_ge(s, v))

    def do(self, op, *marks):
        self.wait(*marks)
        self.count += 1
        self.steps.append(lambda e: op(e).then_inc(self.sem, 1))
        return self.sem, self.count

    def quiet(self, op, *marks):
        self.wait(*marks)
        self.steps.append(op)

    @property
    def last(self):
        return (self.sem, self.count)


class Buffer:
    def __init__(self, ap):
        self.ap, self.free = ap, ()

    def release(self, *marks):
        self.free = marks


class Rotation:

    def __init__(self, aps):
        self.buffers, self.n = [Buffer(a) for a in aps], 0

    def take(self):
        b = self.buffers[self.n % len(self.buffers)]
        self.n += 1
        assert b.free is not None, "taken before its readers are queued"
        out = Buffer(b.ap)
        out.free, b.free = b.free, None
        out.release = lambda *marks, b=b: setattr_free(b, marks)
        return out


def setattr_free(b, marks):
    b.free = marks


def build(nc, io, stages=None):
    with ExitStack() as ctx:
        def sbuf(name, shape, dt=F32):
            return ctx.enter_context(nc.sbuf_tensor(name, shape, dt))

        def sem(name):
            return ctx.enter_context(nc.semaphore(name))

        x = sbuf("x", [P, KD, T])
        h = sbuf("h", [P, KD, T])
        ring = sbuf("ring", [P, NSLOT, SLOT])
        arena = sbuf("arena", [P, 48 * T])
        const = sbuf("const", [P, CONST_W])
        param = sbuf("param", [P, PARAM_W])
        rowp = sbuf("rowp", [1, ROW_W])
        small = sbuf("small", [P, 512])
        psum = ctx.enter_context(nc.psum_tensor("psum", [P, 8, T], F32))

        V, A, PE, G = (Queue(sem(f"{n}_done")) for n in ("vector", "scalar", "tensor", "gpsimd"))
        S = Queue(sem("sync_unused"))
        slot_full = [sem(f"slot{i}_full") for i in range(NSLOT)]
        s_const, s_x, s_out = sem("const_loaded"), sem("x_loaded"), sem("out_stored")

        def tile(i, n=1):
            return arena[:, i * T:(i + n) * T]

        def K(name, a=0, b=None):
            lo, hi = CONST_AT[name]
            return const[:, lo + a:(hi if b is None else lo + b)]

        def W(name, a=0, b=None):
            lo, hi = PARAM_AT[name]
            return param[:, lo + a:(hi if b is None else lo + b)]

        banks = Rotation([psum[:, i, :] for i in range(8)])

        def mm(out, lhsT, rhs, start, stop, *marks, last=False, loose=False):
            def op(e):
                return e.matmul(out, lhsT, rhs, start=start, stop=stop, skip_group_check=loose)
            return PE.do(op, *marks) if last else PE.quiet(op, *marks)

        def act(out, in_, func, *marks, scale=1.0, bias=0.0, accum=None):
            if accum is not None:
                return A.do(lambda e: e.activation(out, in_, func, bias=bias, scale=scale, accum_out=accum), *marks)
            return A.do(lambda e: e.activation(out, in_, func, bias=bias, scale=scale), *marks)

        def tt(out, a, b, op, *marks, q=V):
            return q.do(lambda e: e.tensor_tensor(out, a, b, op), *marks)

        def ts(out, a, s1, s2, op0, op1, *marks, q=V):
            if op1 is None:
                return q.do(lambda e: e.tensor_scalar(out, a, s1, None, op0), *marks)
            return q.do(lambda e: e.tensor_scalar(out, a, s1, s2, op0, op1), *marks)

        def stt(out, a, s, b, op0, op1, *marks):
            return V.do(lambda e: e.scalar_tensor_tensor(out=out, in0=a, scalar=s, in1=b, op0=op0, op1=op1), *marks)

        def copy(out, a, *marks, q=V):
            if q is A:
                return act(out, a, ACT.Copy, *marks)
            return q.do(lambda e: e.tensor_copy(out, a), *marks)

        def fence():
            marks = [q.last for q in (V, A, PE, G) if q.count]
            for q in (V, A, PE, G):
                q.wait(*[m for m in marks])

        loads = [0]
        slot_free = [()] * NSLOT

        def load(src, width=SLOT):
            i = loads[0] % NSLOT
            use = loads[0] // NSLOT + 1
            loads[0] += 1
            assert slot_free[i] is not None, "slot filled before its readers are queued"
            S.wait(*slot_free[i])
            slot_free[i] = None
            S.steps.append(lambda e: e.dma_start(ring[:, i, 0:width], src).then_inc(slot_full[i], 16))
            return i, (slot_full[i], 16 * use)

        def done_with(i, *marks):
            slot_free[i] = marks

        def inv_root(out, ss, n, eps, *marks):
            m = act(out, ss, ACT.Ln, *marks, scale=1.0 / n, bias=K(eps)[0:out.shape[0]])
            return act(out, out, ACT.Exp, m, scale=-0.5)

        def sigmoid_of(buf, src, *marks):
            return act(buf, src, ACT.Sigmoid, *marks)

        def silu_of(buf, src, *marks):
            return act(buf, src, ACT.Silu, *marks)

        S.steps.append(lambda e: e.dma_start(const[:, :], io["consts"]).then_inc(s_const, 16))
        S.steps.append(lambda e: e.dma_start(param[:, :], io["params"]).then_inc(s_const, 16))
        S.steps.append(lambda e: e.dma_start(rowp[:, :], io["rows"]).then_inc(s_const, 16))
        S.steps.append(lambda e: e.dma_start(x[:, :, :], io["xT"].rearrange("(t p) n -> p t n", p=P)).then_inc(s_x, 16))
        for q in (V, A, PE, G):
            q.wait((s_const, 48), (s_x, 16))

        temps = Rotation([tile(i) for i in range(40, 48)])
        sums = Rotation([sbuf(f"square_sum{i}", [P, T])[:, :] for i in range(2)])

        class SquareSum:

            def __init__(self, n, stat="ones"):
                self.n, self.k, self.stat = n, 0, stat
                self.acc = temps.take() if n == 1 else sums.take()

            def add(self, src, *marks):
                self.k += 1
                if self.k == 1:
                    self.mark = act(self.acc.ap, src, ACT.Square, *marks, *self.acc.free)
                    return
                buf = temps.take()
                m = act(buf.ap, src, ACT.Square, *marks, *buf.free)
                self.mark = tt(self.acc.ap, self.acc.ap, buf.ap, ALU.add, m, self.mark, q=G)
                buf.release(self.mark)

            def flush(self):
                assert self.k == self.n
                self.bank = banks.take()
                self.mark = mm(self.bank.ap, K(self.stat), self.acc.ap, True, True, self.mark, *self.bank.free, last=True)
                self.acc.release(self.mark)

        def rms_to_h(stats, gain, at):
            stats.flush()
            r = temps.take()
            m = inv_root(r.ap, stats.bank.ap, D, "rms_eps", stats.mark, *r.free)
            stats.bank.release(m)
            marks = [stt(h[:, k, :], x[:, k, :], W(gain, at + k, at + k + 1), r.ap, ALU.mult, ALU.mult,
                         m, PE.last) for k in range(KD)]
            r.release(marks[-1])
            return marks

        def project(out, kt_n, lhs, rhs, *marks, rhs_marks=None):
            for kt in range(kt_n):
                extra = (rhs_marks[kt],) if rhs_marks else ()
                m = mm(out, lhs(kt), rhs(kt), kt == 0, kt == kt_n - 1, *(marks if kt == 0 else ()), *extra,
                       last=kt == kt_n - 1)
            return m

        mod = small[:, 0:6 * KD]
        c_act = small[:, 48:56]
        mod_acc = Rotation([arena[:, 22 * T + i * CW:22 * T + (i + 1) * CW] for i in range(8)])
        mod_waiting = []

        def mod_start():
            m = act(c_act, W("c"), ACT.Exp, scale=-1.0)
            m = ts(c_act, c_act, 1.0, None, ALU.add, None, m)
            m = V.do(lambda e: e.reciprocal(c_act, c_act), m)
            return tt(c_act, c_act, W("c"), ALU.mult, m)

        def mod_step(j, ready):
            i, full = load(io["w_mod"][j])
            acc = mod_acc.take()
            m = ts(acc.ap, ring[:, i, 0:CW], c_act[:, 0:1], None, ALU.mult, None, full, ready, *acc.free)
            for k in range(1, KD):
                m = stt(acc.ap, ring[:, i, k * CW:(k + 1) * CW], c_act[:, k:k + 1], acc.ap, ALU.mult, ALU.add, m)
            done_with(i, m)
            mod_waiting.append((j, acc, m))

        def mod_columns():
            if not mod_waiting:
                return
            b = banks.take()
            for at, (j, acc, m) in enumerate(mod_waiting):
                for n in range(2):
                    mark = mm(b.ap[:, 2 * at + n:2 * at + n + 1], acc.ap[:, n * P:(n + 1) * P], K("one"), True, True, m,
                              *b.free, last=True)
                acc.release(mark)
            j0, n = mod_waiting[0][0], len(mod_waiting)
            m = tt(mod[:, 2 * j0:2 * (j0 + n)], b.ap[:, 0:2 * n], W("b_mod", 2 * j0, 2 * (j0 + n)), ALU.add, mark)
            b.release(m)
            mod_waiting.clear()
            mod_marks.append(m)

        def ffn(h_ready, w_in, w_out, stats, aside=None):
            hid_ready = []
            for j in range(FF // CW):
                ig, full_g = load(w_in[j])
                iu, full_u = load(w_in[FF // CW + j])
                for n in range(2):
                    f = 2 * j + n
                    bg, bu = banks.take(), banks.take()
                    cols = slice(n * P, (n + 1) * P)
                    mg = project(bg.ap, KD, lambda k: ring[:, ig, k * CW + n * P:k * CW + n * P + P],
                                 lambda k: h[:, k, :], full_g, *bg.free, rhs_marks=h_ready)
                    mu = project(bu.ap, KD, lambda k: ring[:, iu, k * CW + n * P:k * CW + n * P + P],
                                 lambda k: h[:, k, :], full_u, *bu.free)
                    s = temps.take()
                    m = silu_of(s.ap, bg.ap, mg, *s.free)
                    bg.release(m)
                    m = tt(tile(f), bu.ap, s.ap, ALU.mult, m, mu)
                    bu.release(m)
                    s.release(m)
                    hid_ready.append(m)
                done_with(ig, mg)
                done_with(iu, mu)
                if aside:
                    aside(j)
            for j in range(D // CW):
                bb = [banks.take(), banks.take()]
                for k0 in range(0, KF, KD):
                    kn = min(KD, KF - k0)
                    i, full = load(w_out[j, :, k0 * CW:(k0 + kn) * CW], kn * CW)
                    for n in range(2):
                        for k in range(kn):
                            kt = k0 + k
                            m = mm(bb[n].ap, ring[:, i, k * CW + n * P:k * CW + n * P + P], tile(kt), kt == 0,
                                   kt == KF - 1, full, hid_ready[kt], *(bb[n].free if kt == 0 else ()),
                                   last=k == kn - 1)
                        if kt == KF - 1:
                            d = 2 * j + n
                            mx = stt(x[:, d, :], bb[n].ap, 0.5, x[:, d, :], ALU.mult, ALU.add, m)
                            bb[n].release(mx)
                            if stats:
                                stats.add(x[:, d, :], mx)
                    done_with(i, m)

        def mixer1(layer, h_ready, stats):
            w_in, w_out = io["mix_w_in"][layer], io["mix_w_out"][layer]
            gate_b, q_sb, k_sb, v_sb, q_r, k_r, v_r, g_r, acc = 20, 0, 4, 8, 12, 14, 16, 18, 20
            vpad = arena[:, 22 * T:22 * T + 2 * (PAD + T)].rearrange("p (t n) -> p t n", t=2)
            soft = [arena[:, 25 * T + 1280 * i:25 * T + 1280 * (i + 1)] for i in range(6)]
            m_pad = V.do(lambda e: e.memset(vpad[:, :, 0:PAD], 0.0))

            def proj_T(j, take):
                i, full = load(w_in[j])
                for n in range(2):
                    b = banks.take()
                    m = project(b.ap, KD, lambda k: ring[:, i, k * CW + n * P:k * CW + n * P + P],
                                lambda k: h[:, k, :], full, *b.free, rhs_marks=h_ready)
                    take(n, b, m)
                done_with(i, m)

            def proj_N(j, take):
                i, full = load(w_in[j])
                for t in range(NT):
                    b = banks.take()
                    m = project(b.ap[:, 0:CW], KD, lambda k: h[:, k, t * P:(t + 1) * P],
                                lambda k: ring[:, i, k * CW:(k + 1) * CW], full, *b.free)
                    take(t, b, m)
                done_with(i, m)

            def keep(dst, q=A, scale=1.0):
                def take(n, b, m):
                    if scale == 1.0:
                        mk = copy(tile(dst + n), b.ap, m, q=q)
                    else:
                        mk = act(tile(dst + n), b.ap, ACT.Copy, m, scale=scale)
                    b.release(mk)
                    ready[dst + n] = mk
                return take

            ready = {}
            a_banks = []
            proj_T(0, lambda n, b, m: a_banks.append((b, m)))

            def conv_gate(n, b, m):
                s = temps.take()
                ms = sigmoid_of(s.ap, b.ap, m, *s.free)
                b.release(ms)
                ab, ma = a_banks[n]
                mv = tt(vpad[:, n, PAD:PAD + T], ab.ap, s.ap, ALU.mult, ma, ms)
                ab.release(mv)
                s.release(mv)
                ready["v", n] = mv
            proj_T(1, conv_gate)
            for j in range(2):
                proj_T(2 + j, keep(q_sb + 2 * j, scale=HEAD ** -0.5))
            for j in range(2):
                proj_T(4 + j, keep(k_sb + 2 * j, q=V))
            for j in range(2):
                def keep_v(t, b, m, j=j):
                    mk = copy(tile(v_sb + t)[:, j * CW:(j + 1) * CW], b.ap[:, 0:CW], m, q=A)
                    b.release(mk)
                    ready["v_sb", t, j] = mk
                proj_N(6 + j, keep_v)

            def rotate(dst):
                def take(n, b, m):
                    plain = temps.take()
                    mp = copy(plain.ap, b.ap, m, *plain.free, q=A)
                    b.release(mp)
                    sw = banks.take()
                    ms = mm(sw.ap, K("swap64"), plain.ap, True, True, mp, *sw.free, last=True)
                    m1 = tt(tile(dst + n), plain.ap, K("cos64"), ALU.mult, mp)
                    turned = temps.take()
                    m2 = tt(turned.ap, sw.ap, K("sin64"), ALU.mult, ms, *turned.free)
                    sw.release(m2)
                    plain.release(m1, ms)
                    m3 = tt(tile(dst + n), tile(dst + n), turned.ap, ALU.add, m1, m2)
                    turned.release(m3)
                    ready[dst + n] = m3
                return take
            proj_T(8, rotate(q_r))
            proj_T(9, rotate(k_r))

            def keep_vr(t, b, m):
                mk = copy(arena[:, v_r * T + t * CW:v_r * T + (t + 1) * CW], b.ap[:, 0:CW], m, q=A)
                b.release(mk)
                ready["v_r", t] = mk
            proj_N(10, keep_vr)
            proj_T(11, keep(g_r, q=V))
            projected = PE.last

            def conv_taps():
                for tap in range(CONV_TAPS):
                    for n in range(2):
                        at = (layer * 2 + n) * CONV_TAPS + tap
                        w = W("conv_w", at, at + 1)
                        src = vpad[:, n, tap:tap + T]
                        if tap == 0:
                            b0 = W("conv_b", layer * 2 + n, layer * 2 + n + 1)
                            ready["conv", n] = ts(tile(acc + n), src, w, b0, ALU.mult, ALU.add, m_pad, ready["v", n])
                        else:
                            ready["conv", n] = stt(tile(acc + n), src, w, tile(acc + n), ALU.mult, ALU.add,
                                                   ready["conv", n])
                        yield
            conv = conv_taps()

            def conv_some(n):
                for _ in range(n):
                    next(conv, None)

            part = {0: (0, 0, 0), 1: (512, 1, 0), 3: (896, 1, 384), 2: (1024, 2, 0)}
            order = (0, 1, 3, 2)
            spans = ((0, 512), (512, 1024), (1024, 1280))
            turns = [Rotation(soft[2 * i:2 * i + 2]) for i in range(3)]

            def head_rows(i):
                return slice(HEAD * (i % 2), HEAD * (i % 2) + HEAD)

            def before_only(buf, queue_after):
                marks = []
                for kt in order:
                    blk = buf[:, part[kt][0]:part[kt][0] + P]
                    marks.append(G.do(lambda e, blk=blk: e.affine_select(
                        out=blk, in_=blk, compare_op=ALU.is_gt, fill=0.0, base=0, pattern=[[1, P]],
                        channel_multiplier=-1), queue_after))
                return marks[-1]

            def sb_scores(i):
                rows = head_rows(i)
                q, k = tile(q_sb + i // 2), tile(k_sb + i // 2)
                bb = [banks.take() for _ in range(3)]
                for kt in order:
                    _, bi, c = part[kt]
                    n = T - kt * P
                    m = mm(bb[bi].ap[:, c:c + n], k[rows, kt * P:(kt + 1) * P], q[rows, kt * P:T],
                           c == 0, True, *bb[bi].free, ready[q_sb + i // 2], ready[k_sb + i // 2],
                           last=True, loose=True)
                e, sp = turns[0].take(), turns[1].take()
                for bi, (a, b) in enumerate(spans):
                    me = act(e.ap[:, a:b], bb[bi].ap[:, 0:b - a], ACT.Abs, m, *e.free)
                me = act(e.ap, e.ap, ACT.Exp, me, scale=-1.0)
                me = act(e.ap, e.ap, ACT.Ln, me, bias=K("one"))
                for bi, (a, b) in enumerate(spans):
                    ms = stt(sp.ap[:, a:b], bb[bi].ap[:, 0:b - a], 0.0, e.ap[:, a:b], ALU.max, ALU.add, me, *sp.free)
                e.release(ms)
                return bb, sp, before_only(sp.ap, ms), ms

            def sb_mix(i, bb, sp, sp_ready, z_read):
                rows = head_rows(i)
                w = turns[2].take()
                for kt in order:
                    _, bi, c = part[kt]
                    for kj in range(kt, NT):
                        off, n = part[kj][0], T - kj * P
                        dst = c + (kj - kt) * P
                        m = mm(bb[bi].ap[:, dst:dst + n], K("neg_suffix" if kj == kt else "neg_ones"),
                               sp.ap[:, off:off + n], False, True, sp_ready, z_read, last=kj == NT - 1, loose=True)
                    if kt == 0:
                        m_first = m
                sp.release(m)
                for bi, (a, b) in enumerate(spans):
                    mw = act(w.ap[:, a:b], bb[bi].ap[:, 0:b - a], ACT.Exp, m_first if bi == 0 else m, *w.free)
                    bb[bi].release(mw)
                return w, before_only(w.ap, mw)

            def sb_out(i, w, mw):
                rows = head_rows(i)
                o = banks.take()
                for kt in range(NT):
                    off, n = part[kt][0], T - kt * P
                    m = mm(o.ap[rows, kt * P:T], tile(v_sb + kt)[:, i * HEAD:(i + 1) * HEAD], w.ap[:, off:off + n],
                           kt == 0, kt == NT - 1, mw, ready["v_sb", kt, i * HEAD // CW], *o.free, last=True)
                w.release(m)
                mo = copy(h[rows, 2 + i // 2, :], o.ap[rows, :], m, projected)
                o.release(mo)
                ready["y", 2 + i // 2, i % 2] = mo

            nxt, mixed = sb_scores(0), None
            for i in range(SB_HEADS):
                cur = nxt
                if i + 1 < SB_HEADS:
                    nxt = sb_scores(i + 1)
                conv_some(8)
                w = sb_mix(i, *cur)
                if mixed:
                    sb_out(*mixed)
                mixed = (i, *w)

            def ret_scores(i):
                rows = head_rows(i)
                out, s = [], turns[0].take()
                for kt in range(NT):
                    n = T - kt * P
                    b, c = banks.take(), part[kt][0]
                    m = mm(b.ap[:, 0:n], tile(k_r + i // 2)[rows, kt * P:(kt + 1) * P],
                           tile(q_r + i // 2)[rows, kt * P:T], True, True, *b.free, ready[q_r + i // 2],
                           ready[k_r + i // 2], last=True)
                    ms = tt(s.ap[:, c:c + n], b.ap[:, 0:n], K(f"decay{i}", 0, n), ALU.mult, m, *s.free)
                    b.release(ms)
                    out.append(ms)
                return s, out

            def ret_mix(i, s, scored):
                rows = head_rows(i)
                o = banks.take()
                for kt, ms in enumerate(scored):
                    n, c = T - kt * P, part[kt][0]
                    m = mm(o.ap[rows, kt * P:T], arena[:, v_r * T + kt * CW + i * HEAD:v_r * T + kt * CW + (i + 1) * HEAD],
                           s.ap[:, c:c + n], kt == 0, kt == NT - 1, ms, ready["v_r", kt], *o.free, last=True)
                s.release(m)
                y = tile(q_sb + i // 2)
                mo = copy(y[rows, :], o.ap[rows, :], m, PE.last, q=A)
                o.release(mo)
                ready["ret", i] = mo

            def conv_centre():
                mean = banks.take()
                for n in range(2):
                    m = mm(mean.ap, K("ones"), tile(acc + n), n == 0, n == 1, ready["conv", n], *mean.free, last=True)
                for n in range(2):
                    m1 = act(tile(k_sb + n), mean.ap, ACT.Copy, m, scale=-1.0 / 256)
                    m2 = tt(tile(acc + n), tile(acc + n), tile(k_sb + n), ALU.add, m1)
                    ready["conv", n] = m2
                    var.add(tile(acc + n), m2)
                mean.release(m1)

            def conv_finish():
                var.flush()
                r = temps.take()
                mr = inv_root(r.ap, var.bank.ap, 256, "rms_eps", var.mark, *r.free)
                var.bank.release(mr)
                for n in range(2):
                    at = layer * 2 + n
                    m = stt(tile(acc + n), tile(acc + n), W("conv_ln_g", at, at + 1), r.ap, ALU.mult, ALU.mult, mr,
                            ready["conv", n])
                    m = ts(tile(acc + n), tile(acc + n), W("conv_ln_b", at, at + 1), None, ALU.add, None, m)
                    m = silu_of(h[:, n, :], tile(acc + n), m, projected)
                    ready["y", n, 0] = ready["y", n, 1] = m
                r.release(m)

            def ret_centre(n):
                b = banks.take()
                m = mm(b.ap, K("centre64"), tile(q_sb + n), True, True, ready["ret", 2 * n], ready["ret", 2 * n + 1],
                       *b.free, last=True)
                sv = SquareSum(1, "sum64")
                sv.add(b.ap, m)
                return b, sv

            var = SquareSum(2)
            nxt = ret_scores(0)
            sb_out(*mixed)
            conv_some(2 * CONV_TAPS)
            for i in range(RET_HEADS):
                cur = nxt
                if i + 1 < RET_HEADS:
                    nxt = ret_scores(i + 1)
                if i == 0:
                    conv_centre()
                ret_mix(i, *cur)
                if i == 2:
                    first_pair = ret_centre(0)
                    conv_finish()
            pairs = [first_pair, ret_centre(1)]
            for n, (b, sv) in enumerate(pairs):
                sv.flush()
                r = temps.take()
                mr = inv_root(r.ap, sv.bank.ap, HEAD, "rms_eps", sv.mark, *r.free)
                sv.bank.release(mr)
                s = temps.take()
                ms = silu_of(s.ap, tile(g_r + n), ready[g_r + n], *s.free)
                m = tt(r.ap, b.ap, r.ap, ALU.mult, mr)
                b.release(m)
                at = layer * 2 + n
                m = stt(h[:, 6 + n, :], r.ap, W("ret_norm_g", at, at + 1), s.ap, ALU.mult, ALU.mult, m, ms, projected)
                r.release(m)
                s.release(m)
                ready["y", 6 + n, 0] = ready["y", 6 + n, 1] = m
            y_ready = [mk for n in range(KD) for mk in (ready["y", n, 0], ready["y", n, 1])]
            out_project(w_out, y_ready, lambda d, b, m: residual(d, b, m, stats), stats)

        def residual(d, b, m, stats):
            mx = tt(x[:, d, :], b.ap, x[:, d, :], ALU.add, m)
            b.release(mx)
            stats.add(x[:, d, :], mx)

        def out_project(w_out, y_ready, take, stats):
            for j in range(D // CW):
                i, full = load(w_out[j])
                for n in range(2):
                    b = banks.take()
                    m = project(b.ap, KD, lambda k: ring[:, i, k * CW + n * P:k * CW + n * P + P],
                                lambda k: h[:, k, :], full, *b.free, *(y_ready if j == 0 and n == 0 else ()))
                    take(2 * j + n, b, m)
                done_with(i, m)

        def mixer2(h_ready):
            qf, kf, v_nat = 0, 8, 16
            gpad = arena[:, 20 * T:20 * T + 6 * (GDN_TAPS - 1 + T)].rearrange("p (t n) -> p t n", t=6)
            z_t = 27
            PP = 16
            ppad = arena[:, 29 * T:29 * T + 2 * (PP + T)].rearrange("p (t n) -> p t n", t=2)
            cq, ckv = 32, 34
            prob = Rotation([tile(i) for i in (35, 36, 37, 38, 32, 33, 34, 44)])
            flip = Rotation([arena[:, 39 * T + 1280 * i:39 * T + 1280 * (i + 1)] for i in range(2)])
            ab = small[:, 64:96].rearrange("p (t n) -> p t n", t=NT)
            w_in = io["w_in2"]
            ready = {}
            m_pads = (V.do(lambda e: e.memset(gpad[:, :, 0:GDN_TAPS - 1], 0.0)),
                      V.do(lambda e: e.memset(ppad[:, :, 0:PP], 0.0)))

            def proj(i, full, n, m_rows, take, at=None, rows=None):
                b = banks.take()
                c0 = n * P if at is None else at
                out = b.ap[0:m_rows, :]
                m = project(out, KD, lambda k: ring[:, i, k * CW + c0:k * CW + c0 + m_rows],
                            lambda k: h[:, k, :], full, *b.free, rhs_marks=h_ready)
                take(n, b, m)
                return m

            def keep(dst, name, q=A):
                def take(n, b, m):
                    mk = copy(dst(n), b.ap, m, *m_pads, q=q)
                    b.release(mk)
                    ready[name, n] = mk
                return take

            i, full = load(w_in[0])
            for n in range(2):
                m = proj(i, full, n, P, keep(lambda n: tile(cq + n), "cq"))
            done_with(i, m)
            i, full = load(w_in[1])
            proj(i, full, 0, P, keep(lambda n: tile(ckv), "ckv"))
            kr = Buffer(tile(44))

            def keep_kr(n, b, m):
                mk = copy(kr.ap[NOPE:QK, :], b.ap[NOPE:QK, :], m, *kr.free, q=A)
                b.release(mk)
                ready["kr"] = mk
            proj(i, full, 1, QK, keep_kr, at=P)
            b = banks.take()
            for t in range(NT):
                m = project(b.ap[:, 8 * t:8 * t + 8], KD, lambda k: h[:, k, t * P:(t + 1) * P],
                            lambda k: ring[:, i, k * CW + P + QK:k * CW + P + QK + 8], full, *b.free)
            mk = copy(ab, b.ap[:, 0:32].rearrange("p (t n) -> p t n", t=NT), m)
            b.release(mk)
            ready["ab"] = mk
            done_with(i, m)
            for g in range(3):
                i, full = load(w_in[2 + g])
                for n in range(2):
                    m = proj(i, full, n, P, keep(lambda n, g=g: gpad[:, 2 * g + n, GDN_TAPS - 1:], ("g", g), q=(A, V)[g % 2]))
                done_with(i, m)
            i, full = load(w_in[5])
            for n in range(2):
                m = proj(i, full, n, P, keep(lambda n: tile(z_t + n), "z"))
            done_with(i, m)
            i, full = load(w_in[6])
            for n in range(2):
                m = proj(i, full, n, P, keep(lambda n: ppad[:, n, PP:], "p", q=V))
            done_with(i, m)
            projected = PE.last

            def latent_norm(tiles, names, gain):
                s = SquareSum(len(tiles))
                for t, nm in zip(tiles, names):
                    s.add(tile(t), ready[nm])
                s.flush()
                r = temps.take()
                m = inv_root(r.ap, s.bank.ap, P * len(tiles), "rms_eps", s.mark, *r.free)
                s.bank.release(m)
                for n, t in enumerate(tiles):
                    mk = stt(tile(t), tile(t), W(gain, n, n + 1), r.ap, ALU.mult, ALU.mult, m)
                r.release(mk)
                return mk
            ckv_ready = latent_norm([ckv], [("ckv", 0)], "kv_norm")
            cq_ready = latent_norm([cq, cq + 1], [("cq", 0), ("cq", 1)], "q_norm")

            def rotate(rows_ap, mp, *marks):
                sw = banks.take()
                r = slice(NOPE, QK)
                ms = mm(sw.ap[r, :], K("swap32")[r, NOPE:QK], rows_ap, True, True, mp, *sw.free, last=True)
                s = temps.take()
                m2 = tt(s.ap[r, :], sw.ap[r, :], K("sin32")[r, :], ALU.mult, ms, *s.free)
                sw.release(m2)
                m1 = tt(rows_ap, rows_ap, K("cos32")[r, :], ALU.mult, mp, ms)
                m3 = tt(rows_ap, rows_ap, s.ap[r, :], ALU.add, m1, m2)
                s.release(m3)
                return m3
            ready["kr"] = rotate(kr.ap[NOPE:QK, :], ready["kr"])

            i, full = load(io["w_ukv"], MLA_HEADS * P)
            for hd in range(MLA_HEADS):
                b = banks.take()
                m = mm(b.ap[0:NOPE, :], ring[:, i, hd * P:hd * P + NOPE], tile(ckv), True, True, full, ckv_ready,
                       *b.free, last=True)
                mk = copy(tile(kf + hd)[0:NOPE, :], b.ap[0:NOPE, :], m, q=A)
                b.release(mk)
                m2 = copy(tile(kf + hd)[NOPE:QK, :], kr.ap[NOPE:QK, :], ready["kr"], q=G)
                ready["k", hd] = (mk, m2)
            for t in range(NT):
                b = banks.take()
                vcols = ring[:, i, 0:MLA_HEADS * P].rearrange("p (h c) -> p h c", c=P)[:, :, NOPE:P]
                m = mm(b.ap, tile(ckv)[:, t * P:(t + 1) * P], vcols, True, True, *b.free, last=True)
                mk = copy(tile(v_nat + t), b.ap, m, q=V)
                b.release(mk)
                ready["v", t] = mk
            done_with(i, m)
            i, full = load(io["w_uq"], 2 * MLA_HEADS * QK)
            for hd in range(MLA_HEADS):
                b = banks.take()
                for k in range(2):
                    c0 = k * MLA_HEADS * QK + hd * QK
                    m = mm(b.ap[0:QK, :], ring[:, i, c0:c0 + QK], tile(cq + k), k == 0, k == 1, full, cq_ready,
                           *b.free, last=True)
                mk = copy(tile(qf + hd)[0:QK, :], b.ap[0:QK, :], m, q=A)
                b.release(mk)
                ready["q", hd] = rotate(tile(qf + hd)[NOPE:QK, :], mk)
            done_with(i, m)

            for b in prob.buffers[4:]:
                b.free = (PE.last, ready["k", MLA_HEADS - 1][1])

            scale = QK ** -0.5
            mx, neg, rs = small[:, 96:128], small[:, 128:160], small[:, 160:192]

            def mla_scores(hd):
                out = []
                for t in range(NT):
                    n = (t + 1) * P
                    c = hd * NT + t
                    b, p = banks.take(), prob.take()
                    m = mm(b.ap[:, 0:n], tile(qf + hd)[0:QK, t * P:n], tile(kf + hd)[0:QK, 0:n], True, True,
                           *b.free, ready["q", hd], *ready["k", hd], last=True)
                    m = V.do(lambda e, b=b, n=n: e.memset(b.ap[0:CHUNK, n - CHUNK:n], -BIG), m)
                    m = V.do(lambda e, b=b, n=n, c=c: e.tensor_reduce(mx[:, c:c + 1], b.ap[:, 0:n], AXX, ALU.max), m)
                    m = ts(neg[:, c:c + 1], mx[:, c:c + 1], -scale, None, ALU.mult, None, m)
                    m = act(p.ap[:, 0:n], b.ap[:, 0:n], ACT.Exp, m, *p.free, scale=scale, bias=neg[:, c:c + 1],
                            accum=rs[:, c:c + 1])
                    b.release(m)
                    m = V.do(lambda e, c=c: e.reciprocal(rs[:, c:c + 1], rs[:, c:c + 1]), m)
                    m = ts(p.ap[:, 0:n], p.ap[:, 0:n], rs[:, c:c + 1], None, ALU.mult, None, m)
                    out.append((p, m))
                return out

            part = {0: (0, 0, 0), 1: (512, 1, 0), 3: (896, 1, 384), 2: (1024, 2, 0)}
            spans = ((0, 512), (512, 1024), (1024, 1280))

            def mla_mix(hd, probs):
                rows = slice(HEAD * (hd % 2), HEAD * (hd % 2) + HEAD)
                bb, f = [banks.take() for _ in range(3)], flip.take()
                for t, (p, mp) in enumerate(probs):
                    for kt in range(t + 1):
                        _, bi, c = part[kt]
                        c += (t - kt) * P
                        m = PE.do(lambda e, o=bb[bi].ap[:, c:c + P], s=p.ap[:, kt * P:(kt + 1) * P]:
                                  e.transpose(o, s, K("ident")), mp, *bb[bi].free)
                    p.release(m)
                for bi, (a, b) in enumerate(spans):
                    mf = copy(f.ap[:, a:b], bb[bi].ap[:, 0:b - a], m, *f.free, q=V if bi == 0 else A)
                    bb[bi].release(mf)
                    if bi == 0:
                        mf0 = mf
                o = banks.take()
                for kt in range(NT):
                    off, n = part[kt][0], T - kt * P
                    m = mm(o.ap[rows, kt * P:T], tile(v_nat + kt)[:, hd * HEAD:(hd + 1) * HEAD], f.ap[:, off:off + n],
                           kt == 0, kt == NT - 1, mf0, mf, ready["v", kt], *o.free, last=True)
                f.release(m)
                mo = copy(h[rows, hd // 2, :], o.ap[rows, :], m, projected, q=A)
                o.release(mo)
                ready["y", hd // 2, hd % 2] = mo

            nxt = mla_scores(0)
            for hd in range(MLA_HEADS):
                cur = nxt
                if hd + 1 < MLA_HEADS:
                    nxt = mla_scores(hd + 1)
                mla_mix(hd, cur)

            s2, s4 = (arena[:, 35 * T + i * 2 * (PP + T):35 * T + (i + 1) * 2 * (PP + T)].rearrange(
                "p (t n) -> p t n", t=2) for i in range(2))
            fence()
            lo, hi = slice(0, 64), slice(64, 128)
            sums = {}
            src, mk = ppad, (ready["p", 0], ready["p", 1], *m_pads)
            W16 = PP + T
            sel = [tile(41), tile(42)]
            m = None
            cur, nxt_ = ppad, [s2, s4]
            for lvl, sh in enumerate((1, 2, 4, 8)):
                dst = nxt_[lvl % 2]
                ma = V.do(lambda e, d=dst, c=cur, sh=sh: e.tensor_copy(d[:, :, 0:sh], c[:, :, 0:sh]), *(mk if m is None else (m,)))
                mb = tt(dst[:, :, sh:W16], cur[:, :, sh:W16], cur[:, :, 0:W16 - sh], ALU.add, *(mk if m is None else (m,)))
                g, rows = lvl // 2, (lo, hi)[lvl % 2]
                mc = tt(sel[g][rows, :], dst[rows, g, PP:W16], K(f"inv_count{g}")[rows, :], ALU.mult, ma, mb)
                m = mc
                cur = dst
            scaled = []
            for g in range(2):
                m1 = tt(sel[g], sel[g], ppad[:, g, PP:W16], ALU.subtract, m)
                b, b2 = banks.take(), banks.take()
                mA = mm(b.ap[lo, :], W("pool_w", g * 64, g * 64 + 64)[lo, :], sel[g][lo, :], True, True, m1, *b.free, last=True)
                mB = mm(b2.ap[hi, :], W("pool_w", g * 64, g * 64 + 64)[hi, :], sel[g][hi, :], True, True, m1, *b2.free, last=True)
                for bb_, rows, mm_ in ((b, lo, mA), (b2, hi, mB)):
                    mk2 = ts(h[rows, 6 + g, :], bb_.ap[rows, :], W("pool_scale", g, g + 1)[rows, :], None, ALU.mult, None,
                             mm_, projected)
                    bb_.release(mk2)
                    ready["y", 6 + g, 0 if rows is lo else 1] = mk2

            fence()
            gtemps = Rotation([tile(15), tile(46), tile(47)])
            qkv = arena[:, 0:6 * T]
            mc = []
            for n in range(6):
                for tap in range(GDN_TAPS):
                    w = W("gdn_conv", n * GDN_TAPS + tap, n * GDN_TAPS + tap + 1)
                    src = gpad[:, n, tap:tap + T]
                    if tap == 0:
                        m = ts(tile(n), src, w, None, ALU.mult, None)
                    else:
                        m = stt(tile(n), src, w, tile(n), ALU.mult, ALU.add, m)
            conv_ready = silu_of(qkv, qkv, m)
            qT, kT, vT = (lambda f: tile(f)), (lambda f: tile(2 + f)), (lambda f: tile(4 + f))
            unit = []
            for n in range(4):
                s = gtemps.take()
                m = act(s.ap, tile(n), ACT.Square, conv_ready, *s.free)
                b = banks.take()
                m = mm(b.ap, K("sum64"), s.ap, True, True, m, *b.free, last=True)
                s.release(m)
                r = gtemps.take()
                m = inv_root(r.ap, b.ap, 1.0, "rms_eps", m, *r.free)
                b.release(m)
                m = stt(tile(n), tile(n), HEAD ** -0.5 if n < 2 else 1.0, r.ap, ALU.mult, ALU.mult, m)
                r.release(m)
                unit.append(m)

            def cols(a):
                return small[:, a:a + 16]
            g_c, beta_c, t_c, gc_c, be_c, kd_c, dt_c = (cols(a) for a in (192, 208, 224, 240, 256, 272, 288))
            bc = small[:, 304:312]
            b = banks.take()
            m = mm(b.ap[:, 0:8], K("ones")[0:1, :], rowp[0:1, 0:8], True, True, *b.free, last=True)
            m = copy(bc, b.ap[:, 0:8], m)
            b.release(m)
            m_exp = act(bc[:, 4:8], bc[:, 4:8], ACT.Exp, m)
            for t in range(NT):
                m = tt(dt_c[:, 4 * t:4 * t + 4], ab[:, t, 0:4], bc[:, 0:4], ALU.add, m)
            m1 = act(t_c, dt_c, ACT.Abs, m)
            m1 = act(t_c, t_c, ACT.Exp, m1, scale=-1.0)
            m1 = act(t_c, t_c, ACT.Ln, m1, bias=K("one"))
            m1 = stt(t_c, dt_c, 0.0, t_c, ALU.max, ALU.add, m1)
            for t in range(NT):
                m1 = stt(g_c[:, 4 * t:4 * t + 4], t_c[:, 4 * t:4 * t + 4], -1.0, bc[:, 4:8], ALU.mult, ALU.mult, m1, m_exp)
            m2 = act(beta_c.rearrange("p (t n) -> p t n", t=NT), ab[:, :, 4:8], ACT.Exp, ready["ab"], scale=-1.0)
            m2 = ts(beta_c, beta_c, 1.0, None, ALU.add, None, m2)
            m2 = V.do(lambda e: e.reciprocal(beta_c, beta_c), m2)
            b = banks.take()
            m = mm(b.ap[:, 0:16], K("incl"), g_c, True, True, m1, *b.free, last=True)
            mB = mm(b.ap[:, 16:32], K("later"), g_c, True, True, last=True)
            m = copy(gc_c, b.ap[:, 0:16], mB)
            me = act(be_c, b.ap[:, 0:16], ACT.Exp, mB, m)
            me2 = act(kd_c, b.ap[:, 16:32], ACT.Exp, mB, m)
            b.release(m, me2)
            gates = tt(be_c, be_c, beta_c, ALU.mult, me, m2)
            gates2 = (m, me2, gates)

            AT, QKT, TT, UU, XX = 38, 42, 6, 20, 10
            BT = (24, 25, 26, 14)
            eB, kb = (36, 37), (32, 33)
            for hd in range(GDN_HEADS):
                rows, f = slice(HEAD * (hd % 2), HEAD * (hd % 2) + HEAD), hd // 2
                gb, bbk = banks.take(), banks.take()
                for which, col, mat, bank in ((0, g_c, "incl", gb), (1, beta_c, "ident", bbk)):
                    s = gtemps.take()
                    for t in range(NT):
                        c = 4 * t + hd
                        m = ts(s.ap[:, t * P:(t + 1) * P], K("ones"), col[:, c:c + 1], None, ALU.mult, None,
                               *s.free, m1, m2, q=G)
                    for t in range(NT):
                        m = mm(bank.ap[:, t * P:(t + 1) * P], s.ap[:, t * P:(t + 1) * P], K(mat), True, True, m,
                               *bank.free, last=True)
                    s.release(m)
                    if which == 0:
                        m_gb = m
                    else:
                        m_bb = m
                me = act(tile(eB[f])[rows, :], gb.ap[rows, :], ACT.Exp, m_gb)
                ready["e", hd] = me
                dT = gtemps.take()
                for t in range(NT):
                    c = 4 * t + hd
                    m = ts(dT.ap[:, t * P:(t + 1) * P], gb.ap[:, t * P:(t + 1) * P], gc_c[:, c:c + 1], 0.0,
                           ALU.subtract, ALU.min, m_gb, me, *dT.free, *gates2)
                gb.release(m, me)
                m = act(dT.ap, dT.ap, ACT.Exp, m)
                m_kb = tt(tile(kb[f])[rows, :], kT(f)[rows, :], bbk.ap[rows, :], ALU.mult, m_bb, unit[2 + f])
                bbk.release(m_kb)
                ab_, qb_ = banks.take(), banks.take()
                for bank, rhs in ((ab_, tile(kb[f])), (qb_, qT(f))):
                    for t in range(NT):
                        sl = slice(t * P, (t + 1) * P)
                        mk = mm(bank.ap[:, sl], kT(f)[rows, sl], rhs[rows, sl], True, True, m_kb, unit[f], unit[2 + f],
                                *bank.free, last=True)
                for bank, dst, mask in ((ab_, AT + hd, "strict"), (qb_, QKT + hd, "incl")):
                    m3 = tt(tile(dst), bank.ap, dT.ap, ALU.mult, mk, m)
                    bank.release(m3)
                    for t in range(NT):
                        sl = slice(t * P, (t + 1) * P)
                        m4 = tt(tile(dst)[:, sl], tile(dst)[:, sl], K(mask), ALU.mult, m3, q=G)
                    ready[dst] = m4
                dT.release(m3)

            t_ready, u_ready = {}, {}
            for lv in range(6):
                for hd in range(GDN_HEADS):
                    B_, X_ = tile(BT[hd]), tile(XX + hd)
                    T_, U_ = tile(TT + hd), tile(UU + hd)
                    for t in range(NT):
                        sl = slice(t * P, (t + 1) * P)
                        mb = tt(B_[:, sl], tile(AT + hd)[:, sl], K(f"level{lv}"), ALU.mult, ready[AT + hd],
                                *((u_ready[hd], t_ready[hd]) if lv else ()), q=G)
                    b = banks.take()
                    for t in range(NT):
                        sl = slice(t * P, (t + 1) * P)
                        m = mm(b.ap[:, sl], B_[:, sl], K("ident") if lv == 0 else T_[:, sl], True, True, mb, *b.free,
                               *((t_ready[hd],) if lv else ()), last=True)
                    if lv == 0:
                        for t in range(NT):
                            sl = slice(t * P, (t + 1) * P)
                            t_ready[hd] = tt(T_[:, sl], K("ident"), b.ap[:, sl], ALU.subtract, m)
                            u_ready[hd] = tt(U_[:, sl], K("ident"), B_[:, sl], ALU.subtract, mb)
                        b.release(t_ready[hd])
                        continue
                    mx_ = copy(X_, b.ap, m, q=A)
                    b.release(mx_)
                    b1, b2 = banks.take(), banks.take()
                    for t in range(NT):
                        sl = slice(t * P, (t + 1) * P)
                        if lv < 5:
                            ma_ = mm(b1.ap[:, sl], U_[:, sl], X_[:, sl], True, True, mx_, u_ready[hd], *b1.free, last=True)
                        mb_ = mm(b2.ap[:, sl], X_[:, sl], U_[:, sl], True, True, mx_, u_ready[hd], *b2.free, last=True)
                    if lv < 5:
                        t_ready[hd] = tt(T_, T_, b1.ap, ALU.subtract, ma_, mb_)
                        b1.release(t_ready[hd])
                    else:
                        b1.release(*b1.free)
                    u_ready[hd] = tt(U_, U_, b2.ap, ALU.subtract, mb_)
                    b2.release(u_ready[hd])

            fence()
            knat, vb, kbg, kdc, uu, wT, qd, oT = (arena[:, a * T:(a + 2) * T] for a in (6, 8, 10, 12, 14, 16, 18, 34))
            for src, dst in ((2, knat), (4, vb)):
                for half in range(2):
                    b = banks.take()
                    for tl in range(2):
                        t = 2 * half + tl
                        for f in range(2):
                            m = PE.do(lambda e, o=b.ap[:, tl * CW + f * P:tl * CW + (f + 1) * P],
                                      s=tile(src + f)[:, t * P:(t + 1) * P]: e.transpose(o, s, K("ident")), *b.free)
                    mk = copy(dst[:, half * T:(half + 1) * T], b.ap, m, q=(V, A)[half])
                    b.release(mk)
                    ready["nat", src, half] = mk
            nat = [ready["nat", s, hf] for s in (2, 4) for hf in range(2)]
            for c in range(16):
                sl = slice(c * HEAD, (c + 1) * HEAD)
                m_kbg = ts(kbg[:, sl], knat[:, sl], be_c[:, c:c + 1], None, ALU.mult, None, *nat)
                m_vb = ts(vb[:, sl], vb[:, sl], beta_c[:, c:c + 1], None, ALU.mult, None, *nat)
                m_kd = ts(kdc[:, sl], knat[:, sl], kd_c[:, c:c + 1], None, ALU.mult, None, *nat, q=G)
            for f in range(2):
                m_qd = tt(qd[:, f * T:(f + 1) * T], qT(f), tile(eB[f]), ALU.mult)
            ub = [banks.take(), banks.take()]
            for c in range(16):
                t, hd = c // 4, c % 4
                m = mm(ub[c // 8].ap[:, c % 8 * HEAD:(c % 8 + 1) * HEAD], tile(UU + hd)[:, t * P:(t + 1) * P],
                       vb[:, c * HEAD:(c + 1) * HEAD], True, True, m_vb, *ub[c // 8].free, last=True)
            for i in range(2):
                m_u = copy(uu[:, i * T:(i + 1) * T], ub[i].ap, m)
                ub[i].release(m_u)
            for f in range(2):
                bp = [banks.take(), banks.take()]
                for t in range(NT):
                    for par in range(2):
                        hd, c = 2 * f + par, 4 * t + 2 * f + par
                        rows = slice(HEAD * par, HEAD * par + HEAD)
                        m = mm(bp[par].ap[rows, t * P:(t + 1) * P], kbg[:, c * HEAD:(c + 1) * HEAD],
                               tile(UU + hd)[:, t * P:(t + 1) * P], True, True, m_kbg, *bp[par].free, last=True)
                for par in range(2):
                    rows = slice(HEAD * par, HEAD * par + HEAD)
                    m_w = copy(wT[rows, f * T:(f + 1) * T], bp[par].ap[rows, :], m, q=A)
                    bp[par].release(m_w)

            state = tile(46)[:, 0:2 * HEAD]
            vn = tile(47)[:, 0:4 * HEAD]
            m_s = [V.do(lambda e: e.memset(state, 0.0))] * 2
            m_vn0 = V.do(lambda e: e.memset(vn, 0.0))
            m_vn = m_vn0
            last_o = ()
            for ch in range(T // CHUNK):
                t, c0 = ch // 2, CHUNK * (ch % 2)
                crow = slice(c0, c0 + CHUNK)
                csl = slice(ch * CHUNK, (ch + 1) * CHUNK)
                vbk = [banks.take(), banks.take()]
                for hd in range(GDN_HEADS):
                    f, par = hd // 2, hd % 2
                    rows = slice(HEAD * par, HEAD * par + HEAD)
                    m = mm(vbk[par].ap[crow, f * HEAD:(f + 1) * HEAD], wT[rows, f * T + ch * CHUNK:f * T + (ch + 1) * CHUNK],
                           state[rows, f * HEAD:(f + 1) * HEAD], True, True, m_w, *m_s, *vbk[par].free, last=True)
                for par in range(2):
                    u_ = uu.rearrange("p (t f q d) -> p t f q d", t=NT, f=2, q=2)[crow, t, :, par, :]
                    o_ = vn.rearrange("p (f q d) -> p f q d", f=2, q=2)[crow, :, par, :]
                    m_vn = tt(o_, u_, vbk[par].ap[crow, 0:2 * HEAD].rearrange("p (f d) -> p f d", f=2), ALU.subtract,
                              m, m_u, m_vn0, *last_o)
                    vbk[par].release(m_vn)
                sbk = [banks.take(), banks.take()]
                for hd in range(GDN_HEADS):
                    f, par = hd // 2, hd % 2
                    rows = slice(HEAD * par, HEAD * par + HEAD)
                    c = 4 * t + hd
                    m = mm(sbk[par].ap[rows, f * HEAD:(f + 1) * HEAD], kdc[crow, c * HEAD:(c + 1) * HEAD],
                           vn[crow, hd * HEAD:(hd + 1) * HEAD], True, True, m_vn, m_kd, *sbk[par].free, last=True)
                obk = [banks.take(), banks.take()]
                for hd in range(GDN_HEADS):
                    f, par = hd // 2, hd % 2
                    rows = slice(HEAD * par, HEAD * par + HEAD)
                    o = obk[par].ap[rows, f * HEAD:(f + 1) * HEAD]
                    mm(o, state[rows, f * HEAD:(f + 1) * HEAD], qd[rows, f * T + ch * CHUNK:f * T + (ch + 1) * CHUNK],
                       True, False, m_qd, *obk[par].free)
                    mo = mm(o, vn[:, hd * HEAD:(hd + 1) * HEAD], tile(QKT + hd)[:, csl], False, True, m_vn, last=True)
                m_s = []
                for hd in range(GDN_HEADS):
                    f, par = hd // 2, hd % 2
                    rows = slice(HEAD * par, HEAD * par + HEAD)
                    st = state[rows, f * HEAD:(f + 1) * HEAD]
                    m_s.append(stt(st, st, tile(eB[f])[rows, (ch + 1) * CHUNK - 1:(ch + 1) * CHUNK],
                                   sbk[par].ap[rows, f * HEAD:(f + 1) * HEAD], ALU.mult, ALU.add, m, mo))
                for par in range(2):
                    sbk[par].release(m_s[-1])
                    rows = slice(HEAD * par, HEAD * par + HEAD)
                    m_o = copy(oT.rearrange("p (f n) -> p f n", f=2)[rows, :, csl],
                               obk[par].ap[rows, 0:2 * HEAD].rearrange("p (f d) -> p f d", f=2), mo, q=A)
                    obk[par].release(m_o)
                last_o = (mo,)
            for f in range(2):
                s, r = gtemps_late[f]
                o_ = oT[:, f * T:(f + 1) * T]
                m = act(tile(s), o_, ACT.Square, m_o)
                b = banks.take()
                m = mm(b.ap, K("sum64"), tile(s), True, True, m, *b.free, last=True)
                m = inv_root(tile(r), b.ap, HEAD, "rms_eps", m)
                b.release(m)
                m = stt(o_, o_, W("gdn_g"), tile(r), ALU.mult, ALU.mult, m)
                m2 = silu_of(tile(s), tile(z_t + f), m)
                m = tt(h[:, 4 + f, :], o_, tile(s), ALU.mult, m, m2)
                ready["y", 4 + f, 0] = ready["y", 4 + f, 1] = m
            return [mk for n in range(KD) for mk in (ready["y", n, 0], ready["y", n, 1])]
        gtemps_late = ((6, 8), (10, 12))

        def layer_norm(marks, gain, shift):
            mean = banks.take()
            for k in range(KD):
                m = mm(mean.ap, K("ones"), x[:, k, :], k == 0, k == KD - 1, marks[k], *mean.free, last=True)
            mu = Buffer(tile(39))
            m = act(mu.ap, mean.ap, ACT.Copy, m, V.last, scale=-1.0 / D)
            mean.release(m)
            var = SquareSum(KD)
            for k in range(KD):
                mc_ = tt(x[:, k, :], x[:, k, :], mu.ap, ALU.add, m)
                var.add(x[:, k, :], mc_)
            var.flush()
            r = temps.take()
            m = inv_root(r.ap, var.bank.ap, D, "ln_eps", var.mark, *r.free)
            var.bank.release(m)
            out = []
            for k in range(KD):
                m1 = stt(x[:, k, :], x[:, k, :], W(gain, k, k + 1), r.ap, ALU.mult, ALU.mult, m)
                out.append(ts(x[:, k, :], x[:, k, :], W(shift, k, k + 1), None, ALU.add, None, m1))
            r.release(out[-1])
            return out

        def modulate(x_ready, which):
            sh, sc = which * 3 * KD, which * 3 * KD + KD
            return [ts(h[:, k, :], x[:, k, :], mod[:, sc + k:sc + k + 1], mod[:, sh + k:sh + k + 1], ALU.mult, ALU.add,
                       x_ready[k], PE.last) for k in range(KD)]

        def gated(d, src, which, m, release=None):
            gt = which * 3 * KD + 2 * KD + d
            s = temps.take()
            m = ts(s.ap, src, mod[:, gt:gt + 1], None, ALU.mult, None, m, *s.free)
            if release:
                release(m)
            m = stt(x[:, d, :], x[:, d, :], ALPHA, s.ap, ALU.mult, ALU.add, m)
            s.release(m)
            return m

        def route(h_ready):
            nat = small[:, 320:448]
            ids, wts = small[:, 96:104], small[:, 104:112]
            for t in range(NT):
                b = banks.take()
                for k in range(KD):
                    mm(b.ap[:, 0:36], h[:, k, t * P:(t + 1) * P], W("router_w", 36 * k, 36 * k + 36), k == 0, False,
                       h_ready[k], *b.free)
                m = mm(b.ap[:, 0:36], K("ones")[0:1, :], rowp[0:1, 8:44], False, True, last=True)
                g8, top, e_ = nat[:, 0:8], nat[:, 8:16], nat[:, 16:24]
                m1 = copy(g8[:, 0:4], b.ap[:, 0:4], m)
                m1 = copy(g8[:, 4:8], K("pad"), m1)
                m1 = V.do(lambda e: e.max(top, g8), m1)
                idx = small[:, 448:456].bitcast(U32)
                m1 = V.do(lambda e: e.max_index(idx, top, g8), m1)
                gi, gp, ng = nat[:, 24:25], nat[:, 25:26], nat[:, 26:27]
                m1 = copy(gi, idx[:, 0:1], m1)
                m1 = ts(ng, top[:, 0:1], -1.0, None, ALU.mult, None, m1)
                ma = act(e_[:, 0:4], g8[:, 0:4], ACT.Exp, m1, bias=ng, accum=gp)
                m_gp = V.do(lambda e: e.reciprocal(gp, gp), ma)
                lg, keep_ = nat[:, 32:64], nat[:, 64:96]
                m1 = ts(nat[:, 27:28], gi, float(PER_GROUP), None, ALU.mult, None, m1)
                m1 = ts(keep_, K("expert_id"), nat[:, 27:28], None, ALU.subtract, None, m1)
                m1 = ts(lg, keep_, 0.0, None, ALU.is_ge, None, m1)
                m1 = ts(keep_, keep_, float(PER_GROUP), None, ALU.is_lt, None, m1)
                m1 = tt(keep_, keep_, lg, ALU.mult, m1)
                m1 = ts(lg, keep_, 1.0, BIG, ALU.subtract, ALU.mult, m1)
                m1 = tt(keep_, keep_, b.ap[:, 4:36], ALU.mult, m1)
                b.release(m1)
                m1 = tt(lg, lg, keep_, ALU.add, m1)
                m1 = V.do(lambda e: e.max(top, lg), m1)
                m1 = V.do(lambda e: e.max_index(idx, top, lg), m1)
                m1 = copy(ids[:, 2 * t:2 * t + 2], idx[:, 0:2], m1)
                d2 = nat[:, 30:31]
                m1 = tt(d2, top[:, 1:2], top[:, 0:1], ALU.subtract, m1)
                m1 = act(d2, d2, ACT.Exp, m1)
                w1, w2 = wts[:, 2 * t:2 * t + 1], wts[:, 2 * t + 1:2 * t + 2]
                m1 = ts(w1, d2, 1.0, None, ALU.add, None, m1)
                m1 = V.do(lambda e, w1=w1: e.reciprocal(w1, w1), m1)
                m1 = tt(w1, w1, gp, ALU.mult, m1, m_gp)
                m1 = tt(w2, w1, d2, ALU.mult, m1)
            return ids, wts, m1

        def moe(h_ready):
            def at(first, n):
                return arena[:, first * T:first * T + n]

            s_rows, s_init, s_scatter, s_back = (sem(n) for n in ("h_rows", "slots_cleared", "slots_scattered", "slots_read"))
            rows_buf = [at(0, D), at(2, D), at(4, D), at(6, D)]
            for t in range(NT):
                for half in range(2):
                    b = banks.take()
                    for k in range(4):
                        d = 4 * half + k
                        m = PE.do(lambda e, o=b.ap[:, k * P:(k + 1) * P], i_=h[:, d, t * P:(t + 1) * P]:
                                  e.transpose(o, i_, K("ident")), h_ready[d], *b.free)
                    m = copy(rows_buf[t][:, half * T:(half + 1) * T], b.ap, m, q=(A, V)[half])
                    b.release(m)
                    if half == 0:
                        m0 = m
                S.wait(m0, m)
                S.steps.append(lambda e, t=t: e.dma_start(io["h_rows"][t * P:(t + 1) * P, :], rows_buf[t]).then_inc(s_rows, 16))

            ids, wts, m_route = route(h_ready)

            picks = at(8, 2 * NT * EXPERTS)
            both = at(9, NT * EXPERTS)
            prod = at(10, 2 * NT * EXPERTS)
            run, total = at(11, EXPERTS), arena[:, 11 * T + 64:11 * T + 64 + EXPERTS]
            first = arena[:, 11 * T + 128:11 * T + 128 + EXPERTS]
            for c in range(2 * NT):
                m = ts(picks[:, c * EXPERTS:(c + 1) * EXPERTS], K("expert_id"), ids[:, c:c + 1], None, ALU.is_equal, None, m_route)
            for t in range(NT):
                m = tt(both[:, t * EXPERTS:(t + 1) * EXPERTS], picks[:, 2 * t * EXPERTS:(2 * t + 1) * EXPERTS],
                       picks[:, (2 * t + 1) * EXPERTS:(2 * t + 2) * EXPERTS], ALU.add, m)
            rank = banks.take()
            for t in range(NT):
                o = rank.ap[:, t * EXPERTS:(t + 1) * EXPERTS]
                for u in range(t + 1):
                    mr = mm(o, K("before") if u == t else K("ones"), both[:, u * EXPERTS:(u + 1) * EXPERTS], u == 0,
                            u == t, m, *rank.free, last=True)
            count = banks.take()
            for t in range(NT):
                mc = mm(count.ap[:, 0:EXPERTS], K("ones"), both[:, t * EXPERTS:(t + 1) * EXPERTS], t == 0, t == NT - 1,
                        *count.free, last=True)
            m = ts(total, count.ap[:, 0:EXPERTS], 0.0, None, ALU.is_gt, None, mc)
            for lim in (128.0, 256.0, 384.0):
                m = ts(run, count.ap[:, 0:EXPERTS], lim, None, ALU.is_gt, None, m)
                m = tt(total, total, run, ALU.add, m)
            count.release(m)
            m = V.do(lambda e: e.tensor_tensor_scan(run, K("ones")[:, 0:EXPERTS], total, 0.0, ALU.mult, ALU.add), m)
            m = tt(first, run, total, ALU.subtract, m)
            m_first = ts(first, first, float(P), None, ALU.mult, None, m)
            ends = at(12, NBLOCK * EXPERTS)
            for blk in range(NBLOCK):
                m = ts(ends[:, blk * EXPERTS:(blk + 1) * EXPERTS], run, float(blk), None, ALU.is_le, None, m_first)
            bexp = small[:, 128:128 + NBLOCK]
            m = V.do(lambda e: e.tensor_reduce(bexp, ends.rearrange("p (b n) -> p b n", n=EXPERTS), AXX, ALU.add), m)
            bexp_u = small[:, 168:168 + NBLOCK].bitcast(U32)
            m_blk = ts(bexp_u, bexp, float(EXPERTS - 1), None, ALU.min, None, m)
            dest, dest_u = small[:, 112:120], small[:, 120:128].bitcast(U32)
            for t in range(NT):
                r_ = rank.ap[:, t * EXPERTS:(t + 1) * EXPERTS]
                m = tt(both[:, t * EXPERTS:(t + 1) * EXPERTS], r_, first, ALU.add, mr, mc, m_first)
                for k in range(2):
                    c = 2 * t + k
                    sl = slice(c * EXPERTS, (c + 1) * EXPERTS)
                    m1 = tt(prod[:, sl], picks[:, sl], both[:, t * EXPERTS:(t + 1) * EXPERTS], ALU.mult, m)
            rank.release(m)
            m = V.do(lambda e: e.tensor_reduce(dest, prod.rearrange("p (c n) -> p c n", n=EXPERTS), AXX, ALU.add), m1)
            m_dest = copy(dest_u, dest, m)

            zero = at(15, P)
            mz = G.do(lambda e: e.memset(zero[0:NBLOCK, :], 0.0))
            G.wait(mz)
            slots = io["slot_token"]
            G.steps.append(lambda e: e.dma_start(slots.rearrange("(b p) o -> b (p o)", p=P), zero[0:NBLOCK, :]).then_inc(s_init, 16))
            G.wait((s_init, 16), m_dest)
            for c in range(2 * NT):
                G.steps.append(lambda e, c=c: e.indirect_dma_start(
                    out=slots, out_offset=bass.IndirectOffsetOnAxis(ap=dest_u[:, c:c + 1], axis=0),
                    in_=K("token_id")[:, c // 2:c // 2 + 1], in_offset=None).then_inc(s_scatter, 16))
            G.wait((s_scatter, 16 * 2 * NT))
            tok_rows = at(16, P)
            G.steps.append(lambda e: e.dma_start(tok_rows[0:NBLOCK, :], slots.rearrange("(b p) o -> b (p o)", p=P)).then_inc(s_back, 16))
            b = banks.take()
            m = PE.do(lambda e: e.transpose(b.ap[:, 0:NBLOCK], tok_rows[0:NBLOCK, :], K("ident")[0:NBLOCK, 0:NBLOCK]),
                      (s_back, 16), *b.free)
            tok_u = small[:, 208:208 + NBLOCK].bitcast(U32)
            m_tok = copy(tok_u, b.ap[:, 0:NBLOCK], m)
            b.release(m_tok)

            NG = 3
            gathered = [at(17 + 2 * i, D) for i in range(NG)]
            s_gather = [sem(f"gathered{i}") for i in range(NG)]
            gather_free = [()] * NG
            turned = Rotation([at(23 + 2 * i, D) for i in range(2)])
            hid = Rotation([at(27, CW), arena[:, 27 * T + CW:28 * T]])
            hid_t = Rotation([at(28, CW), arena[:, 28 * T + CW:29 * T]])
            outs = Rotation([at(29 + 2 * i, D) for i in range(3)])
            s_y = [sem(f"block_rows_stored{i}") for i in range(3)]
            G.wait((s_rows, 16 * NT), m_tok)

            def gather(blk):
                i = blk % NG
                G.wait(*gather_free[i])
                G.steps.append(lambda e: e.indirect_dma_start(
                    out=gathered[i], out_offset=None, in_=io["h_rows"],
                    in_offset=bass.IndirectOffsetOnAxis(ap=tok_u[:, blk:blk + 1], axis=0)).then_inc(s_gather[i], 16))
                return i, (s_gather[i], 16 * (blk // NG + 1))

            def turn(blk, g):
                i, full = g
                x_t = turned.take()
                marks = []
                for half in range(2):
                    b = banks.take()
                    for k in range(4):
                        m = PE.do(lambda e, o=b.ap[:, k * P:(k + 1) * P], s=gathered[i][:, (4 * half + k) * P:(4 * half + k + 1) * P]:
                                  e.transpose(o, s, K("ident")), full, *b.free)
                    mk = copy(x_t.ap[:, half * T:(half + 1) * T], b.ap, m, *x_t.free, q=(A, V)[half])
                    b.release(mk)
                    marks.append(mk)
                gather_free[i] = (m,)
                return x_t, marks

            expert_of = {}

            def expert_load(name, blk, half, marks=()):
                def src(e):
                    if blk not in expert_of:
                        expert_of[blk] = e.value_load(bexp_u[0:1, blk:blk + 1], min_val=0, max_val=EXPERTS - 1)
                    w = io[name][bass.DynSlice(expert_of[blk], 1)]
                    w = w.rearrange("a p c -> (a p) c")
                    return w if half is None else w[:, half * SLOT:(half + 1) * SLOT]
                return load_with(src)

            def load_with(src):
                i = loads[0] % NSLOT
                use = loads[0] // NSLOT + 1
                loads[0] += 1
                S.wait(*slot_free[i])
                slot_free[i] = None
                S.steps.append(lambda e: e.dma_start(ring[:, i, :], src(e)).then_inc(slot_full[i], 16))
                return i, (slot_full[i], 16 * use)

            def gate_up(blk, x_t, x_marks):
                b = banks.take()
                for half in range(2):
                    i, full = expert_load("moe_in", blk, half)
                    for k in range(4):
                        m = mm(b.ap, x_t.ap[:, (4 * half + k) * P:(4 * half + k + 1) * P], ring[:, i, k * T:(k + 1) * T],
                               half + k == 0, half == 1 and k == 3, full, x_marks[half], *b.free, last=k == 3)
                    done_with(i, m)
                x_t.release(m)
                hb = hid.take()
                m = silu_of(hb.ap, b.ap[:, 0:CW], m, *hb.free)
                m = tt(hb.ap, hb.ap, b.ap[:, CW:2 * CW], ALU.mult, m)
                b.release(m)
                return hb, m

            def turn_hidden(hb, m):
                b, ht = banks.take(), hid_t.take()
                for k in range(2):
                    mk = PE.do(lambda e, o=b.ap[:, k * P:(k + 1) * P], s=hb.ap[:, k * P:(k + 1) * P]:
                               e.transpose(o, s, K("ident")), m, *b.free)
                hb.release(mk)
                mk = copy(ht.ap, b.ap[:, 0:CW], mk, *ht.free)
                b.release(mk)
                return ht, mk

            def down(blk, ht, m_ht):
                i, full = expert_load("moe_down", blk, None)
                ob = outs.take()
                marks = []
                for half in range(2):
                    b = banks.take()
                    for k in range(2):
                        m = mm(b.ap, ht.ap[:, k * P:(k + 1) * P], ring[:, i, k * D + half * T:k * D + (half + 1) * T], k == 0,
                               k == 1, full, m_ht, *b.free, last=True)
                    mk = copy(ob.ap[:, half * T:(half + 1) * T], b.ap, m, *ob.free, q=(A, V)[half])
                    b.release(mk)
                    marks.append(mk)
                ht.release(m)
                done_with(i, m)
                A.wait(*marks)
                A.steps.append(lambda e: e.dma_start(io["block_rows"][blk * P:(blk + 1) * P, :], ob.ap).then_inc(s_y[blk % 3], 16))
                ob.release((s_y[blk % 3], 16 * (blk // 3 + 1)))

            S.wait(m_blk)
            g = [gather(0), gather(1)]
            cur = turn(0, g[0])
            held = None
            for blk in range(NBLOCK):
                if blk + 2 < NBLOCK:
                    g.append(gather(blk + 2))
                hb, m = gate_up(blk, *cur)
                if blk + 1 < NBLOCK:
                    cur = turn(blk + 1, g[blk + 1])
                if held:
                    down(*held)
                held = (blk, *turn_hidden(hb, m))
            down(*held)

            fence()
            G.wait(*[(s_y[i], 16 * len(range(i, NBLOCK, 3))) for i in range(3)])
            pair = [[at(4 * t + 2 * k, D) for k in range(2)] for t in range(NT)]
            s_pair = [[sem(f"pair{t}{k}") for k in range(2)] for t in range(NT)]
            for t in range(NT):
                for k in range(2):
                    c = 2 * t + k
                    G.steps.append(lambda e, t=t, k=k, c=c: e.indirect_dma_start(
                        out=pair[t][k], out_offset=None, in_=io["block_rows"],
                        in_offset=bass.IndirectOffsetOnAxis(ap=dest_u[:, c:c + 1], axis=0)).then_inc(s_pair[t][k], 16))
            bb = [banks.take() for _ in range(KD)]
            for t in range(NT):
                m = ts(pair[t][0], pair[t][0], wts[:, 2 * t:2 * t + 1], None, ALU.mult, None, (s_pair[t][0], 16))
                m = stt(pair[t][0], pair[t][1], wts[:, 2 * t + 1:2 * t + 2], pair[t][0], ALU.mult, ALU.add, m, (s_pair[t][1], 16))
                for d in range(KD):
                    mt = PE.do(lambda e, o=bb[d].ap[:, t * P:(t + 1) * P], s=pair[t][0][:, d * P:(d + 1) * P]:
                               e.transpose(o, s, K("ident")), m, *bb[d].free)
            return bb, mt

        def run():
            stats = SquareSum(KD)
            for k in range(KD):
                stats.add(x[:, k, :])
            c_ready = mod_start()
            for layer in range(DEPTH):
                hr = rms_to_h(stats, "ffn1_norm", layer * KD)
                stats = SquareSum(KD)
                aside = None
                if layer == 0:
                    def aside(j):
                        mod_columns()
                        for n in range(24 * j // 11, 24 * (j + 1) // 11):
                            mod_step(n, c_ready)
                ffn(hr, io["ffn1_in"][layer], io["ffn1_out"][layer], stats, aside)
                if layer == 0:
                    mod_columns()
                    for a in (KD, 4 * KD):
                        sl = mod[:, a:a + 2 * KD]
                        mod_marks.append(ts(sl, sl, 1.0, None, ALU.add, None, *mod_marks))
                if stage("ffn1"):
                    return
                hr = rms_to_h(stats, "mix_norm", layer * KD)
                fence()
                stats = SquareSum(KD)
                mixer1(layer, hr, stats)
                if stage("mix1"):
                    return
                hr = rms_to_h(stats, "ffn2_norm", layer * KD)
                fence()
                stats = SquareSum(KD)
                ffn(hr, io["ffn2_in"][layer], io["ffn2_out"][layer], stats)
                if stage("ffn2"):
                    return
            stats.flush()
            r = temps.take()
            m = inv_root(r.ap, stats.bank.ap, D, "rms_eps", stats.mark, *r.free)
            stats.bank.release(m)
            xr = [stt(x[:, k, :], x[:, k, :], W("final_norm", k, k + 1), r.ap, ALU.mult, ALU.mult, m) for k in range(KD)]
            r.release(xr[-1])
            fence()
            if stage("first"):
                return
            hr = modulate(xr, 0)
            V.wait(hr[-1])
            nonlocal_temps(45, 48)
            y_ready = mixer2(hr)
            fence()
            nonlocal_temps(40, 48)
            if stage("mixed"):
                for k in range(KD):
                    copy(x[:, k, :], h[:, k, :])
                return
            xr = [None] * KD

            def take(d, b, m):
                xr[d] = gated(d, b.ap, 0, m, b.release)
            out_project(io["w_out2"], y_ready, take, None)
            xr = layer_norm(xr, "ln1_g", "ln1_b")
            if stage("ln1"):
                return
            hr = modulate(xr, 1)
            fence()
            bb, m = moe(hr)
            xr = [gated(d, bb[d].ap, 1, m, bb[d].release) for d in range(KD)]
            layer_norm(xr, "ln2_g", "ln2_b")

        def nonlocal_temps(a, b):
            temps.buffers, temps.n = [Buffer(tile(i)) for i in range(a, b)], 0

        seen = {}
        mod_marks = []

        def stage(name):
            seen[name] = seen.get(name, 0) + 1
            return stages == f"{name}.{seen[name]}"

        run()
        S.wait(V.last)
        S.steps.append(lambda e: e.dma_start(io["outT"].rearrange("(t p) n -> p t n", p=P), x[:, :, :]).then_inc(s_out, 16))
        S.wait((s_out, 16))

        block = ctx.enter_context(nc.Block())

        @block.sync
        def _(e):
            for s in S.steps:
                s(e)

        @block.scalar
        def _(e):
            for s in A.steps:
                s(e)

        @block.vector
        def _(e):
            for s in V.steps:
                s(e)

        @block.gpsimd
        def _(e):
            for s in G.steps:
                s(e)

        @block.tensor
        def _(e):
            for s in PE.steps:
                s(e)


def column_chunks(w):
    *lead, k, n = w.shape
    w = w.reshape(*lead, k // P, P, n // CW, CW)
    w = np.moveaxis(w, -2, -4)
    return np.ascontiguousarray(np.swapaxes(w, -3, -2)).reshape(*lead, n // CW, P, k // P * CW)


def feature_columns(v):
    v = np.asarray(v)
    return v.reshape(-1, P).T


def pack(i):
    a = {k: np.asarray(v) for k, v in i.items()}
    w2 = a["w_in_2"][0]
    perm = np.concatenate([np.arange(0, 384), np.arange(320, 416), np.arange(1440, 1448), np.arange(0, 24),
                           np.arange(416, 1440), np.arange(1448, 1704)])
    params = {
        "ffn1_norm": feature_columns(a["ffn1_norm"]), "mix_norm": feature_columns(a["mix_norm"]),
        "ffn2_norm": feature_columns(a["ffn2_norm"]), "final_norm": feature_columns(a["final_norm"]),
        "conv_w": a["conv_w"].reshape(DEPTH, CONV_TAPS, 2, P).transpose(3, 0, 2, 1).reshape(P, -1),
        "conv_b": feature_columns(a["conv_b"]), "conv_ln_g": feature_columns(a["conv_ln_g"]),
        "conv_ln_b": feature_columns(a["conv_ln_b"]), "ret_norm_g": feature_columns(a["ret_norm_g"]),
        "c": feature_columns(a["c_2"]), "b_mod": feature_columns(a["b_mod_2"]),
        "q_norm": feature_columns(a["mla_q_norm_2"]), "kv_norm": feature_columns(a["mla_kv_norm_2"]),
        "gdn_conv": a["gdn_conv_2"][0].reshape(GDN_TAPS, 6, P).transpose(2, 1, 0).reshape(P, -1),
        "gdn_g": np.concatenate([a["gdn_out_norm_2"][0]] * 2)[:, None],
        "pool_scale": feature_columns(a["pool_scale_2"]),
        "pool_w": a["pool_w_2"][0].reshape(2, 2, 64, 64).transpose(1, 2, 0, 3).reshape(P, 128),
        "router_w": np.concatenate([a["router_w_group_2"][0], a["router_w_expert_2"][0]], 1)
        .reshape(KD, P, 36).transpose(1, 0, 2).reshape(P, -1),
        "ln1_g": feature_columns(a["ln1_g_2"]), "ln1_b": feature_columns(a["ln1_b_2"]),
        "ln2_g": feature_columns(a["ln2_g_2"]), "ln2_b": feature_columns(a["ln2_b_2"]),
    }
    return {
        "xT": np.ascontiguousarray(a["x"][0].T),
        "consts": np.concatenate(list(CONSTS.values()), 1),
        "params": np.ascontiguousarray(np.concatenate([params[k] for k in PARAM_AT], 1)),
        "rows": np.concatenate([a["gdn_dt_bias_2"][0], a["gdn_a_log_2"][0], a["router_b_group_2"][0],
                                a["router_b_expert_2"][0]])[None, :],
        "ffn1_in": column_chunks(a["ffn1_w_in"]), "ffn1_out": column_chunks(a["ffn1_w_out"]),
        "mix_w_in": column_chunks(a["mix_w_in"]), "mix_w_out": column_chunks(a["mix_w_out"]),
        "ffn2_in": column_chunks(a["ffn2_w_in"]), "ffn2_out": column_chunks(a["ffn2_w_out"]),
        "w_mod": column_chunks(a["w_mod_2"][0]),
        "w_in2": column_chunks(w2[:, perm]),
        "w_uq": np.ascontiguousarray(a["mla_w_uq_2"][0].reshape(2, P, MLA_HEADS * QK).transpose(1, 0, 2)).reshape(P, -1),
        "w_ukv": np.ascontiguousarray(a["mla_w_ukv_2"][0]),
        "w_out2": column_chunks(a["w_out_2"][0]),
        "moe_in": np.ascontiguousarray(np.stack([a["moe_w_gate_2"][0], a["moe_w_up_2"][0]], 2)
                                       .reshape(EXPERTS, KD, P, 2 * CW).transpose(0, 2, 1, 3)).reshape(EXPERTS, P, -1),
        "moe_down": np.ascontiguousarray(a["moe_w_down_2"][0].reshape(EXPERTS, 2, P, D).transpose(0, 2, 1, 3))
        .reshape(EXPERTS, P, 2 * D),
    }


def kernel(**inputs):
    import concourse.bacc as bacc
    from concourse.bass_utils import run_bass_kernel_spmd

    nc = bacc.Bacc("TRN2", target_bir_lowering=False, num_devices=1)
    arrays = pack(inputs)
    io = {k: nc.dram_tensor(k, v.shape, mybir.dt.from_np(v.dtype), kind="ExternalInput").ap() for k, v in arrays.items()}
    for name, shape in SCRATCH.items():
        io[name] = nc.dram_tensor(name, shape, F32, kind="Internal").ap()
    io["outT"] = nc.dram_tensor("outT", (D, T), F32, kind="ExternalOutput").ap()
    build(nc, io)
    r = run_bass_kernel_spmd(nc, [arrays], core_ids=[0])
    return np.ascontiguousarray(np.asarray(r.results[0]["outT"]).T)[None]
```

```python
from contextlib import ExitStack

import concourse.bass as bass
import numpy as np
from concourse import mybir

F32 = mybir.dt.float32
F32R = mybir.dt.float32r
U32 = mybir.dt.uint32
ACT = mybir.ActivationFunctionType
ALU = mybir.AluOpType
AXX = mybir.AxisListType.X

P = 128
T = 512
D = 1024
KD = D // P
NT = T // P
DEPTH = 2
FF = 2816
KF = FF // P
CW = 256
SLOT = KD * CW
NSLOT = 3
SUB = SLOT // 2
NSUB = 3
MOE_SLOTS = 6
HID_TILES = 12
HEAD = 64
CHUNK = 64
SB_HEADS = 8
RET_HEADS = 4
CONV_TAPS = 31
PAD = CONV_TAPS - 1
MLA_HEADS = 8
NOPE, ROPE = 64, 32
QK = NOPE + ROPE
GDN_HEADS = 4
GDN_TAPS = 4
POOL_WINDOWS = (2, 4, 8, 16)
POOL_PAD = 16
EXPERTS = 32
NBLOCK = EXPERTS + (2 * T - EXPERTS) // P
GROUPS = 4
PER_GROUP = EXPERTS // GROUPS
ALPHA = 2 ** 0.25
RMS_EPS, LN_EPS = 1e-6, 1e-5
BIG = 1e30
FFN_PARTS = ((0, HID_TILES // 2), (HID_TILES // 2, FF // CW))


def constant_tables():
    i = np.arange(P)
    row, col = i[:, None], i[None, :]
    same64 = (row // 64) == (col // 64)
    t = {}
    t["ident"] = np.eye(P)
    t["ones"] = np.ones((P, P))
    t["sum64"] = same64 * 1.0
    t["mean64"] = same64 / 64.0
    t["centre64"] = np.eye(P) - same64 / 64.0
    t["neg_suffix"] = -1.0 * (row >= col)
    t["neg_ones"] = -np.ones((P, P))
    t["swap64"] = np.where(same64, np.where(row == col + 32, -1.0 * (col % 64 < 32), 0.0)
                           + np.where(row == col - 32, 1.0 * (col % 64 >= 32), 0.0), 0.0)
    r, c = row - NOPE, col - NOPE
    inside = (r >= 0) & (r < ROPE) & (c >= 0) & (c < ROPE)
    t["swap32"] = np.where(inside, np.where(r == c + 16, -1.0 * (c < 16), 0.0)
                           + np.where(r == c - 16, 1.0 * (c >= 16), 0.0), 0.0)
    t["incl"] = same64 * (row <= col) * 1.0
    t["strict"] = same64 * (row < col) * 1.0
    t["later"] = same64 * (row > col) * 1.0
    for lv in range(6):
        s = 2 ** lv
        t[f"level{lv}"] = 1.0 * (((col // s) % 2 == 1) & (row // s == col // s - 1))
    pos = np.arange(T, dtype=np.float32)
    inv = (1.0 / (np.float32(10000.0) ** (np.arange(32, dtype=np.float32) / np.float32(32)))).astype(np.float32)
    ang = (pos[None, :] * inv[i % 32][:, None]).astype(np.float32)
    t["cos64"], t["sin64"] = np.cos(ang.astype(np.float64)), np.sin(ang.astype(np.float64))
    inv = (np.float32(10000.0) ** (-np.arange(0, 32, 2, dtype=np.float32) / np.float32(32))).astype(np.float32)
    ang = (pos[None, :] * inv[i % 16][:, None]).astype(np.float32)
    t["cos32"], t["sin32"] = np.cos(ang.astype(np.float64)), np.sin(ang.astype(np.float64))
    tt = np.arange(T)[None, :]
    for h in range(RET_HEADS):
        gamma = 1.0 - 2.0 ** (-5.0 - h)
        t[f"decay{h}"] = np.where(tt // CHUNK >= row // CHUNK, gamma ** np.abs(tt - row), 0.0) * HEAD ** -0.5
    for g in range(2):
        win = np.array([POOL_WINDOWS[2 * g + (p >= 64)] for p in range(P)])[:, None]
        t[f"inv_count{g}"] = 1.0 / np.minimum(tt + 1, win)
    t["rms_eps"] = np.full((P, 1), RMS_EPS)
    t["ln_eps"] = np.full((P, 1), LN_EPS)
    t["one"] = np.ones((P, 1))
    t["expert_id"] = np.tile(np.arange(EXPERTS)[None, :], (P, 1))
    t["before"] = 1.0 * (row < col)
    t["token_id"] = np.repeat(i[:, None] + P * np.arange(NT)[None, :], 2, 1)
    t["slot_id"] = np.tile(i[None, :], (P, 1))
    return {k: np.asarray(v, np.float32) for k, v in t.items()}


def offsets(widths):
    at, out = 0, {}
    for name, w in widths:
        out[name] = (at, at + w)
        at += w
    return out, at


CONSTS = constant_tables()
TABLES = {
    "first": ["swap64", "centre64", "neg_suffix", "neg_ones", "cos64", "sin64"] + [f"decay{i}" for i in range(RET_HEADS)],
    "second": ["swap32", "incl", "strict", "later"] + [f"level{i}" for i in range(6)]
    + ["cos32", "sin32", "inv_count0", "inv_count1"],
    "experts": ["before", "token_id", "slot_id", "expert_id"],
}
TABLES["common"] = [k for k in CONSTS if k not in TABLES["first"] + TABLES["second"] + TABLES["experts"]]
TABLE_AT = {g: offsets([(k, CONSTS[k].shape[1]) for k in names]) for g, names in TABLES.items()}
PARAM_AT, PARAM_W = offsets([
    ("ffn1_norm", DEPTH * KD), ("mix_norm", DEPTH * KD), ("ffn2_norm", DEPTH * KD), ("final_norm", KD),
    ("conv_w", DEPTH * 2 * CONV_TAPS), ("conv_b", DEPTH * 2), ("conv_ln_g", DEPTH * 2),
    ("conv_ln_b", DEPTH * 2), ("ret_norm_g", DEPTH * 2),
    ("c", KD), ("b_mod", 6 * KD), ("q_norm", 2), ("kv_norm", 1), ("gdn_conv", 6 * GDN_TAPS),
    ("gdn_g", 1), ("pool_scale", 2), ("pool_w", 128), ("router_w", KD * (GROUPS + EXPERTS)),
    ("ln1_g", KD), ("ln1_b", KD), ("ln2_g", KD), ("ln2_b", KD)])
ROW_AT, ROW_W = offsets([("dt_bias", GDN_HEADS), ("a_log", GDN_HEADS), ("router_b", GROUPS + EXPERTS)])


SCRATCH = {"h_rows": (T, D), "block_rows": (NBLOCK * P, D)}


class Queue:

    def __init__(self, sem):
        self.sem, self.count, self.steps, self.reached = sem, 0, [], {}

    def wait(self, *marks):
        for sem, value in marks:
            if value > self.reached.get(id(sem), 0):
                self.reached[id(sem)] = value
                self.steps.append(lambda e, s=sem, v=value: e.wait_ge(s, v))

    def do(self, op, *marks):
        self.wait(*marks)
        self.count += 1
        self.steps.append(lambda e, s=self.sem: op(e).then_inc(s, 1))
        return self.sem, self.count

    def quiet(self, op, *marks):
        self.wait(*marks)
        self.steps.append(op)

    @property
    def last(self):
        return (self.sem, self.count)


class Buffer:
    def __init__(self, ap):
        self.ap, self.free = ap, ()

    def release(self, *marks):
        self.free = marks


class Rotation:

    def __init__(self, aps):
        self.buffers, self.n = [Buffer(a) for a in aps], 0

    def take(self):
        for _ in self.buffers:
            b = self.buffers[self.n % len(self.buffers)]
            self.n += 1
            if b.free is not None:
                break
        assert b.free is not None, "all taken, before their readers are queued"
        out = Buffer(b.ap)
        out.free, b.free = b.free, None
        out.release = lambda *marks, b=b: set_free(b, marks)
        return out


def set_free(b, marks):
    b.free = marks


def build(nc, io, stages=None):
    with ExitStack() as ctx:
        def sbuf(name, shape, dt=F32):
            return ctx.enter_context(nc.sbuf_tensor(name, shape, dt))

        def sem(name):
            return ctx.enter_context(nc.semaphore(name))

        x = sbuf("x", [P, KD, T])
        ring = sbuf("ring", [P, NSLOT, SLOT])
        param = sbuf("param", [P, PARAM_W])
        rowp = sbuf("rowp", [1, ROW_W])
        small = sbuf("small", [P, 464])
        tables = {"common": sbuf("common_tables", [P, TABLE_AT["common"][1]])}
        sums = Rotation([sbuf(f"square_sum{i}", [P, POOL_PAD + T])[:, :] for i in range(2)])
        psum = ctx.enter_context(nc.psum_tensor("psum", [P, 8, T], F32))

        V, A, PE, G = (Queue(sem(f"{n}_done")) for n in ("vector", "scalar", "tensor", "gpsimd"))
        S = Queue(sem("sync_unused"))
        slot_full = [sem(f"slot{i}_full") for i in range(NSLOT)]
        s_const, s_param, s_out = sem("common_tables_loaded"), sem("parameters_loaded"), sem("out_stored")
        s_tables, s_filled = sem("tables_loaded"), sem("unused_rows_filled")

        def tile(i, n=1):
            return arena[:, i * T:(i + n) * T]

        def K(name, a=0, b=None):
            group = next(g for g, (at_, _) in TABLE_AT.items() if name in at_)
            lo, hi = TABLE_AT[group][0][name]
            return tables[group][:, lo + a:(hi if b is None else lo + b)]

        def W(name, a=0, b=None):
            lo, hi = PARAM_AT[name]
            return param[:, lo + a:(hi if b is None else lo + b)]

        banks = Rotation([psum[:, i, :] for i in range(8)])
        arena, temps = None, None
        hid_hi = hid_lo = None
        phase, phases = [None], []

        def begin(name, tiles, temp_tiles, group=None, hidden=False):
            nonlocal arena, temps, hid_hi, hid_lo
            fence()
            if phase[0]:
                phase[0].close()
            phase[0] = ExitStack()
            n = len(phases)
            phases.append(name)
            if hidden:
                hid_hi = phase[0].enter_context(nc.sbuf_tensor(f"hidden_hi{n}", [P, HID_TILES, T], F32R))
                hid_lo = phase[0].enter_context(nc.sbuf_tensor(f"hidden_lo{n}", [P, HID_TILES, T], F32R))
            arena = phase[0].enter_context(nc.sbuf_tensor(f"arena{n}", [P, tiles * T], F32))
            temps = Rotation([tile(i) for i in temp_tiles])
            if group:
                tables[group] = phase[0].enter_context(nc.sbuf_tensor(f"tables{n}", [P, TABLE_AT[group][1]], F32))
                dst = tables[group]
                G.steps.append(lambda e: e.dma_start(dst[:, :], io[group]).then_inc(s_tables, 16))
                loaded[0] += 16

        loaded = [0]

        def mm(out, lhsT, rhs, start, stop, *marks, last=False, loose=False):
            def op(e):
                return e.matmul(out, lhsT, rhs, start=start, stop=stop, skip_group_check=loose)
            return PE.do(op, *marks) if last else PE.quiet(op, *marks)

        holds_exp_ln = [False]

        def act(out, in_, func, *marks, scale=1.0, bias=0.0, accum=None):
            if func in (ACT.Exp, ACT.Ln) and not holds_exp_ln[0]:
                A.steps.append(lambda e: e.preload_act_table_set("natural_log_exp_and_others"))
                holds_exp_ln[0] = True
            elif func in (ACT.Silu, ACT.Sigmoid):
                holds_exp_ln[0] = False
            if accum is not None:
                return A.do(lambda e: e.activation(out, in_, func, bias=bias, scale=scale, accum_out=accum), *marks)
            return A.do(lambda e: e.activation(out, in_, func, bias=bias, scale=scale), *marks)

        def tt(out, a, b, op, *marks, q=V):
            return q.do(lambda e: e.tensor_tensor(out, a, b, op), *marks)

        def ts(out, a, s1, s2, op0, op1, *marks, q=V):
            if op1 is None:
                return q.do(lambda e: e.tensor_scalar(out, a, s1, None, op0), *marks)
            return q.do(lambda e: e.tensor_scalar(out, a, s1, s2, op0, op1), *marks)

        def stt(out, a, s, b, op0, op1, *marks):
            return V.do(lambda e: e.scalar_tensor_tensor(out=out, in0=a, scalar=s, in1=b, op0=op0, op1=op1), *marks)

        def copy(out, a, *marks, q=V):
            if q is A:
                return act(out, a, ACT.Copy, *marks)
            return q.do(lambda e: e.tensor_copy(out, a), *marks)

        def fence():
            marks = [q.last for q in (V, A, PE, G) if q.count]
            for q in (V, A, G):
                q.wait(*marks)

        def sbuf_phase(name, shape):
            return phase[0].enter_context(nc.sbuf_tensor(name, shape, F32))

        loads = [0]
        slot_free = [()] * NSLOT

        def load(src, width=SLOT):
            i = loads[0] % NSLOT
            use = loads[0] // NSLOT + 1
            loads[0] += 1
            assert slot_free[i] is not None, "slot filled before its readers are queued"
            S.wait(*slot_free[i])
            slot_free[i] = None
            S.steps.append(lambda e: e.dma_start(ring[:, i, 0:width], src).then_inc(slot_full[i], 16))
            return i, (slot_full[i], 16 * use)

        def done_with(i, *marks):
            slot_free[i] = marks

        split_ctx = ExitStack()
        w_hi = split_ctx.enter_context(nc.sbuf_tensor("w_hi", [P, NSUB, SUB], F32R))
        w_lo = split_ctx.enter_context(nc.sbuf_tensor("w_lo", [P, NSUB, SUB], F32R))
        h_hi = split_ctx.enter_context(nc.sbuf_tensor("h_hi", [P, KD, T], F32R))
        h_lo = split_ctx.enter_context(nc.sbuf_tensor("h_lo", [P, KD, T], F32R))
        sub_bufs = Rotation([(w_hi[:, i, :], w_lo[:, i, :]) for i in range(NSUB)])

        def split(hi, lo, src, *marks, qlo=V):
            m = act(hi, src, ACT.Copy, *marks)
            return m, tt(lo, src, hi.bitcast(F32), ALU.subtract, m, *marks, q=qlo)

        class Weights:

            def __init__(self, items):
                self.items = list(items)[::-1]
                self.slot, self.raws, self.ready = None, [], []

            def fill(self):
                while len(self.ready) < NSUB - 1:
                    if self.slot is None:
                        if not self.items or (self.items[-1][0] == "raw" and self.raws):
                            return
                        kind, src, width = self.items.pop()
                        i, full = load(src, width)
                        if kind == "raw":
                            self.raws.append((i, full))
                            continue
                        self.slot = i, full, [(a, min(SUB, width - a)) for a in range(0, width, SUB)]
                    i, full, pieces = self.slot
                    a, n = pieces.pop(0)
                    b = sub_bufs.take()
                    mh, ml = split(b.ap[0][:, 0:n], b.ap[1][:, 0:n], ring[:, i, a:a + n], full, *b.free)
                    self.ready.append((b, n, mh, ml))
                    if not pieces:
                        done_with(i, mh, ml)
                        self.slot = None

            def take(self):
                if not self.ready:
                    self.fill()
                got = self.ready.pop(0)
                self.fill()
                return got

            def raw(self):
                if not self.raws:
                    self.fill()
                return self.raws.pop(0)

        def three(out, l_hi, l_lo, r_hi, r_lo, first, final, *marks, last=False):
            mm(out, l_hi, r_hi, first, False, *marks)
            mm(out, l_hi, r_lo, False, False)
            return mm(out, l_lo, r_hi, False, final, last=last)

        def product_T(kt_n, r_hi, r_lo, marks_of):
            bb, k0, out = [banks.take(), banks.take()], 0, [None, None]
            while k0 < kt_n:
                b, width, mh, ml = weights.take()
                kn = width // CW
                for n in range(2):
                    for k in range(kn):
                        c = slice(k * CW + n * P, k * CW + n * P + P)
                        first, final = k0 + k == 0, k0 + k == kt_n - 1
                        m = three(bb[n].ap, b.ap[0][:, c], b.ap[1][:, c], r_hi(k0 + k), r_lo(k0 + k), first, final,
                                  mh, ml, *marks_of(k0 + k), *(bb[n].free if first else ()), last=k == kn - 1)
                    out[n] = m
                b.release(m)
                k0 += kn
            return list(zip(bb, out))

        def inv_root(out, ss, n, eps, *marks):
            m = act(out, ss, ACT.Ln, *marks, scale=1.0 / n, bias=K(eps)[0:out.shape[0]])
            return act(out, out, ACT.Exp, m, scale=-0.5)

        def sigmoid_of(buf, src, *marks):
            return act(buf, src, ACT.Sigmoid, *marks)

        def silu_of(buf, src, *marks):
            return act(buf, src, ACT.Silu, *marks)

        s_pairs = [sem(f"x_pair{i}_loaded") for i in range(KD // 2)]
        for i in range(KD // 2):
            S.steps.append(lambda e, i=i: e.dma_start(x[:, 2 * i:2 * i + 2, :], io["xT"][2 * i * P:(2 * i + 2) * P, :]
                                                      .rearrange("(t p) n -> p t n", p=P)).then_inc(s_pairs[i], 16))
        A.steps.append(lambda e: e.dma_start(param[:, :], io["params"]).then_inc(s_param, 16))
        A.steps.append(lambda e: e.dma_start(tables["common"][:, :], io["common"]).then_inc(s_const, 16))
        A.steps.append(lambda e: e.dma_start(rowp[:, :], io["rows"]).then_inc(s_const, 16))
        for q in (V, A):
            q.wait((s_param, 16))

        class SquareSum:

            def __init__(self, n, stat="ones"):
                self.n, self.k, self.stat = n, 0, stat
                self.acc = temps.take() if n == 1 else sums.take()
                self.sum = self.acc.ap[:, 0:T]

            def add(self, src, *marks):
                self.k += 1
                if self.k == 1:
                    self.mark = act(self.sum, src, ACT.Square, *marks, *self.acc.free)
                    return
                buf = temps.take()
                m = act(buf.ap, src, ACT.Square, *marks, *buf.free)
                self.mark = tt(self.sum, self.sum, buf.ap, ALU.add, m, self.mark, q=G)
                buf.release(self.mark)

            def flush(self):
                assert self.k == self.n
                self.bank = banks.take()
                self.mark = mm(self.bank.ap, K(self.stat), self.sum, True, True, self.mark, *self.bank.free, last=True)
                self.acc.release(self.mark)

        class Normed:

            def __init__(self, gain, at):
                self.gain, self.at, self.stats, self.ready, self.r = gain, at, SquareSum(KD), [], None

            def add(self, d, *marks, h_read=()):
                t = temps.take()
                m = ts(t.ap, x[:, d, :], W(self.gain, self.at + d, self.at + d + 1), None, ALU.mult, None, *marks, *t.free)
                m = split(h_hi[:, d, :], h_lo[:, d, :], t.ap, m, *h_read, qlo=G)
                t.release(*m)
                self.ready.append(m)

            def root(self, dst):
                self.stats.flush()
                self.r, self.r_ready = dst, inv_root(dst, self.stats.bank.ap, D, "rms_eps", self.stats.mark)
                self.stats.bank.release(self.r_ready)

            def scaled(self, out, src, *marks, scale=1.0):
                if scale == 1.0:
                    return tt(out, src, self.r, ALU.mult, self.r_ready, *marks)
                return stt(out, src, scale, self.r, ALU.mult, ALU.mult, self.r_ready, *marks)

        mod = small[:, 0:6 * KD]
        c_act = small[:, 48:56]
        mod_acc = Rotation([None] * 8)
        mod_waiting = []

        def mod_start():
            m = act(c_act, W("c"), ACT.Exp, scale=-1.0)
            m = ts(c_act, c_act, 1.0, None, ALU.add, None, m)
            m = V.do(lambda e: e.reciprocal(c_act, c_act), m)
            return tt(c_act, c_act, W("c"), ALU.mult, m)

        def mod_step(j, ready):
            i, full = weights.raw()
            acc = mod_acc.take()
            m = ts(acc.ap, ring[:, i, 0:CW], c_act[:, 0:1], None, ALU.mult, None, full, ready, *acc.free)
            for k in range(1, KD):
                m = stt(acc.ap, ring[:, i, k * CW:(k + 1) * CW], c_act[:, k:k + 1], acc.ap, ALU.mult, ALU.add, m)
            done_with(i, m)
            mod_waiting.append((j, acc, m))

        def mod_columns():
            if not mod_waiting:
                return
            b = banks.take()
            for at, (j, acc, m) in enumerate(mod_waiting):
                for n in range(2):
                    mark = mm(b.ap[:, 2 * at + n:2 * at + n + 1], acc.ap[:, n * P:(n + 1) * P], K("one"), True, True, m,
                              *b.free, last=True)
                acc.release(mark)
            j0, n = mod_waiting[0][0], len(mod_waiting)
            m = tt(mod[:, 2 * j0:2 * (j0 + n)], b.ap[:, 0:2 * n], W("b_mod", 2 * j0, 2 * (j0 + n)), ALU.add, mark)
            b.release(m)
            mod_waiting.clear()
            mod_marks.append(m)

        def ffn_weights(w_in, w_out, mod=False):
            n_mod = 0
            for j0, j1 in FFN_PARTS:
                for j in range(j0, j1):
                    for w in (w_in[j], w_in[FF // CW + j]):
                        yield "split", w, SLOT
                        if mod:
                            yield "raw", io["w_mod"][n_mod], SLOT
                            n_mod += 1
                for j in range(D // CW):
                    for k0 in range(2 * j0, 2 * j1, KD):
                        k1 = min(k0 + KD, 2 * j1)
                        yield "split", w_out[j, :, k0 * CW:k1 * CW], (k1 - k0) * CW
                    if mod and j % 2 and j1 < FF // CW:
                        yield "raw", io["w_mod"][n_mod], SLOT
                        n_mod += 1

        def ffn(h, r_tile, then, aside=None):
            hk = (lambda k: h_hi[:, k, :]), (lambda k: h_lo[:, k, :]), (lambda k: h.ready[k])
            for j0, j1 in FFN_PARTS:
                hid_ready = []
                for j in range(j0, j1):
                    gate, act_ = product_T(KD, *hk), []
                    if h.r is None:
                        h.root(r_tile)
                    if aside:
                        aside()
                    for b, m in gate:
                        s = temps.take()
                        ms = h.scaled(s.ap, b.ap, m, *s.free)
                        b.release(ms)
                        ms = tt(s.ap, s.ap, h.r, ALU.mult, silu_of(s.ap, s.ap, ms), q=G)
                        act_.append((s, ms))
                    for n, (b, m) in enumerate(product_T(KD, *hk)):
                        s, ms = act_[n]
                        ms = tt(s.ap, b.ap, s.ap, ALU.mult, ms, m)
                        b.release(ms)
                        f = 2 * (j - j0) + n
                        marks = split(hid_hi[:, f, :], hid_lo[:, f, :], s.ap, ms, qlo=G)
                        s.release(*marks)
                        hid_ready.append(marks)
                    if aside:
                        aside()
                if j1 == FF // CW:
                    h_read = PE.last
                for j in range(D // CW):
                    for n, (b, m) in enumerate(product_T(len(hid_ready), lambda k: hid_hi[:, k, :], lambda k: hid_lo[:, k, :],
                                                         lambda k: hid_ready[k])):
                        d = 2 * j + n
                        mx = stt(x[:, d, :], b.ap, 0.5, x[:, d, :], ALU.mult, ALU.add, m)
                        b.release(mx)
                        if j1 == FF // CW:
                            then(d, mx, h_read)
                    if aside and j % 2 and j1 < FF // CW:
                        aside()

        def mixer1(layer, h, r_tile, then):
            q_sb, k_sb, v_sb, q_r, k_r, v_r, g_r, acc = 0, 4, 8, 12, 14, 16, 18, 20
            vpad = arena[:, 22 * T:22 * T + 2 * (PAD + T)].rearrange("p (t n) -> p t n", t=2)
            soft = [arena[:, 25 * T + 1280 * i:25 * T + 1280 * (i + 1)] for i in range(4)]
            m_pad = V.do(lambda e: e.memset(vpad[:, :, 0:PAD], 0.0))

            def proj_T(take):
                for n, (b, m) in enumerate(product_T(KD, lambda k: h_hi[:, k, :], lambda k: h_lo[:, k, :],
                                                     lambda k: h.ready[k])):
                    take(n, b, m)

            def keep(dst, scale=1.0):
                def take(n, b, m):
                    mk = h.scaled(tile(dst + n), b.ap, m, scale=scale)
                    b.release(mk)
                    ready[dst + n] = mk
                return take

            ready = {}
            a_banks = []
            proj_T(lambda n, b, m: a_banks.append((b, m)))
            h.root(r_tile)
            b = banks.take()
            r_col = small[:, 96:96 + NT]
            for t in range(NT):
                m = mm(b.ap[:, t:t + 1], h.stats.sum[:, t * P:(t + 1) * P], K("one"), True, True, *b.free, last=True)
            h.stats.acc.release(m)
            r_col_ready = inv_root(r_col, b.ap[:, 0:NT], D, "rms_eps", m)
            b.release(r_col_ready)

            def conv_gate(n, b, m):
                s = temps.take()
                ms = h.scaled(s.ap, b.ap, m, *s.free)
                b.release(ms)
                ms = sigmoid_of(s.ap, s.ap, ms)
                ab, ma = a_banks[n]
                mv = h.scaled(vpad[:, n, PAD:PAD + T], ab.ap, ma, m_pad)
                ab.release(mv)
                mv = tt(vpad[:, n, PAD:PAD + T], vpad[:, n, PAD:PAD + T], s.ap, ALU.mult, mv, ms)
                s.release(mv)
                ready["v", n] = mv
            proj_T(conv_gate)
            for j in range(2):
                proj_T(keep(q_sb + 2 * j, scale=HEAD ** -0.5))
            for j in range(2):
                proj_T(keep(k_sb + 2 * j))
            vb_ = [banks.take() for _ in range(NT)]
            k0 = 0
            while k0 < KD:
                w, width, mh, ml = weights.take()
                kn = width // T
                for t in range(NT):
                    for k in range(kn):
                        tok = slice(t * P, (t + 1) * P)
                        c = slice(k * T, (k + 1) * T)
                        m = three(vb_[t].ap, h_hi[:, k0 + k, tok], h_lo[:, k0 + k, tok], w.ap[0][:, c], w.ap[1][:, c],
                                  k0 + k == 0, k0 + k == KD - 1, mh, ml, *vb_[t].free, last=k == kn - 1)
                w.release(m)
                k0 += kn
            for t in range(NT):
                mk = ts(tile(v_sb + t), vb_[t].ap, r_col[:, t:t + 1], None, ALU.mult, None, m, r_col_ready)
                vb_[t].release(mk)
                ready["v_sb", t] = mk
            for q in (V, PE):
                q.wait((s_tables, loaded[0]))

            def rotate(dst):
                def take(n, b, m):
                    plain = temps.take()
                    mp = h.scaled(plain.ap, b.ap, m, *plain.free)
                    b.release(mp)
                    sw = banks.take()
                    ms = mm(sw.ap, K("swap64"), plain.ap, True, True, mp, *sw.free, last=True)
                    m1 = tt(tile(dst + n), plain.ap, K("cos64"), ALU.mult, mp)
                    turned = temps.take()
                    m2 = tt(turned.ap, sw.ap, K("sin64"), ALU.mult, ms, *turned.free)
                    sw.release(m2)
                    plain.release(m1, ms)
                    m3 = tt(tile(dst + n), tile(dst + n), turned.ap, ALU.add, m1, m2)
                    turned.release(m3)
                    ready[dst + n] = m3
                return take
            proj_T(rotate(q_r))
            proj_T(rotate(k_r))

            part = {0: (0, 0, 0), 1: (512, 1, 0), 3: (896, 1, 384), 2: (1024, 2, 0)}
            order = (0, 1, 3, 2)
            spans = ((0, 512), (512, 1024), (1024, 1280))
            exps, softs, wts_ = Rotation(soft[0:1]), Rotation(soft[1:3]), Rotation(soft[3:4])

            def head_rows(i):
                return slice(HEAD * (i % 2), HEAD * (i % 2) + HEAD)

            def before_only(buf, queue_after):
                marks = []
                for kt in order:
                    blk = buf[:, part[kt][0]:part[kt][0] + P]
                    marks.append(G.do(lambda e, blk=blk: e.affine_select(
                        out=blk, in_=blk, compare_op=ALU.is_gt, fill=0.0, base=0, pattern=[[1, P]],
                        channel_multiplier=-1), queue_after))
                return marks[-1]

            def sb_scores(i):
                rows = head_rows(i)
                q, k = tile(q_sb + i // 2), tile(k_sb + i // 2)
                bb = [banks.take() for _ in range(3)]
                for kt in order:
                    _, bi, c = part[kt]
                    n = T - kt * P
                    m = mm(bb[bi].ap[:, c:c + n], k[rows, kt * P:(kt + 1) * P], q[rows, kt * P:T],
                           c == 0, True, *bb[bi].free, ready[q_sb + i // 2], ready[k_sb + i // 2],
                           last=True, loose=True)
                e, sp = exps.take(), softs.take()
                for bi, (a, b) in enumerate(spans):
                    me = act(e.ap[:, a:b], bb[bi].ap[:, 0:b - a], ACT.Abs, m, *e.free)
                me = act(e.ap, e.ap, ACT.Exp, me, scale=-1.0)
                me = act(e.ap, e.ap, ACT.Ln, me, bias=K("one"))
                for bi, (a, b) in enumerate(spans):
                    ms = stt(sp.ap[:, a:b], bb[bi].ap[:, 0:b - a], 0.0, e.ap[:, a:b], ALU.max, ALU.add, me, *sp.free)
                e.release(ms)
                return bb, sp, before_only(sp.ap, ms), ms

            plain_v = []

            def keep_plain(n, b, m):
                t = temps.take()
                mk = h.scaled(t.ap, b.ap, m, *t.free)
                b.release(mk)
                plain_v.append((t, mk))
            scores0 = sb_scores(0)
            proj_T(keep_plain)
            proj_T(keep(g_r))
            for half in range(2):
                b = banks.take()
                for tl in range(2):
                    for n, (s_, mk) in enumerate(plain_v):
                        t = 2 * half + tl
                        m = PE.do(lambda e, o=b.ap[:, tl * CW + n * P:tl * CW + (n + 1) * P], i_=s_.ap[:, t * P:(t + 1) * P]:
                                  e.transpose(o, i_, K("ident")), mk, *b.free)
                mk2 = copy(tile(v_r + half), b.ap, m, q=A)
                b.release(mk2)
                ready["v_r", 2 * half] = ready["v_r", 2 * half + 1] = mk2
            for s_, _ in plain_v:
                s_.release(m)
            projected = PE.last

            def conv_taps():
                for tap in range(CONV_TAPS):
                    for n in range(2):
                        at = (layer * 2 + n) * CONV_TAPS + tap
                        w = W("conv_w", at, at + 1)
                        src = vpad[:, n, tap:tap + T]
                        if tap == 0:
                            b0 = W("conv_b", layer * 2 + n, layer * 2 + n + 1)
                            ready["conv", n] = ts(tile(acc + n), src, w, b0, ALU.mult, ALU.add, m_pad, ready["v", n])
                        else:
                            ready["conv", n] = stt(tile(acc + n), src, w, tile(acc + n), ALU.mult, ALU.add,
                                                   ready["conv", n])
                        yield
            conv = conv_taps()

            def conv_some(n):
                for _ in range(n):
                    next(conv, None)

            def sb_mix(i, bb, sp, sp_ready, z_read):
                rows = head_rows(i)
                w = wts_.take()
                for kt in order:
                    _, bi, c = part[kt]
                    for kj in range(kt, NT):
                        off, n = part[kj][0], T - kj * P
                        dst = c + (kj - kt) * P
                        m = mm(bb[bi].ap[:, dst:dst + n], K("neg_suffix" if kj == kt else "neg_ones"),
                               sp.ap[:, off:off + n], False, True, sp_ready, z_read, last=kj == NT - 1, loose=True)
                    if kt == 0:
                        m_first = m
                sp.release(m)
                for bi, (a, b) in enumerate(spans):
                    mw = act(w.ap[:, a:b], bb[bi].ap[:, 0:b - a], ACT.Exp, m_first if bi == 0 else m, *w.free)
                    bb[bi].release(mw)
                return w, before_only(w.ap, mw)

            def sb_out(i, w, mw):
                rows = head_rows(i)
                o = banks.take()
                for kt in range(NT):
                    off, n = part[kt][0], T - kt * P
                    m = mm(o.ap[rows, kt * P:T], tile(v_sb + kt)[:, i * HEAD:(i + 1) * HEAD], w.ap[:, off:off + n],
                           kt == 0, kt == NT - 1, mw, ready["v_sb", kt], *o.free, last=True)
                w.release(m)
                mo = split(h_hi[rows, 2 + i // 2, :], h_lo[rows, 2 + i // 2, :], o.ap[rows, :], m, projected)
                o.release(*mo)
                ready["y", 2 + i // 2, i % 2] = mo

            nxt, mixed = scores0, None
            for i in range(SB_HEADS):
                cur = nxt
                if i + 1 < SB_HEADS:
                    nxt = sb_scores(i + 1)
                conv_some(8)
                if mixed:
                    sb_out(*mixed)
                mixed = (i, *sb_mix(i, *cur))

            def ret_scores(i):
                rows = head_rows(i)
                out, s = [], softs.take()
                for kt in range(NT):
                    n = T - kt * P
                    b, c = banks.take(), part[kt][0]
                    m = mm(b.ap[:, 0:n], tile(k_r + i // 2)[rows, kt * P:(kt + 1) * P],
                           tile(q_r + i // 2)[rows, kt * P:T], True, True, *b.free, ready[q_r + i // 2],
                           ready[k_r + i // 2], last=True)
                    ms = tt(s.ap[:, c:c + n], b.ap[:, 0:n], K(f"decay{i}", 0, n), ALU.mult, m, *s.free)
                    b.release(ms)
                    out.append(ms)
                return s, out

            def ret_mix(i, s, scored):
                rows = head_rows(i)
                o = banks.take()
                for kt, ms in enumerate(scored):
                    n, c = T - kt * P, part[kt][0]
                    m = mm(o.ap[rows, kt * P:T], arena[:, v_r * T + kt * CW + i * HEAD:v_r * T + kt * CW + (i + 1) * HEAD],
                           s.ap[:, c:c + n], kt == 0, kt == NT - 1, ms, ready["v_r", kt], *o.free, last=True)
                s.release(m)
                y = tile(q_sb + i // 2)
                mo = copy(y[rows, :], o.ap[rows, :], m, PE.last, q=A)
                o.release(mo)
                ready["ret", i] = mo

            def conv_centre():
                mean = banks.take()
                for n in range(2):
                    m = mm(mean.ap, K("ones"), tile(acc + n), n == 0, n == 1, ready["conv", n], *mean.free, last=True)
                for n in range(2):
                    m1 = act(tile(k_sb + n), mean.ap, ACT.Copy, m, scale=-1.0 / 256)
                    m2 = tt(tile(acc + n), tile(acc + n), tile(k_sb + n), ALU.add, m1)
                    ready["conv", n] = m2
                    var.add(tile(acc + n), m2)
                mean.release(m1)

            def conv_finish():
                var.flush()
                r = temps.take()
                mr = inv_root(r.ap, var.bank.ap, 256, "rms_eps", var.mark, *r.free)
                var.bank.release(mr)
                for n in range(2):
                    at = layer * 2 + n
                    m = stt(tile(acc + n), tile(acc + n), W("conv_ln_g", at, at + 1), r.ap, ALU.mult, ALU.mult, mr,
                            ready["conv", n])
                    m = ts(tile(acc + n), tile(acc + n), W("conv_ln_b", at, at + 1), None, ALU.add, None, m)
                    m = silu_of(tile(acc + n), tile(acc + n), m)
                    ready["y", n, 0] = ready["y", n, 1] = split(h_hi[:, n, :], h_lo[:, n, :], tile(acc + n), m, projected, qlo=G)
                r.release(m)

            def ret_centre(n):
                b = banks.take()
                m = mm(b.ap, K("centre64"), tile(q_sb + n), True, True, ready["ret", 2 * n], ready["ret", 2 * n + 1],
                       *b.free, last=True)
                sv = SquareSum(1, "sum64")
                sv.add(b.ap, m)
                return b, sv

            var = SquareSum(2)
            nxt = ret_scores(0)
            sb_out(*mixed)
            conv_some(2 * CONV_TAPS)
            for i in range(RET_HEADS):
                cur = nxt
                if i + 1 < RET_HEADS:
                    nxt = ret_scores(i + 1)
                if i == 0:
                    conv_centre()
                ret_mix(i, *cur)
                if i == 2:
                    first_pair = ret_centre(0)
                    conv_finish()
            pairs = [first_pair, ret_centre(1)]
            for n, (b, sv) in enumerate(pairs):
                sv.flush()
                r = temps.take()
                mr = inv_root(r.ap, sv.bank.ap, HEAD, "rms_eps", sv.mark, *r.free)
                sv.bank.release(mr)
                s = temps.take()
                ms = silu_of(s.ap, tile(g_r + n), ready[g_r + n], *s.free)
                m = tt(r.ap, b.ap, r.ap, ALU.mult, mr)
                b.release(m)
                at = layer * 2 + n
                m = stt(r.ap, r.ap, W("ret_norm_g", at, at + 1), s.ap, ALU.mult, ALU.mult, m, ms)
                s.release(m)
                mo = split(h_hi[:, 6 + n, :], h_lo[:, 6 + n, :], r.ap, m, projected, qlo=(V, G)[n])
                r.release(*mo)
                ready["y", 6 + n, 0] = ready["y", 6 + n, 1] = mo
            out_project([(*ready["y", n, 0], *ready["y", n, 1]) for n in range(KD)],
                        lambda d, b, m: residual(d, b, m, then))

        def residual(d, b, m, then):
            mx = tt(x[:, d, :], b.ap, x[:, d, :], ALU.add, m)
            b.release(mx)
            then(d, mx)

        def out_project(y_ready, take):
            for j in range(D // CW):
                for n, (b, m) in enumerate(product_T(KD, lambda k: h_hi[:, k, :], lambda k: h_lo[:, k, :],
                                                     lambda k: y_ready[k])):
                    take(2 * j + n, b, m)

        def mixer2(h_ready):
            qf, kf, v_nat = 0, 8, 16
            gpad = arena[:, 20 * T:20 * T + 6 * (GDN_TAPS - 1 + T)].rearrange("p (t n) -> p t n", t=6)
            z_t = 27
            PP = POOL_PAD
            ppad = arena[:, 29 * T:29 * T + 2 * (PP + T)].rearrange("p (t n) -> p t n", t=2)
            cq, ckv = 32, 34
            prob = Rotation([arena[:, 32 * T + 1280 * i:32 * T + 1280 * (i + 1)] for i in range(2)])
            flip = Rotation([arena[:, 37 * T:37 * T + 1280]])
            ab = small[:, 64:96].rearrange("p (t n) -> p t n", t=NT)
            ready = {}
            m_pads = (V.do(lambda e: e.memset(gpad[:, :, 0:GDN_TAPS - 1], 0.0)),
                      V.do(lambda e: e.memset(ppad[:, :, 0:PP], 0.0)))

            def proj(*takes):
                for n, (b, m) in enumerate(product_T(KD, lambda k: h_hi[:, k, :], lambda k: h_lo[:, k, :],
                                                     lambda k: h_ready[k])):
                    takes[n](n, b, m)

            def keep(dst, name, q=A):
                def take(n, b, m):
                    mk = copy(dst(n), b.ap, m, *m_pads, q=q)
                    b.release(mk)
                    ready[name, n] = mk
                return take

            take_cq = keep(lambda n: tile(cq + n), "cq")
            proj(take_cq, take_cq)
            kr = Buffer(tile(37))

            def keep_kr(n, b, m):
                mk = copy(kr.ap[NOPE:P, :], b.ap[NOPE:P, :], m, q=A)
                b.release(mk)
                ready["kr"] = mk
            proj(keep(lambda n: tile(ckv), "ckv"), keep_kr)
            b = banks.take()
            for t in range(NT):
                m = PE.do(lambda e, o=b.ap[:, 8 * t:8 * t + 8], i_=kr.ap[QK:QK + 8, t * P:(t + 1) * P]:
                          e.transpose(o, i_, K("ident")[QK:QK + 8, QK:QK + 8]), ready["kr"], *b.free)
            mk = copy(ab, b.ap[:, 0:32].rearrange("p (t n) -> p t n", t=NT), m)
            b.release(mk)
            ready["ab"] = mk
            for g in range(3):
                take_g = keep(lambda n, g=g: gpad[:, 2 * g + n, GDN_TAPS - 1:], ("g", g), q=(A, V)[g % 2])
                proj(take_g, take_g)
            take_z = keep(lambda n: tile(z_t + n), "z")
            proj(take_z, take_z)
            take_p = keep(lambda n: ppad[:, n, PP:], "p", q=V)
            proj(take_p, take_p)
            projected = PE.last
            for q in (V, PE, G):
                q.wait((s_tables, loaded[0]))

            def latent_norm(tiles, names, gain):
                s = SquareSum(len(tiles))
                for t, nm in zip(tiles, names):
                    s.add(tile(t), ready[nm])
                s.flush()
                r = temps.take()
                m = inv_root(r.ap, s.bank.ap, P * len(tiles), "rms_eps", s.mark, *r.free)
                s.bank.release(m)
                for n, t in enumerate(tiles):
                    mk = stt(tile(t), tile(t), W(gain, n, n + 1), r.ap, ALU.mult, ALU.mult, m)
                r.release(mk)
                return mk
            ckv_ready = latent_norm([ckv], [("ckv", 0)], "kv_norm")
            cq_ready = latent_norm([cq, cq + 1], [("cq", 0), ("cq", 1)], "q_norm")

            def rotate(rows_ap, mp, *marks):
                sw = banks.take()
                r = slice(NOPE, QK)
                ms = mm(sw.ap[r, :], K("swap32")[r, NOPE:QK], rows_ap, True, True, mp, *sw.free, last=True)
                s = temps.take()
                m2 = tt(s.ap[r, :], sw.ap[r, :], K("sin32")[r, :], ALU.mult, ms, *s.free)
                sw.release(m2)
                m1 = tt(rows_ap, rows_ap, K("cos32")[r, :], ALU.mult, mp, ms)
                m3 = tt(rows_ap, rows_ap, s.ap[r, :], ALU.add, m1, m2)
                s.release(m3)
                return m3
            ready["kr"] = rotate(kr.ap[NOPE:QK, :], ready["kr"])

            i, full = weights.raw()
            for hd in range(MLA_HEADS):
                b = banks.take()
                m = mm(b.ap[0:NOPE, :], ring[:, i, hd * P:hd * P + NOPE], tile(ckv), True, True, full, ckv_ready,
                       *b.free, last=True)
                mk = copy(tile(kf + hd)[0:NOPE, :], b.ap[0:NOPE, :], m, q=A)
                b.release(mk)
                m2 = copy(tile(kf + hd)[NOPE:QK, :], kr.ap[NOPE:QK, :], ready["kr"], q=G)
                ready["k", hd] = (mk, m2)
            for t in range(NT):
                b = banks.take()
                vcols = ring[:, i, 0:MLA_HEADS * P].rearrange("p (h c) -> p h c", c=P)[:, :, NOPE:P]
                m = mm(b.ap, tile(ckv)[:, t * P:(t + 1) * P], vcols, True, True, *b.free, last=True)
                mk = copy(tile(v_nat + t), b.ap, m, q=V)
                b.release(mk)
                ready["v", t] = mk
            done_with(i, m)
            i, full = weights.raw()
            for hd in range(MLA_HEADS):
                b = banks.take()
                for k in range(2):
                    c0 = k * MLA_HEADS * QK + hd * QK
                    m = mm(b.ap[0:QK, :], ring[:, i, c0:c0 + QK], tile(cq + k), k == 0, k == 1, full, cq_ready,
                           *b.free, last=True)
                mk = copy(tile(qf + hd)[0:QK, :], b.ap[0:QK, :], m, q=A)
                b.release(mk)
                ready["q", hd] = rotate(tile(qf + hd)[NOPE:QK, :], mk)
            done_with(i, m)

            for b in (*prob.buffers, *flip.buffers):
                b.free = (PE.last, ready["k", MLA_HEADS - 1][1])

            scale = QK ** -0.5
            mx, neg, rs = small[:, 96:128], small[:, 128:160], small[:, 160:192]

            def mla_scores(hd):
                out, whole, cs = [], prob.take(), slice(hd * NT, (hd + 1) * NT)
                for t in range(NT):
                    n = (t + 1) * P
                    c = hd * NT + t
                    b = banks.take()
                    a0 = sum((u + 1) * P for u in range(t))
                    p = whole.ap[:, a0:a0 + n]
                    m = mm(b.ap[:, 0:n], tile(qf + hd)[0:QK, t * P:n], tile(kf + hd)[0:QK, 0:n], True, True,
                           *b.free, ready["q", hd], *ready["k", hd], last=True)
                    m = V.do(lambda e, b=b, n=n: e.memset(b.ap[0:CHUNK, n - CHUNK:n], -BIG), m)
                    m = V.do(lambda e, b=b, n=n, c=c: e.tensor_reduce(mx[:, c:c + 1], b.ap[:, 0:n], AXX, ALU.max), m)
                    out.append((b, p, n, c))
                m = ts(neg[:, cs], mx[:, cs], -scale, None, ALU.mult, None, m)
                for b, p, n, c in out:
                    me = act(p, b.ap[:, 0:n], ACT.Exp, m, *whole.free, scale=scale, bias=neg[:, c:c + 1],
                             accum=rs[:, c:c + 1])
                    b.release(me)
                return whole, [p for _, p, _, _ in out], cs, me

            def mla_divide(whole, ps, cs, m):
                m = V.do(lambda e: e.reciprocal(rs[:, cs], rs[:, cs]), m)
                return whole, [(p, ts(p, p, rs[:, cs.start + t:cs.start + t + 1], None, ALU.mult, None, m))
                               for t, p in enumerate(ps)]

            part = {0: (0, 0, 0), 1: (512, 1, 0), 3: (896, 1, 384), 2: (1024, 2, 0)}
            spans = ((0, 512), (512, 1024), (1024, 1280))

            def mla_turn(whole, probs):
                bb, f = [banks.take() for _ in range(3)], flip.take()
                for t, (p, mp) in enumerate(probs):
                    for kt in range(t + 1):
                        _, bi, c = part[kt]
                        c += (t - kt) * P
                        m = PE.do(lambda e, o=bb[bi].ap[:, c:c + P], s=p[:, kt * P:(kt + 1) * P]:
                                  e.transpose(o, s, K("ident")), mp, *bb[bi].free)
                whole.release(m)
                for bi, (a, b) in enumerate(spans):
                    mf = copy(f.ap[:, a:b], bb[bi].ap[:, 0:b - a], m, *f.free, q=V if bi == 0 else A)
                    bb[bi].release(mf)
                    if bi == 0:
                        mf0 = mf
                return f, mf0, mf

            def mla_out(hd, f, mf0, mf):
                rows = slice(HEAD * (hd % 2), HEAD * (hd % 2) + HEAD)
                o = banks.take()
                for kt in range(NT):
                    off, n = part[kt][0], T - kt * P
                    m = mm(o.ap[rows, kt * P:T], tile(v_nat + kt)[:, hd * HEAD:(hd + 1) * HEAD], f.ap[:, off:off + n],
                           kt == 0, kt == NT - 1, mf0, mf, ready["v", kt], *o.free, last=True)
                f.release(m)
                mo = split(h_hi[rows, hd // 2, :], h_lo[rows, hd // 2, :], o.ap[rows, :], m, projected)
                o.release(*mo)
                ready["y", hd // 2, hd % 2] = mo

            lo, hi = slice(0, 64), slice(64, 128)

            def pool(g):
                src, m = ppad[:, g, :], ready["p", g]
                todo = [lo, hi]
                b = [sums.take(), sums.take()]
                rows = slice(0, P)
                for lvl in range(4):
                    sh, w = 2 ** lvl, 2 ** (lvl + 1)
                    dst = b[lvl % 2].ap
                    m = tt(dst[rows, w - 1:], src[rows, w - 1:], src[rows, w - 1 - sh:PP + T - sh], ALU.add, m, *m_pads,
                           *b[lvl % 2].free)
                    src = dst
                    if w in POOL_WINDOWS[2 * g:2 * g + 2]:
                        r_ = todo.pop(0)
                        m = tt(dst[r_, PP:], dst[r_, PP:], K(f"inv_count{g}")[r_, :], ALU.mult, m)
                        m = tt(ppad[r_, g, PP:], dst[r_, PP:], ppad[r_, g, PP:], ALU.subtract, m)
                        rows = todo[0] if todo else rows
                        if not todo:
                            break
                    yield
                yield
                for r_, u in ((lo, b[0]), (hi, b[1])):
                    o = banks.take()
                    mw = mm(o.ap[r_, :], W("pool_w", g * 64, g * 64 + 64)[r_, :], ppad[r_, g, PP:], True, True, m, *o.free,
                            last=True)
                    t = u.ap[r_, 0:T]
                    mk = ts(t, o.ap[r_, :], W("pool_scale", g, g + 1)[r_, :], None, ALU.mult, None, mw)
                    o.release(mk)
                    mo = split(h_hi[r_, 6 + g, :], h_lo[r_, 6 + g, :], t, mk, projected)
                    u.release(*mo)
                    ready["y", 6 + g, 0 if r_ is lo else 1] = mo

            def qkv_T(n):
                return gpad[:, n, GDN_TAPS - 1:]
            qT, kT = (lambda f: qkv_T(f)), (lambda f: qkv_T(2 + f))
            unit = {}

            def gdn_input(n):
                acc = sums.take()
                a_ = acc.ap[:, 0:T]
                m = ready[("g", n // 2), n % 2]
                for tap in range(GDN_TAPS):
                    w = W("gdn_conv", n * GDN_TAPS + tap, n * GDN_TAPS + tap + 1)
                    src = gpad[:, n, tap:tap + T]
                    if tap == 0:
                        m = ts(a_, src, w, None, ALU.mult, None, m, *acc.free)
                    else:
                        m = stt(a_, src, w, a_, ALU.mult, ALU.add, m)
                m = silu_of(qkv_T(n), a_, m)
                acc.release(m)
                unit[n] = m
                yield
                if n >= 4:
                    return
                s = temps.take()
                m = act(s.ap, qkv_T(n), ACT.Square, m, *s.free)
                yield
                b = banks.take()
                m = mm(b.ap, K("sum64"), s.ap, True, True, m, *b.free, last=True)
                m = inv_root(s.ap, b.ap, 1.0, "rms_eps", m)
                b.release(m)
                yield
                unit[n] = stt(qkv_T(n), qkv_T(n), HEAD ** -0.5 if n < 2 else 1.0, s.ap, ALU.mult, ALU.mult, m)
                s.release(unit[n])

            AT, QKT, TT, UU, XX, BT = 0, 4, 12, 16, 32, 36
            eB, kb = (10, 11), (8, 9)

            def decay(hd):
                rows, f = slice(HEAD * (hd % 2), HEAD * (hd % 2) + HEAD), hd // 2
                spread = []
                for col in (g_c, beta_c):
                    s = temps.take()
                    m = G.do(lambda e, s=s, col=col: e.tensor_copy(
                        s.ap.rearrange("p (t n) -> p t n", t=NT),
                        col.rearrange("p (t n) -> p t n", t=NT)[:, :, hd:hd + 1].to_broadcast([P, NT, P])), *s.free, m1, m2)
                    spread.append((s, m))
                yield
                scores_read = PE.last
                for n, mat in enumerate(("incl", "ident")):
                    (s, m), bank = spread[n], banks.take()
                    for t in range(NT):
                        m = mm(bank.ap[:, t * P:(t + 1) * P], s.ap[:, t * P:(t + 1) * P], K(mat), True, True, m,
                               *bank.free, last=True)
                    s.release(m)
                    spread[n] = bank, m
                (gb, m_gb), (bbk, m_bb) = spread
                me = act(tile(eB[f])[rows, :], gb.ap[rows, :], ACT.Exp, m_gb, scores_read)
                ready["e", hd] = me
                m_kb = tt(tile(kb[f])[rows, :], kT(f)[rows, :], bbk.ap[rows, :], ALU.mult, m_bb, unit[2 + f], scores_read)
                bbk.release(m_kb)
                dT = temps.take()
                for t in range(NT):
                    c = 4 * t + hd
                    m = ts(dT.ap[:, t * P:(t + 1) * P], gb.ap[:, t * P:(t + 1) * P], gc_c[:, c:c + 1], 0.0,
                           ALU.subtract, ALU.min, m_gb, me, *dT.free, *gates2)
                gb.release(m, me)
                m = act(dT.ap, dT.ap, ACT.Exp, m)
                yield
                scores_read = PE.last
                ab_, qb_ = banks.take(), banks.take()
                for bank, rhs in ((ab_, tile(kb[f])), (qb_, qT(f))):
                    for t in range(NT):
                        sl = slice(t * P, (t + 1) * P)
                        mk = mm(bank.ap[:, sl], kT(f)[rows, sl], rhs[rows, sl], True, True, m_kb, unit[f], unit[2 + f],
                                *bank.free, last=True)
                for bank, dst, mask in ((ab_, AT + hd, "strict"), (qb_, QKT + hd, "incl")):
                    m3 = tt(tile(dst), bank.ap, dT.ap, ALU.mult, mk, m, scores_read)
                    bank.release(m3)
                    ready[dst] = masked(tile(dst), tile(dst), mask, m3)
                dT.release(m3)

            def masked(out, src, name, *marks):
                return tt(out.rearrange("p (t n) -> p t n", t=NT), src.rearrange("p (t n) -> p t n", t=NT),
                          K(name).unsqueeze(1).to_broadcast([P, NT, P]), ALU.mult, *marks, q=G)

            def cols(a):
                return small[:, a:a + 16]
            g_c, beta_c, t_c, gc_c, be_c, kd_c, dt_c = (cols(a) for a in (192, 208, 224, 240, 256, 272, 288))
            bc = small[:, 304:312]
            b = banks.take()
            m = mm(b.ap[:, 0:8], K("ones")[0:1, :], rowp[0:1, 0:8], True, True, *b.free, last=True)
            m = copy(bc, b.ap[:, 0:8], m)
            b.release(m)
            m_exp = act(bc[:, 4:8], bc[:, 4:8], ACT.Exp, m)
            for t in range(NT):
                m = tt(dt_c[:, 4 * t:4 * t + 4], ab[:, t, 0:4], bc[:, 0:4], ALU.add, m)
            m1 = act(t_c, dt_c, ACT.Abs, m)
            m1 = act(t_c, t_c, ACT.Exp, m1, scale=-1.0)
            m1 = act(t_c, t_c, ACT.Ln, m1, bias=K("one"))
            m1 = stt(t_c, dt_c, 0.0, t_c, ALU.max, ALU.add, m1)
            for t in range(NT):
                m1 = stt(g_c[:, 4 * t:4 * t + 4], t_c[:, 4 * t:4 * t + 4], -1.0, bc[:, 4:8], ALU.mult, ALU.mult, m1, m_exp)
            m2 = act(beta_c.rearrange("p (t n) -> p t n", t=NT), ab[:, :, 4:8], ACT.Exp, ready["ab"], scale=-1.0)
            m2 = ts(beta_c, beta_c, 1.0, None, ALU.add, None, m2)
            m2 = V.do(lambda e: e.reciprocal(beta_c, beta_c), m2)
            b = banks.take()
            m = mm(b.ap[:, 0:16], K("incl"), g_c, True, True, m1, *b.free, last=True)
            mB = mm(b.ap[:, 16:32], K("later"), g_c, True, True, last=True)
            m = copy(gc_c, b.ap[:, 0:16], mB)
            me = act(be_c, b.ap[:, 0:16], ACT.Exp, mB, m)
            me2 = act(kd_c, b.ap[:, 16:32], ACT.Exp, mB, m)
            b.release(m, me2)
            gates = tt(be_c, be_c, beta_c, ALU.mult, me, m2)
            gates2 = (m, me2, gates)


            inputs = {n: gdn_input(n) for n in range(6)}
            decays = {n: decay(n) for n in range(GDN_HEADS)}
            pools = (None for g in range(2) for _ in pool(g))

            def step(which, *numbers):
                for n in numbers:
                    if n in which:
                        next(which[n], None)

            def beside(hd):
                if hd == 0:
                    step(inputs, 0, 2)
                elif hd == 1:
                    step(inputs, 0, 2)
                    step(inputs, 0, 2)
                    step(inputs, 1, 3)
                    step(inputs, 0, 2)
                    step(inputs, 1, 3)
                elif hd == 2:
                    step(inputs, 1, 3)
                    step(inputs, 4, 5)
                    step(inputs, 1, 3)
                step(decays, hd - 4)
                step(decays, hd - 3)
                if hd >= 2:
                    step(decays, hd - 2)

            soft = {hd: mla_divide(*mla_scores(hd)) for hd in range(2)}
            for hd in range(MLA_HEADS):
                turned_ = mla_turn(*soft.pop(hd))
                coming = mla_scores(hd + 2) if hd + 2 < MLA_HEADS else None
                mla_out(hd, *turned_)
                beside(hd)
                if coming:
                    soft[hd + 2] = mla_divide(*coming)
                if hd >= 4:
                    for _ in range(3):
                        next(pools, None)
            for _ in pools:
                pass
            fence()

            knat, vb, kbg, uu, wT, oT = (arena[:, a * T:(a + 2) * T] for a in (29, 40, 8, 0, 2, 12))
            kdc = knat

            def turn_rows(src, dst):
                out = []
                for half in range(2):
                    b = banks.take()
                    for tl in range(2):
                        t = 2 * half + tl
                        for f in range(2):
                            m = PE.do(lambda e, o=b.ap[:, tl * CW + f * P:tl * CW + (f + 1) * P],
                                      s=qkv_T(src + f)[:, t * P:(t + 1) * P]: e.transpose(o, s, K("ident")), *b.free)
                    mk = copy(dst[:, half * T:(half + 1) * T], b.ap, m, q=A)
                    b.release(mk)
                    out.append(mk)
                return out

            def scaled_rows(dst, src, col, *marks):
                v = [a.rearrange("p (c d) -> p c d", d=HEAD) for a in (dst, src)]
                return tt(v[0], v[1], col.unsqueeze(2).to_broadcast([P, NT * GDN_HEADS, HEAD]), ALU.mult, *marks)

            t_ready, u_ready = {}, {}
            for lv in range(6):
                if lv == 1:
                    m_nat = turn_rows(2, knat)
                elif lv == 2:
                    m_kbg = scaled_rows(kbg, knat, be_c, *m_nat)
                    m_nat = turn_rows(4, vb)
                elif lv == 3:
                    m_kd = scaled_rows(kdc, knat, kd_c, m_kbg)
                elif lv == 4:
                    m_vb = scaled_rows(vb, vb, beta_c, *m_nat)
                elif lv == 5:
                    for f in range(2):
                        m_qd = tt(qT(f), qT(f), tile(eB[f]), ALU.mult)
                for hd in range(GDN_HEADS):
                    B_, X_ = tile(BT + hd), tile(XX + hd)
                    T_, U_ = tile(TT + hd), tile(UU + hd)
                    mb = masked(B_, tile(AT + hd), f"level{lv}", ready[AT + hd], *((u_ready[hd], t_ready[hd]) if lv else ()))
                    b = banks.take()
                    for t in range(NT):
                        sl = slice(t * P, (t + 1) * P)
                        m = mm(b.ap[:, sl], B_[:, sl], K("ident") if lv == 0 else T_[:, sl], True, True, mb, *b.free,
                               *((t_ready[hd],) if lv else ()), last=True)
                    if lv == 0:
                        for t in range(NT):
                            sl = slice(t * P, (t + 1) * P)
                            t_ready[hd] = tt(T_[:, sl], K("ident"), b.ap[:, sl], ALU.subtract, m)
                            u_ready[hd] = tt(U_[:, sl], K("ident"), B_[:, sl], ALU.subtract, mb)
                        b.release(t_ready[hd])
                        continue
                    mx_ = copy(X_, b.ap, m, q=A)
                    b.release(mx_)
                    b1, b2 = banks.take(), banks.take()
                    for t in range(NT):
                        sl = slice(t * P, (t + 1) * P)
                        if lv < 5:
                            ma_ = mm(b1.ap[:, sl], U_[:, sl], X_[:, sl], True, True, mx_, u_ready[hd], *b1.free, last=True)
                        mb_ = mm(b2.ap[:, sl], X_[:, sl], U_[:, sl], True, True, mx_, u_ready[hd], *b2.free, last=True)
                    if lv < 5:
                        t_ready[hd] = tt(T_, T_, b1.ap, ALU.subtract, ma_, mb_)
                        b1.release(t_ready[hd])
                    else:
                        b1.release(*b1.free)
                    u_ready[hd] = tt(U_, U_, b2.ap, ALU.subtract, mb_)
                    b2.release(u_ready[hd])

            ub = [banks.take(), banks.take()]
            for c in range(16):
                t, hd = c // 4, c % 4
                m = mm(ub[c // 8].ap[:, c % 8 * HEAD:(c % 8 + 1) * HEAD], tile(UU + hd)[:, t * P:(t + 1) * P],
                       vb[:, c * HEAD:(c + 1) * HEAD], True, True, m_vb, u_ready[hd],
                       *ub[c // 8].free, last=True)
            for i in range(2):
                m_u = copy(uu[:, i * T:(i + 1) * T], ub[i].ap, m)
                ub[i].release(m_u)
            for f in range(2):
                bp = [banks.take(), banks.take()]
                for t in range(NT):
                    for par in range(2):
                        hd, c = 2 * f + par, 4 * t + 2 * f + par
                        rows = slice(HEAD * par, HEAD * par + HEAD)
                        m = mm(bp[par].ap[rows, t * P:(t + 1) * P], kbg[:, c * HEAD:(c + 1) * HEAD],
                               tile(UU + hd)[:, t * P:(t + 1) * P], True, True, m_kbg, *bp[par].free, last=True)
                for par in range(2):
                    rows = slice(HEAD * par, HEAD * par + HEAD)
                    m_w = copy(wT[rows, f * T:(f + 1) * T], bp[par].ap[rows, :], m, q=A)
                    bp[par].release(m_w)

            states = [tile(31)[:, i * 2 * HEAD:(i + 1) * 2 * HEAD] for i in range(2)]
            vns = [tile(42)[:, i * 4 * HEAD:(i + 1) * 4 * HEAD] for i in range(2)]
            m_s = [V.do(lambda e: e.memset(states[0], 0.0))] * 2
            m_vn0 = V.do(lambda e: e.memset(tile(42), 0.0))
            m_vn = m_vn0
            vn_read, state_read = [(), ()], m_vn0
            for ch in range(T // CHUNK):
                t, c0 = ch // 2, CHUNK * (ch % 2)
                vn = vns[ch % 2]
                state, after = states[ch % 2], states[(ch + 1) % 2]
                crow = slice(c0, c0 + CHUNK)
                csl = slice(ch * CHUNK, (ch + 1) * CHUNK)
                vbk = [banks.take(), banks.take()]
                for hd in range(GDN_HEADS):
                    f, par = hd // 2, hd % 2
                    rows = slice(HEAD * par, HEAD * par + HEAD)
                    m = mm(vbk[par].ap[crow, f * HEAD:(f + 1) * HEAD], wT[rows, f * T + ch * CHUNK:f * T + (ch + 1) * CHUNK],
                           state[rows, f * HEAD:(f + 1) * HEAD], True, True, m_w, *m_s, *vbk[par].free, last=True)
                obk = [banks.take(), banks.take()]

                def o_of(hd):
                    f, par = hd // 2, hd % 2
                    return obk[par].ap[HEAD * par:HEAD * par + HEAD, f * HEAD:(f + 1) * HEAD]
                for hd in range(GDN_HEADS):
                    f, par = hd // 2, hd % 2
                    rows = slice(HEAD * par, HEAD * par + HEAD)
                    m_read = mm(o_of(hd), state[rows, f * HEAD:(f + 1) * HEAD],
                                qT(f)[rows, ch * CHUNK:(ch + 1) * CHUNK], f == 0, False, m_qd, *obk[par].free,
                                last=True, loose=True)
                for par in range(2):
                    u_ = uu.rearrange("p (t f q d) -> p t f q d", t=NT, f=2, q=2)[crow, t, :, par, :]
                    o_ = vn.rearrange("p (f q d) -> p f q d", f=2, q=2)[crow, :, par, :]
                    m_vn = tt(o_, u_, vbk[par].ap[crow, 0:2 * HEAD].rearrange("p (f d) -> p f d", f=2), ALU.subtract,
                              m, m_u, m_vn0, *vn_read[ch % 2])
                    vbk[par].release(m_vn)
                sbk = [banks.take(), banks.take()]
                for hd in range(GDN_HEADS):
                    f, par = hd // 2, hd % 2
                    rows = slice(HEAD * par, HEAD * par + HEAD)
                    c = 4 * t + hd
                    m = mm(sbk[par].ap[rows, f * HEAD:(f + 1) * HEAD], kdc[crow, c * HEAD:(c + 1) * HEAD],
                           vn[crow, hd * HEAD:(hd + 1) * HEAD], True, True, m_vn, m_kd, *sbk[par].free, last=True)
                for hd in range(GDN_HEADS):
                    mo = mm(o_of(hd), vn[:, hd * HEAD:(hd + 1) * HEAD], tile(QKT + hd)[:, csl], False, True, m_vn,
                            last=True, loose=True)
                vn_read[ch % 2] = (mo,)
                m_s = []
                for hd in range(GDN_HEADS):
                    f, par = hd // 2, hd % 2
                    rows = slice(HEAD * par, HEAD * par + HEAD)
                    fs = slice(f * HEAD, (f + 1) * HEAD)
                    m_s.append(stt(after[rows, fs], state[rows, fs], tile(eB[f])[rows, (ch + 1) * CHUNK - 1:(ch + 1) * CHUNK],
                                   sbk[par].ap[rows, fs], ALU.mult, ALU.add, m, state_read))
                state_read = m_read
                for par in range(2):
                    sbk[par].release(m_s[-1])
                    rows = slice(HEAD * par, HEAD * par + HEAD)
                    m_o = copy(oT.rearrange("p (f n) -> p f n", f=2)[rows, :, csl],
                               obk[par].ap[rows, 0:2 * HEAD].rearrange("p (f d) -> p f d", f=2), mo, q=A)
                    obk[par].release(m_o)
            for f in range(2):
                s, r = gtemps_late[f]
                o_ = oT[:, f * T:(f + 1) * T]
                m = act(tile(s), o_, ACT.Square, m_o)
                b = banks.take()
                m = mm(b.ap, K("sum64"), tile(s), True, True, m, *b.free, last=True)
                m = inv_root(tile(r), b.ap, HEAD, "rms_eps", m)
                b.release(m)
                m = stt(o_, o_, W("gdn_g"), tile(r), ALU.mult, ALU.mult, m)
                m2 = silu_of(tile(s), tile(z_t + f), m)
                m = tt(o_, o_, tile(s), ALU.mult, m, m2)
                ready["y", 4 + f, 0] = ready["y", 4 + f, 1] = split(h_hi[:, 4 + f, :], h_lo[:, 4 + f, :], o_, m,
                                                                    qlo=(V, G)[f])
            return [(*ready["y", n, 0], *ready["y", n, 1]) for n in range(KD)]
        gtemps_late = ((36, 37), (38, 39))

        class Mean:

            def __init__(self):
                self.bank, self.todo = banks.take(), []

            def add(self, d, m):
                self.todo.append((d, m))
                if len(self.todo) > 1:
                    self.product()

            def product(self):
                d, m = self.todo.pop(0)
                self.mark = mm(self.bank.ap, K("ones"), x[:, d, :], d == 0, d == KD - 1, m, *self.bank.free, last=True)

        def layer_norm(mean, gain, shift):
            while mean.todo:
                mean.product()
            mu = temps.take()
            m = act(mu.ap, mean.bank.ap, ACT.Copy, mean.mark, *mu.free, scale=-1.0 / D)
            mean.bank.release(m)
            var = banks.take()
            for k in range(KD):
                mc_ = tt(x[:, k, :], x[:, k, :], mu.ap, ALU.add, m)
                sq = temps.take()
                ms = act(sq.ap, x[:, k, :], ACT.Square, mc_, *sq.free)
                mv = mm(var.ap, K("ones"), sq.ap, k == 0, k == KD - 1, ms, *var.free, last=True)
                sq.release(mv)
            mu.release(mc_)
            r = temps.take()
            m = inv_root(r.ap, var.ap, D, "ln_eps", mv, *r.free)
            var.release(m)
            out = []
            for k in range(KD):
                m1 = stt(x[:, k, :], x[:, k, :], W(gain, k, k + 1), r.ap, ALU.mult, ALU.mult, m)
                out.append(act(x[:, k, :], x[:, k, :], ACT.Identity, m1, bias=W(shift, k, k + 1)))
            r.release(m1)
            return out

        def modulate(x_ready, which, plain=None):
            sh, sc = which * 3 * KD, which * 3 * KD + KD
            out = []
            for k in range(KD):
                t = Buffer(plain[:, k, :]) if plain is not None else temps.take()
                m = ts(t.ap, x[:, k, :], mod[:, sc + k:sc + k + 1], mod[:, sh + k:sh + k + 1], ALU.mult, ALU.add,
                       x_ready[k], *t.free)
                if plain is None:
                    m = split(h_hi[:, k, :], h_lo[:, k, :], t.ap, m, PE.last, qlo=G)
                    t.release(*m)
                out.append(m)
            return out

        def gated(d, src, which, m, release=None):
            gt = which * 3 * KD + 2 * KD + d
            s = temps.take()
            m = ts(s.ap, src, mod[:, gt:gt + 1], None, ALU.mult, None, m, *s.free)
            if release:
                release(m)
            m = stt(x[:, d, :], x[:, d, :], ALPHA, s.ap, ALU.mult, ALU.add, m)
            s.release(m)
            return m

        def route(h, h_ready, work):
            def area(at_, n, dt=None):
                a = work[:, at_:at_ + NT * n]
                return (a if dt is None else a.bitcast(dt)).rearrange("p (t n) -> p t n", t=NT)
            ids, wts = small[:, 96:104], small[:, 104:112]
            w_ = wts.rearrange("p (t k) -> p t k", t=NT)
            g8, top, e_, idx = area(0, 8), area(32, 8), area(64, 4), area(80, 8, U32)
            gi, gp, d2 = (area(a, 1) for a in (112, 116, 120))
            lg, keep_ = area(128, EXPERTS), area(256, EXPERTS)
            m_pad = V.do(lambda e: e.memset(g8[:, :, GROUPS:8], -BIG))
            N = GROUPS + EXPERTS
            bt = banks.take()
            for k in range(KD):
                m = mm(bt.ap[0:N, :], W("router_w", N * k, N * k + N), h[:, k, :], k == 0, k == KD - 1, h_ready[k], *bt.free,
                       last=True, loose=True)
                if k == 0:
                    for t in range(NT):
                        mm(bt.ap[0:N, t * P:(t + 1) * P], rowp[0:1, 8:8 + N], K("ones")[0:1, :], False, False, loose=True)
            lt = temps.take()
            m = copy(lt.ap[0:N, :], bt.ap[0:N, :], m, *lt.free)
            bt.release(m)
            b = banks.take()
            logits = b.ap[:, 0:NT * N].rearrange("p (t n) -> p t n", t=NT)
            for t in range(NT):
                m2 = PE.do(lambda e, t=t: e.transpose(logits[:, t, :], lt.ap[0:N, t * P:(t + 1) * P], K("ident")[0:N, 0:N]),
                           m, *b.free)
            lt.release(m2)
            m = m2
            yield

            def top8(src, m):
                for t in range(NT):
                    m = V.do(lambda e, t=t: e.max(top[:, t, :], src[:, t, :]), m)
                for t in range(NT):
                    m = V.do(lambda e, t=t: e.max_index(idx[:, t, :], top[:, t, :], src[:, t, :]), m)
                return m
            m1 = copy(g8[:, :, 0:GROUPS], logits[:, :, 0:GROUPS], m, m_pad)
            m1 = top8(g8, m1)
            m2 = tt(e_, g8[:, :, 0:GROUPS], top[:, :, 0:1].to_broadcast([P, NT, GROUPS]), ALU.subtract, m1)
            m2 = act(e_, e_, ACT.Exp, m2)
            m1 = copy(gi, idx[:, :, 0:1], m1)
            m1 = ts(gi, gi, float(PER_GROUP), None, ALU.mult, None, m1)
            m1 = tt(keep_, K("expert_id").unsqueeze(1).to_broadcast([P, NT, EXPERTS]), gi.to_broadcast([P, NT, EXPERTS]),
                    ALU.subtract, m1)
            m1 = ts(lg, keep_, 0.0, None, ALU.is_ge, None, m1)
            m1 = ts(keep_, keep_, float(PER_GROUP), None, ALU.is_lt, None, m1)
            m1 = tt(keep_, keep_, lg, ALU.mult, m1)
            m1 = ts(lg, keep_, 1.0, BIG, ALU.subtract, ALU.mult, m1)
            m1 = tt(keep_, keep_, logits[:, :, GROUPS:36], ALU.mult, m1)
            b.release(m1)
            m1 = tt(lg, lg, keep_, ALU.add, m1)
            m1 = top8(lg, m1)
            m_ids = copy(ids.rearrange("p (t k) -> p t k", t=NT), idx[:, :, 0:2], m1)
            m1 = tt(d2, top[:, :, 1:2], top[:, :, 0:1], ALU.subtract, m1)
            m3 = act(d2, d2, ACT.Exp, m1)
            yield ids, wts, m_ids
            m2 = V.do(lambda e: e.tensor_reduce(gp, e_, AXX, ALU.add), m2)
            m2 = V.do(lambda e: e.reciprocal(gp, gp), m2)
            m1 = ts(w_[:, :, 0:1], d2, 1.0, None, ALU.add, None, m3)
            m1 = V.do(lambda e: e.reciprocal(w_[:, :, 0:1], w_[:, :, 0:1]), m1)
            m1 = tt(w_[:, :, 0:1], w_[:, :, 0:1], gp, ALU.mult, m1, m2)
            tt(w_[:, :, 1:2], w_[:, :, 0:1], d2, ALU.mult, m1)
            yield

        def moe(h, h_ready):
            def at(first, n):
                return arena[:, first * T:first * T + n]

            s_rows = sem("h_rows")
            start = [q.last for q in (V, A, PE, G)]
            routing = route(h, h_ready, at(27, T))
            next(routing)
            rows_buf = [at(0, D), at(2, D), at(4, D), at(6, D)]
            for t in range(NT):
                for half in range(2):
                    b = banks.take()
                    for k in range(4):
                        d = 4 * half + k
                        m = PE.do(lambda e, o=b.ap[:, k * P:(k + 1) * P], i_=h[:, d, t * P:(t + 1) * P]:
                                  e.transpose(o, i_, K("ident")), h_ready[d], *b.free)
                    m = copy(rows_buf[t][:, half * T:(half + 1) * T], b.ap, m, q=A)
                    b.release(m)
                    if half == 0:
                        m0 = m
                S.wait(m0, m)
                S.steps.append(lambda e, t=t: e.dma_start(io["h_rows"][t * P:(t + 1) * P, :], rows_buf[t]).then_inc(s_rows, 16))

            for q in (V, PE):
                q.wait((s_tables, loaded[0]))
            ids, wts, m_route = next(routing)

            picks = at(8, 2 * NT * EXPERTS)
            both = at(9, NT * EXPERTS)
            prod = at(10, 2 * NT * EXPERTS)
            run, total = at(11, EXPERTS), arena[:, 11 * T + 64:11 * T + 64 + EXPERTS]
            first = arena[:, 11 * T + 128:11 * T + 128 + EXPERTS]
            picks_ = picks.rearrange("p (c n) -> p c n", n=EXPERTS)
            picks4 = picks.rearrange("p (t k n) -> p t k n", t=NT, k=2)
            both_ = both.rearrange("p (t n) -> p t n", n=EXPERTS)
            m = tt(picks_, K("expert_id").unsqueeze(1).to_broadcast([P, 2 * NT, EXPERTS]),
                   ids.unsqueeze(2).to_broadcast([P, 2 * NT, EXPERTS]), ALU.is_equal, m_route)
            m = tt(both_, picks4[:, :, 0, :], picks4[:, :, 1, :], ALU.add, m)
            rank, count = banks.take(), banks.take()
            W_ = NT * EXPERTS
            mc = mm(count.ap[:, 0:W_], K("ones"), both, True, True, m, *count.free, last=True)
            mr = mm(rank.ap[:, 0:W_], K("before"), both, True, True, *rank.free, last=True)
            base = arena[:, 16 * T:16 * T + (NT + 1) * EXPERTS].rearrange("p (t n) -> p t n", n=EXPERTS)
            for t in range(NT):
                c_t = count.ap[:, t * EXPERTS:(t + 1) * EXPERTS]
                if t == 0:
                    m = V.do(lambda e: e.memset(base[:, 0, :], 0.0))
                    m = copy(base[:, 1, :], c_t, mc, m)
                else:
                    m = tt(base[:, t + 1, :], base[:, t, :], c_t, ALU.add, m)
            count.release(m)
            m = ts(total, base[:, NT, :], 0.0, None, ALU.is_gt, None, m)
            for lim in (128.0, 256.0, 384.0):
                m = stt(total, base[:, NT, :], lim, total, ALU.is_gt, ALU.add, m)
            m = V.do(lambda e: e.tensor_tensor_scan(run, K("ones")[:, 0:EXPERTS], total, 0.0, ALU.mult, ALU.add), m)
            m = tt(first, run, total, ALU.subtract, m)
            m_first = ts(first, first, float(P), None, ALU.mult, None, m)
            ends = at(12, NBLOCK * EXPERTS)
            ends_ = ends.rearrange("p (b n) -> p b n", n=EXPERTS)
            for b0 in range(0, NBLOCK, EXPERTS):
                n = min(EXPERTS, NBLOCK - b0)
                if b0:
                    m = ts(total, run, float(b0), None, ALU.subtract, None, m)
                m = tt(ends_[:, b0:b0 + n, :], (total if b0 else run).unsqueeze(1).to_broadcast([P, n, EXPERTS]),
                       K("expert_id")[:, 0:n].unsqueeze(2).to_broadcast([P, n, EXPERTS]), ALU.is_le, m, m_first)
            bexp = small[:, 128:128 + NBLOCK]
            m = V.do(lambda e: e.tensor_reduce(bexp, ends.rearrange("p (b n) -> p b n", n=EXPERTS), AXX, ALU.add), m)
            bexp_u = small[:, 168:168 + NBLOCK].bitcast(U32)
            m_blk = ts(bexp_u, bexp, float(EXPERTS - 1), None, ALU.min, None, m)
            used_u = small[0:1, 262:263].bitcast(U32)
            m_blk = copy(used_u, run[0:1, EXPERTS - 1:EXPERTS], m_blk)
            dest, dest_u = small[:, 112:120], small[:, 120:128].bitcast(U32)
            m = tt(both_, rank.ap[:, 0:NT * EXPERTS].rearrange("p (t n) -> p t n", n=EXPERTS),
                   first.unsqueeze(1).to_broadcast([P, NT, EXPERTS]), ALU.add, mr, mc, m_first)
            m = tt(both_, both_, base[:, 0:NT, :], ALU.add, m)
            for k in range(2):
                m1 = tt(prod.rearrange("p (t k n) -> p t k n", t=NT, k=2)[:, :, k, :], picks4[:, :, k, :], both_, ALU.mult, m)
            rank.release(m)
            m = V.do(lambda e: e.tensor_reduce(dest, prod.rearrange("p (c n) -> p c n", n=EXPERTS), AXX, ALU.add), m1)
            m_dest = copy(dest_u, dest, m)

            place = at(26, 4 * 2 * NT).rearrange("p (a c) -> p a c", c=2 * NT)
            place_u = place.bitcast(U32)
            m = V.do(lambda e: e.tensor_scalar(place_u[:, 0, :], dest_u, 7, None, ALU.logical_shift_right), m_dest)
            m = V.do(lambda e: e.tensor_scalar(place_u[:, 1, :], dest_u, P - 1, None, ALU.bitwise_and), m)
            m = copy(place[:, 2:4, :], place_u[:, 0:2, :], m)
            in_slot = at(23, 2 * NT * P)
            in_block = at(25, 2 * NT * NBLOCK)
            s3, b3 = in_slot.rearrange("p (c n) -> p c n", n=P), in_block.rearrange("p (c n) -> p c n", n=NBLOCK)

            def hot(out, n, at_place, *marks):
                return tt(out, K("slot_id")[:, 0:n].unsqueeze(1).to_broadcast([P, 2 * NT, n]),
                          place[:, at_place, :].unsqueeze(2).to_broadcast([P, 2 * NT, n]), ALU.is_equal, *marks)
            m1 = hot(b3, NBLOCK, 2, m)
            m1 = tt(b3, b3, K("token_id").unsqueeze(2).to_broadcast([P, 2 * NT, NBLOCK]), ALU.mult, m1)
            m1 = hot(s3, P, 3, m1)
            b = banks.take()
            for c in range(2 * NT):
                m = mm(b.ap[:, 0:NBLOCK], s3[:, c, :], b3[:, c, :], c == 0, c == 2 * NT - 1, m1, *b.free, last=True)
            tok_u = small[:, 208:208 + NBLOCK].bitcast(U32)
            m_tok = copy(tok_u, b.ap[:, 0:NBLOCK], m)
            b.release(m_tok)
            next(routing)

            NG = 3
            gathered = [at(17 + 2 * i, D) for i in range(NG)]
            s_gather = [sem(f"gathered{i}") for i in range(NG)]
            gather_free = [()] * NG
            turned = Rotation([at(23 + 2 * i, D) for i in range(2)])
            hid = Rotation([at(27, CW), arena[:, 27 * T + CW:28 * T]])
            hid_t = Rotation([at(28, CW), arena[:, 28 * T + CW:29 * T]])
            outs = Rotation([at(29 + 2 * i, D) for i in range(3)])
            s_y = [sem(f"block_rows_stored{i}") for i in range(3)]
            G.wait((s_rows, 16 * NT), m_tok)

            def gather(blk):
                i = blk % NG
                G.wait(*gather_free[i])
                G.steps.append(lambda e: e.indirect_dma_start(
                    out=gathered[i], out_offset=None, in_=io["h_rows"],
                    in_offset=bass.IndirectOffsetOnAxis(ap=tok_u[:, blk:blk + 1], axis=0)).then_inc(s_gather[i], 16))
                return i, (s_gather[i], 16 * (blk // NG + 1))

            def turn(blk, g):
                i, full = g
                x_t = turned.take()
                marks = []
                for half in range(2):
                    b = banks.take()
                    for k in range(4):
                        m = PE.do(lambda e, o=b.ap[:, k * P:(k + 1) * P], s=gathered[i][:, (4 * half + k) * P:(4 * half + k + 1) * P]:
                                  e.transpose(o, s, K("ident")), full, *b.free)
                    mk = copy(x_t.ap[:, half * T:(half + 1) * T], b.ap, m, *x_t.free, q=(A, V)[half])
                    b.release(mk)
                    marks.append(mk)
                gather_free[i] = (m,)
                return x_t, marks

            expert_of = {}

            def expert_load(name, blk, half, marks=()):
                def src(e):
                    if blk not in expert_of:
                        expert_of[blk] = e.value_load(bexp_u[0:1, blk:blk + 1], min_val=0, max_val=EXPERTS - 1)
                    w = io[name][bass.DynSlice(expert_of[blk], 1)]
                    w = w.rearrange("a p c -> (a p) c")
                    return w if half is None else w[:, half * SLOT:(half + 1) * SLOT]
                return load_with(src)

            moe_ring = sbuf_phase("expert_ring", [P, MOE_SLOTS, SLOT])
            moe_full = [sem(f"expert_slot{i}_full") for i in range(MOE_SLOTS)]
            moe_free, n_moe = [()] * MOE_SLOTS, [0]

            def load_with(src):
                if n_moe[0] == 2:
                    S.wait((s_gather[0], 16))
                i, use = n_moe[0] % MOE_SLOTS, n_moe[0] // MOE_SLOTS + 1
                n_moe[0] += 1
                S.wait(*moe_free[i])
                moe_free[i] = None
                S.steps.append(lambda e: e.dma_start(moe_ring[:, i, :], src(e)).then_inc(moe_full[i], 16))
                return i, (moe_full[i], 16 * use)

            def gate_up(blk, x_t, x_marks):
                b = banks.take()
                for half in range(2):
                    i, full = expert_load("moe_in", blk, half)
                    for k in range(4):
                        m = mm(b.ap, x_t.ap[:, (4 * half + k) * P:(4 * half + k + 1) * P], moe_ring[:, i, k * T:(k + 1) * T],
                               half + k == 0, half == 1 and k == 3, full, x_marks[half], *b.free, last=k == 3)
                    moe_free[i] = (m,)
                x_t.release(m)
                hb = hid.take()
                m = silu_of(hb.ap, b.ap[:, 0:CW], m, *hb.free)
                m = tt(hb.ap, hb.ap, b.ap[:, CW:2 * CW], ALU.mult, m)
                b.release(m)
                return hb, m

            def turn_hidden(hb, m):
                b, ht = banks.take(), hid_t.take()
                for k in range(2):
                    mk = PE.do(lambda e, o=b.ap[:, k * P:(k + 1) * P], s=hb.ap[:, k * P:(k + 1) * P]:
                               e.transpose(o, s, K("ident")), m, *b.free)
                hb.release(mk)
                mk = copy(ht.ap, b.ap[:, 0:CW], mk, *ht.free)
                b.release(mk)
                return ht, mk

            def down(blk, ht, m_ht):
                i, full = expert_load("moe_down", blk, None)
                ob = outs.take()
                marks = []
                for half in range(2):
                    b = banks.take()
                    for k in range(2):
                        m = mm(b.ap, ht.ap[:, k * P:(k + 1) * P], moe_ring[:, i, k * D + half * T:k * D + (half + 1) * T], k == 0,
                               k == 1, full, m_ht, *b.free, last=True)
                    mk = copy(ob.ap[:, half * T:(half + 1) * T], b.ap, m, *ob.free, q=(A, V)[half])
                    b.release(mk)
                    marks.append(mk)
                ht.release(m)
                moe_free[i] = (m,)
                A.wait(*marks)
                A.steps.append(lambda e: e.dma_start(io["block_rows"][blk * P:(blk + 1) * P, :], ob.ap).then_inc(s_y[blk % 3], 16))
                ob.release((s_y[blk % 3], 16 * (blk // 3 + 1)))

            def blocks(b0, b1):
                g = {b0: gather(b0), b0 + 1: gather(b0 + 1)}
                cur = turn(b0, g[b0])
                held = None
                for blk in range(b0, b1):
                    if blk + 2 < b1:
                        g[blk + 2] = gather(blk + 2)
                    hb, m = gate_up(blk, *cur)
                    if blk + 1 < b1:
                        cur = turn(blk + 1, g[blk + 1])
                    if held:
                        down(*held)
                    held = (blk, *turn_hidden(hb, m))
                down(*held)

            def stored(b1):
                return [(s_y[i], 16 * len(range(i, b1, 3))) for i in range(3)]

            S.wait(*start, m_blk)
            blocks(0, EXPERTS)
            G.wait(*stored(EXPERTS))
            A.wait((s_filled, 16 * (NBLOCK - EXPERTS)))
            engines = (V, A, PE, G, S)
            for q in engines:
                q.wait(m_blk)
            before = [(len(q.steps), q.count, dict(q.reached)) for q in engines]
            blocks(EXPERTS, NBLOCK)
            G.wait(*stored(NBLOCK))
            joined = sem("blocks_done")
            for n, (q, (at_, count_, _)) in enumerate(zip(engines, before)):
                body = q.steps[at_:]
                del q.steps[at_:]

                def either(e, q=q, body=body, count_=count_, count=q.count, own=q.sem):
                    used = e.value_load(used_u, min_val=0, max_val=NBLOCK)
                    with e.If(used > EXPERTS):
                        for step_ in body:
                            step_(e)
                        if q is not S:
                            e.wait_ge(own, count)
                            e.sem_inc(joined, 1)
                    with e.Else():
                        if q is not S:
                            e.wait_ge(own, count_)
                            e.sem_inc(joined, 1)
                q.steps.append(either)
            for q, name in zip(engines, ("vector", "scalar", "tensor", "gpsimd", "sync")):
                q.sem, q.count, q.reached = sem(f"{name}_done_after_blocks"), 0, {}
                q.wait((joined, 4))
            for b in (*banks.buffers, *temps.buffers, *sums.buffers):
                b.free = ()

            pair = [[at(4 * t + 2 * k, D) for k in range(2)] for t in range(NT)]
            s_pair = [[sem(f"pair{t}{k}") for k in range(2)] for t in range(NT)]
            for t in range(NT):
                for k in range(2):
                    c = 2 * t + k
                    G.steps.append(lambda e, t=t, k=k, c=c: e.indirect_dma_start(
                        out=pair[t][k], out_offset=None, in_=io["block_rows"],
                        in_offset=bass.IndirectOffsetOnAxis(ap=dest_u[:, c:c + 1], axis=0)).then_inc(s_pair[t][k], 16))
            bb = [banks.take() for _ in range(KD)]
            for t in range(NT):
                m = ts(pair[t][0], pair[t][0], wts[:, 2 * t:2 * t + 1], None, ALU.mult, None, (s_pair[t][0], 16))
                m = stt(pair[t][0], pair[t][1], wts[:, 2 * t + 1:2 * t + 2], pair[t][0], ALU.mult, ALU.add, m, (s_pair[t][1], 16))
                for d in range(KD):
                    mt = PE.do(lambda e, o=bb[d].ap[:, t * P:(t + 1) * P], s=pair[t][0][:, d * P:(d + 1) * P]:
                               e.transpose(o, s, K("ident")), m, *bb[d].free)
            return bb, mt

        def weight_order():
            for layer in range(DEPTH):
                yield from ffn_weights(io["ffn1_in"][layer], io["ffn1_out"][layer], mod=layer == 0)
                for j in (0, 1, 2, 3, 4, 5, "v0", "v1", 8, 9, 10, 11):
                    if isinstance(j, str):
                        k0 = int(j[1]) * SLOT
                        yield "split", io["mix_v"][layer, :, k0:k0 + SLOT], SLOT
                    else:
                        yield "split", io["mix_w_in"][layer, j], SLOT
                for j in range(D // CW):
                    yield "split", io["mix_w_out"][layer, j], SLOT
                yield from ffn_weights(io["ffn2_in"][layer], io["ffn2_out"][layer])
            for j in range(7):
                yield "split", io["w_in2"][j], SLOT
            yield "raw", io["w_ukv"], MLA_HEADS * P
            yield "raw", io["w_uq"], 2 * MLA_HEADS * QK
            for j in range(D // CW):
                yield "split", io["w_out2"][j], SLOT

        weights = Weights(weight_order())

        def run():
            begin("ffn", 13, range(8), hidden=True)
            mod_acc.buffers = [Buffer(arena[:, 8 * T + i * CW:8 * T + (i + 1) * CW]) for i in range(8)]
            h = Normed("ffn1_norm", 0)
            for d in range(KD):
                h.add(d, (s_pairs[d // 2], 16))
                h.stats.add(x[:, d, :], (s_pairs[d // 2], 16))
            c_ready = mod_start()
            for q in (V, A, PE, G):
                q.wait((s_const, 32))
            for blk in range(EXPERTS, NBLOCK):
                G.steps.append(lambda e, blk=blk: e.dma_start(
                    io["block_rows"][blk * P:(blk + 1) * P, :].rearrange("p (k n) -> p k n", n=P),
                    K("ones").unsqueeze(1).to_broadcast([P, KD, P])).then_inc(s_filled, 16))
            for layer in range(DEPTH):
                if layer:
                    begin("ffn", 13, range(8), hidden=True)
                aside = None
                if layer == 0:
                    def aside():
                        if len(mod_waiting) == 4:
                            mod_columns()
                        mod_step(n_steps[0], c_ready)
                        n_steps[0] += 1

                def after_ffn(nxt):
                    def then(d, m, h_read):
                        nxt.add(d, m, h_read=(h_read,))
                        nxt.stats.add(x[:, d, :], m)
                    return then
                nxt = Normed("mix_norm", layer * KD)
                ffn(h, tile(12), after_ffn(nxt), aside)
                h = nxt
                if layer == 0:
                    mod_columns()
                    for a in (KD, 4 * KD):
                        sl = mod[:, a:a + 2 * KD]
                        mod_marks.append(ts(sl, sl, 1.0, None, ALU.add, None, *mod_marks))
                if stage("ffn1"):
                    return
                begin("mixer1", 43, range(35, 42), "first")
                nxt = Normed("ffn2_norm", layer * KD)
                mixed_ = []
                mixer1(layer, h, tile(42), lambda d, m: (mixed_.append(m), nxt.stats.add(x[:, d, :], m)))
                h = nxt
                for d in range(KD):
                    h.add(d, mixed_[d], h_read=(PE.last,))
                if stage("mix1"):
                    return
                begin("ffn", 13, range(8), hidden=True)
                if layer + 1 < DEPTH:
                    nxt = Normed("ffn1_norm", (layer + 1) * KD)
                    ffn(h, tile(12), after_ffn(nxt))
                    h = nxt
                else:
                    stats = SquareSum(KD)
                    ffn(h, tile(12), lambda d, m, h_read: stats.add(x[:, d, :], m))
                if stage("ffn2"):
                    return
            begin("mixer2", 43, range(40, 43), "second")
            stats.flush()
            r = temps.take()
            m = inv_root(r.ap, stats.bank.ap, D, "rms_eps", stats.mark, *r.free)
            stats.bank.release(m)
            xr = [stt(x[:, k, :], x[:, k, :], W("final_norm", k, k + 1), r.ap, ALU.mult, ALU.mult, m) for k in range(KD)]
            r.release(xr[-1])
            if stage("first"):
                return
            hr = modulate(xr, 0)
            y_ready = mixer2(hr)
            if stage("mixed"):
                fence()
                for k in range(KD):
                    m = copy(x[:, k, :], h_hi[:, k, :].bitcast(F32))
                return
            begin("out", 24, range(8, 16))
            mean = Mean()

            def take(d, b, m):
                mean.add(d, gated(d, b.ap, 0, m, b.release))
            out_project(y_ready, take)
            assert not weights.items and not weights.raws and not weights.ready
            xr = layer_norm(mean, "ln1_g", "ln1_b")
            if stage("ln1"):
                return
            fence()
            phase[0].close()
            phase[0] = None
            split_ctx.close()
            begin("experts", 43, range(35, 43), "experts")
            h = sbuf_phase("h", [P, KD, T])
            hr = modulate(xr, 1, h)
            bb, m = moe(h, hr)
            for d in range(KD):
                m = gated(d, bb[d].ap, 1, m, bb[d].release)
                if d == 0:
                    mean = Mean()
                mean.add(d, m)
            out_ready.extend(layer_norm(mean, "ln2_g", "ln2_b"))

        seen = {}
        mod_marks, n_steps, out_ready = [], [0], []

        def stage(name):
            seen[name] = seen.get(name, 0) + 1
            return stages == f"{name}.{seen[name]}"

        run()
        phase[0].close()
        split_ctx.close()
        if not out_ready:
            out_ready = [V.last] * KD
        for d in range(0, KD, 2):
            S.wait(*out_ready[d:d + 2], V.last if stages else out_ready[d])
            S.steps.append(lambda e, d=d: e.dma_start(io["outT"][d * P:(d + 2) * P, :].rearrange("(t p) n -> p t n", p=P),
                                                      x[:, d:d + 2, :]).then_inc(s_out, 16))
        S.wait((s_out, 16 * (KD // 2)))

        block = ctx.enter_context(nc.Block())

        @block.sync
        def _(e):
            for s in S.steps:
                s(e)

        @block.scalar
        def _(e):
            for s in A.steps:
                s(e)

        @block.vector
        def _(e):
            for s in V.steps:
                s(e)

        @block.gpsimd
        def _(e):
            for s in G.steps:
                s(e)

        @block.tensor
        def _(e):
            for s in PE.steps:
                s(e)


def column_chunks(w):
    *lead, k, n = w.shape
    w = w.reshape(*lead, k // P, P, n // CW, CW)
    w = np.moveaxis(w, -2, -4)
    return np.ascontiguousarray(np.swapaxes(w, -3, -2)).reshape(*lead, n // CW, P, k // P * CW)


def feature_columns(v):
    v = np.asarray(v)
    return v.reshape(-1, P).T


def pack(i):
    a = {k: np.asarray(v) for k, v in i.items()}
    w2 = a["w_in_2"][0]
    perm = np.concatenate([np.arange(0, 384), np.arange(320, 416), np.arange(1440, 1448), np.arange(0, 24),
                           np.arange(416, 1440), np.arange(1448, 1704)])
    params = {
        "ffn1_norm": feature_columns(a["ffn1_norm"]), "mix_norm": feature_columns(a["mix_norm"]),
        "ffn2_norm": feature_columns(a["ffn2_norm"]), "final_norm": feature_columns(a["final_norm"]),
        "conv_w": a["conv_w"].reshape(DEPTH, CONV_TAPS, 2, P).transpose(3, 0, 2, 1).reshape(P, -1),
        "conv_b": feature_columns(a["conv_b"]), "conv_ln_g": feature_columns(a["conv_ln_g"]),
        "conv_ln_b": feature_columns(a["conv_ln_b"]), "ret_norm_g": feature_columns(a["ret_norm_g"]),
        "c": feature_columns(a["c_2"]), "b_mod": feature_columns(a["b_mod_2"]),
        "q_norm": feature_columns(a["mla_q_norm_2"]), "kv_norm": feature_columns(a["mla_kv_norm_2"]),
        "gdn_conv": a["gdn_conv_2"][0].reshape(GDN_TAPS, 6, P).transpose(2, 1, 0).reshape(P, -1),
        "gdn_g": np.concatenate([a["gdn_out_norm_2"][0]] * 2)[:, None],
        "pool_scale": feature_columns(a["pool_scale_2"]),
        "pool_w": a["pool_w_2"][0].reshape(2, 2, 64, 64).transpose(1, 2, 0, 3).reshape(P, 128),
        "router_w": np.concatenate([a["router_w_group_2"][0], a["router_w_expert_2"][0]], 1)
        .reshape(KD, P, 36).transpose(1, 0, 2).reshape(P, -1),
        "ln1_g": feature_columns(a["ln1_g_2"]), "ln1_b": feature_columns(a["ln1_b_2"]),
        "ln2_g": feature_columns(a["ln2_g_2"]), "ln2_b": feature_columns(a["ln2_b_2"]),
    }
    return {
        "xT": np.ascontiguousarray(a["x"][0].T),
        **{g: np.concatenate([CONSTS[k] for k in names], 1) for g, names in TABLES.items()},
        "params": np.ascontiguousarray(np.concatenate([params[k] for k in PARAM_AT], 1)),
        "rows": np.concatenate([a["gdn_dt_bias_2"][0], a["gdn_a_log_2"][0], a["router_b_group_2"][0],
                                a["router_b_expert_2"][0]])[None, :],
        "ffn1_in": column_chunks(a["ffn1_w_in"]), "ffn1_out": column_chunks(a["ffn1_w_out"]),
        "mix_w_in": column_chunks(a["mix_w_in"]), "mix_w_out": column_chunks(a["mix_w_out"]),
        "mix_v": np.ascontiguousarray(a["mix_w_in"][:, :, 1536:2048].reshape(DEPTH, KD, P, T).transpose(0, 2, 1, 3))
        .reshape(DEPTH, P, KD * T),
        "ffn2_in": column_chunks(a["ffn2_w_in"]), "ffn2_out": column_chunks(a["ffn2_w_out"]),
        "w_mod": column_chunks(a["w_mod_2"][0]),
        "w_in2": column_chunks(w2[:, perm]),
        "w_uq": np.ascontiguousarray(a["mla_w_uq_2"][0].reshape(2, P, MLA_HEADS * QK).transpose(1, 0, 2)).reshape(P, -1),
        "w_ukv": np.ascontiguousarray(a["mla_w_ukv_2"][0]),
        "w_out2": column_chunks(a["w_out_2"][0]),
        "moe_in": np.ascontiguousarray(np.stack([a["moe_w_gate_2"][0], a["moe_w_up_2"][0]], 2)
                                       .reshape(EXPERTS, KD, P, 2 * CW).transpose(0, 2, 1, 3)).reshape(EXPERTS, P, -1),
        "moe_down": np.ascontiguousarray(a["moe_w_down_2"][0].reshape(EXPERTS, 2, P, D).transpose(0, 2, 1, 3))
        .reshape(EXPERTS, P, 2 * D),
    }


def kernel(**inputs):
    import concourse.bacc as bacc
    from concourse.bass_utils import run_bass_kernel_spmd

    nc = bacc.Bacc("TRN2", target_bir_lowering=False, num_devices=1)
    arrays = pack(inputs)
    io = {k: nc.dram_tensor(k, v.shape, mybir.dt.from_np(v.dtype), kind="ExternalInput").ap() for k, v in arrays.items()}
    for name, shape in SCRATCH.items():
        io[name] = nc.dram_tensor(name, shape, F32, kind="Internal").ap()
    io["outT"] = nc.dram_tensor("outT", (D, T), F32, kind="ExternalOutput").ap()
    build(nc, io)
    r = run_bass_kernel_spmd(nc, [arrays], core_ids=[0])
    return np.ascontiguousarray(np.asarray(r.results[0]["outT"]).T)[None]
```
